# Optimizing a Trainium2 kernel written in Bass

```python
import math
import jax
import jax.numpy as jnp
from jax import lax
import numpy as np

D_MODEL = 1024
BATCH = 1
SEQ = 256
DEPTH = 2

GRID_W = 64
N_MEM = 256
HEAD_DIM = 64
N_MIXERS = 4
MIXER_WIDTH = D_MODEL // N_MIXERS
MIXER_HEADS = MIXER_WIDTH // HEAD_DIM
D_MIX = N_MIXERS * MIXER_WIDTH

NA_KH_MAX = 8
NA_KW = 16
NA_QCB = 16
NA_KCB = 32

RET_CHUNK = 128
ROPE_BASE = 10000.0

POOL_WINDOWS = (2, 4, 8, 16)
POOL_GROUP = MIXER_WIDTH // 4

GDN_CHUNK = 64
CONV_K = 4

MEM_HEADS = 4
MEM_HEAD_DIM = D_MODEL // MEM_HEADS

N_GROUPS = 4
EXPERTS_PER_GROUP = 8
N_EXPERTS = N_GROUPS * EXPERTS_PER_GROUP
TOP_K = 2
D_EXPERT = D_MODEL // 2
MOE_BLOCK = 128

EPS = 1e-6
F32 = jnp.float32

IN_SPLITS = (3 * MIXER_WIDTH, 7 * MIXER_WIDTH, 8 * MIXER_WIDTH, 12 * MIXER_WIDTH)
P_IN = 12 * MIXER_WIDTH + 4 * MIXER_HEADS

kernel_name = 'hybrid_parallel_heads_encoder'

def rmsnorm(x, g):
    xf = x.astype(F32)
    y = xf * lax.rsqrt(jnp.mean(xf * xf, axis=-1, keepdims=True) + EPS)
    return (y * g.astype(F32)).astype(x.dtype)

def neighbourhood_attention(q, k, v, rpb):
    b, s, _ = q.shape
    h, dh = MIXER_HEADS, HEAD_DIM
    rows = s // GRID_W
    kh = min(NA_KH_MAX, rows)
    ncb = GRID_W // NA_QCB
    r = np.arange(rows)
    key_rows = np.clip(r - kh // 2, 0, rows - kh)[:, None] + np.arange(kh)[None, :]
    band = np.clip(np.arange(ncb) * NA_QCB - NA_KW // 2, 0, GRID_W - NA_KCB)
    key_cols = band[:, None] + np.arange(NA_KCB)[None, :]
    q_cols = np.arange(GRID_W).reshape(ncb, NA_QCB)
    win = np.clip(q_cols - NA_KW // 2, 0, GRID_W - NA_KW)
    col_ok = (key_cols[:, None, :] >= win[:, :, None]) & (key_cols[:, None, :] < win[:, :, None] + NA_KW)
    n_keys = kh * NA_KCB
    mask = np.broadcast_to(col_ok[:, :, None, :], (ncb, NA_QCB, kh, NA_KCB)).reshape(ncb, NA_QCB, n_keys)
    key_idx = (key_rows[:, None, :, None] * GRID_W + key_cols[None, :, None, :]).reshape(rows, ncb, n_keys)
    d_row = key_rows - r[:, None] + (NA_KH_MAX - 1)
    d_col = np.clip(key_cols[:, None, :] - q_cols[:, :, None], -(NA_KW - 1), NA_KW - 1) + (NA_KW - 1)
    bias = rpb[:, d_row[:, None, None, :, None], d_col[None, :, :, None, :]]
    bias = bias.reshape(h, rows, ncb, NA_QCB, n_keys).astype(F32)
    qg = q.reshape(b, rows, ncb, NA_QCB, h, dh)
    kg = k.reshape(b, s, h, dh)[:, key_idx]
    vg = v.reshape(b, s, h, dh)[:, key_idx]
    scores = jnp.einsum('brnqhd,brnkhd->bhrnqk', qg, kg).astype(F32) * (dh ** -0.5) + bias
    scores = jnp.where(mask, scores, -jnp.inf)
    p = jax.nn.softmax(scores, axis=-1).astype(v.dtype)
    o = jnp.einsum('bhrnqk,brnkhd->brnqhd', p, vg)
    return o.reshape(b, s, h * dh)

def rotary(x):
    s, dh = x.shape[1], x.shape[-1]
    half = dh // 2
    inv = ROPE_BASE ** (-jnp.arange(half, dtype=F32) / half)
    ang = jnp.arange(s, dtype=F32)[:, None] * inv[None, :]
    cos = jnp.cos(ang)[None, :, None, :]
    sin = jnp.sin(ang)[None, :, None, :]
    x1, x2 = x[..., :half], x[..., half:]
    return jnp.concatenate([x1 * cos - x2 * sin, x1 * sin + x2 * cos], axis=-1)

def retention_direction(q, k, v, log_gamma, include_diag):
    b, h, s, d = q.shape
    c = RET_CHUNK
    nc = s // c
    q, k, v = (t.reshape(b, h, nc, c, d) for t in (q, k, v))
    pos = jnp.arange(c, dtype=F32)
    diff = pos[:, None] - pos[None, :]
    keep = diff >= 0 if include_diag else diff > 0
    decay = jnp.where(keep, jnp.exp(log_gamma[:, None, None] * jnp.maximum(diff, 0.0)), 0.0)
    scores = jnp.einsum('bhnid,bhnjd->bhnij', q, k) * decay[:, None]
    o = jnp.einsum('bhnij,bhnjd->bhnid', scores, v)
    k_dec = k * jnp.exp(log_gamma[:, None] * (c - 1 - pos))[:, None, :, None]
    kv = jnp.einsum('bhnjd,bhnje->nbhde', k_dec, v)
    chunk_decay = jnp.exp(log_gamma * c)[None, :, None, None]

    def step(state, kv_n):
        return state * chunk_decay + kv_n, state

    _, prev = lax.scan(step, jnp.zeros((b, h, d, d), kv.dtype), kv)
    q_dec = q * jnp.exp(log_gamma[:, None] * (pos + 1.0))[:, None, :, None]
    o = o + jnp.einsum('bhnid,nbhde->bhnie', q_dec, prev)
    return o.reshape(b, h, s, d)

def retention_mixer(q, k, v, gate, norm_g):
    b, s, _ = q.shape
    h, dh = MIXER_HEADS, HEAD_DIM
    heads = lambda t: t.astype(F32).reshape(b, s, h, dh)
    qh = jnp.swapaxes(rotary(heads(q)), 1, 2)
    kh = jnp.swapaxes(rotary(heads(k)) * (dh ** -0.5), 1, 2)
    vh = jnp.swapaxes(heads(v), 1, 2)
    log_g_fwd = jnp.log1p(-jnp.exp2(-5.0 - jnp.arange(h, dtype=F32)))
    log_g_bwd = log_g_fwd[::-1]
    flip = lambda t: jnp.flip(t, axis=2)
    o_f = retention_direction(qh, kh, vh, log_g_fwd, True)
    o_b = flip(retention_direction(flip(qh), flip(kh), flip(vh), log_g_bwd, False))
    o = jnp.swapaxes(o_f + o_b, 1, 2)
    mu = jnp.mean(o, axis=-1, keepdims=True)
    var = jnp.mean(jnp.square(o - mu), axis=-1, keepdims=True)
    o = ((o - mu) * lax.rsqrt(var + EPS)).reshape(b, s, h * dh) * norm_g.astype(F32)
    o = o * jax.nn.silu(gate.astype(F32))
    return o.astype(q.dtype)

def multiscale_pool(u, w_pool, scale):
    b, s, _ = u.shape
    uf = u.astype(F32)
    csum = jnp.concatenate([jnp.zeros((b, 1, MIXER_WIDTH), F32), jnp.cumsum(uf, axis=1)], axis=1)
    t = np.arange(s)
    diffs = []
    for gi, win in enumerate(POOL_WINDOWS):
        lo = np.clip(t - win // 2, 0, s)
        hi = np.clip(t + win // 2, 0, s)
        sl = slice(gi * POOL_GROUP, (gi + 1) * POOL_GROUP)
        mean = (csum[:, hi, sl] - csum[:, lo, sl]) / (hi - lo).astype(np.float32)[None, :, None]
        diffs.append(mean - uf[..., sl])
    d = jnp.stack(diffs, axis=2)
    y = jnp.einsum('bsgc,gce->bsge', d, w_pool.astype(F32)).reshape(b, s, MIXER_WIDTH) * scale.astype(F32)
    return y.astype(u.dtype)

def short_conv(u, w):
    pad = (CONV_K // 2, CONV_K - 1 - CONV_K // 2)
    return lax.conv_general_dilated(u, w[:, None, :], window_strides=(1,), padding=(pad,),
                                    dimension_numbers=('NWC', 'WIO', 'NWC'),
                                    feature_group_count=u.shape[-1])

def gated_delta_direction(q, k, v, g, beta):
    b, h, s, d = q.shape
    c = GDN_CHUNK
    nc = s // c
    q, k, v = (t.reshape(b, h, nc, c, d) for t in (q, k, v))
    g = g.reshape(b, h, nc, c)
    beta = beta.reshape(b, h, nc, c)
    gc = jnp.cumsum(g, axis=-1)
    idx = jnp.arange(c)
    incl = idx[:, None] >= idx[None, :]
    strict = idx[:, None] > idx[None, :]
    gdiff = gc[..., :, None] - gc[..., None, :]
    decay = jnp.where(incl, jnp.exp(jnp.where(incl, gdiff, 0.0)), 0.0)
    k_beta = k * beta[..., None]
    lmat = jnp.where(strict, jnp.einsum('bhnid,bhnjd->bhnij', k_beta, k) * decay, 0.0)
    rhs = jnp.concatenate([v * beta[..., None], k_beta * jnp.exp(gc)[..., None]], axis=-1)
    sol = lax.linalg.triangular_solve(lmat + jnp.eye(c, dtype=F32), rhs, left_side=True, lower=True)
    u_val, w_dec = sol[..., :d], sol[..., d:]
    attn = jnp.einsum('bhnid,bhnjd->bhnij', q, k) * decay
    q_dec = q * jnp.exp(gc)[..., None]
    g_last = gc[..., -1]
    k_state = k * jnp.exp(g_last[..., None] - gc)[..., None]

    def step(state, inp):
        q_n, u_n, w_n, a_n, ks_n, gl_n = inp
        v_new = u_n - jnp.einsum('bhcd,bhde->bhce', w_n, state)
        o_n = jnp.einsum('bhcd,bhde->bhce', q_n, state) + jnp.einsum('bhij,bhje->bhie', a_n, v_new)
        state = state * jnp.exp(gl_n)[..., None, None] + jnp.einsum('bhcd,bhce->bhde', ks_n, v_new)
        return state, o_n

    to_scan = lambda t: jnp.moveaxis(t, 2, 0)
    xs = (to_scan(q_dec), to_scan(u_val), to_scan(w_dec), to_scan(attn), to_scan(k_state), to_scan(g_last))
    _, o = lax.scan(step, jnp.zeros((b, h, d, d), F32), xs)
    return jnp.moveaxis(o, 0, 2).reshape(b, h, s, d)

def gated_deltanet_mixer(qkv, gate, ab, conv_w, a_log, dt_bias, norm_g):
    b, s, _ = qkv.shape
    h, dh = MIXER_HEADS, HEAD_DIM
    u = jax.nn.silu(short_conv(qkv.astype(F32), conv_w.astype(F32)))
    q, k, v = (jnp.swapaxes(t.reshape(b, s, h, dh), 1, 2) for t in jnp.split(u, 3, axis=-1))
    q = q * lax.rsqrt(jnp.sum(q * q, axis=-1, keepdims=True) + EPS) * (dh ** -0.5)
    k = k * lax.rsqrt(jnp.sum(k * k, axis=-1, keepdims=True) + EPS)
    a_f, a_b, b_f, b_b = jnp.transpose(ab.astype(F32).reshape(b, s, 4, h), (2, 0, 3, 1))
    a_log = a_log.astype(F32)
    dt_bias = dt_bias.astype(F32)
    g_f = -jnp.exp(a_log[0])[None, :, None] * jax.nn.softplus(a_f + dt_bias[0][None, :, None])
    g_b = -jnp.exp(a_log[1])[None, :, None] * jax.nn.softplus(a_b + dt_bias[1][None, :, None])
    flip = lambda t: jnp.flip(t, axis=2)
    o_f = gated_delta_direction(q, k, v, g_f, jax.nn.sigmoid(b_f))
    o_b = flip(gated_delta_direction(flip(q), flip(k), flip(v), flip(g_b), flip(jax.nn.sigmoid(b_b))))
    o = jnp.swapaxes(o_f + o_b, 1, 2)
    o = o * lax.rsqrt(jnp.mean(o * o, axis=-1, keepdims=True) + EPS) * norm_g.astype(F32)
    o = o * jax.nn.silu(gate.astype(F32).reshape(b, s, h, dh))
    return o.reshape(b, s, MIXER_WIDTH).astype(qkv.dtype)

def memory_cross_attention(hq, m, w_q, w_k, w_v, w_o):
    b, s, _ = hq.shape
    nm = m.shape[1]
    q = (hq @ w_q).reshape(b, s, MEM_HEADS, MEM_HEAD_DIM)
    k = (m @ w_k).reshape(b, nm, MEM_HEADS, MEM_HEAD_DIM)
    v = (m @ w_v).reshape(b, nm, MEM_HEADS, MEM_HEAD_DIM)
    scores = jnp.einsum('bshe,bmhe->bhsm', q, k).astype(F32) * (MEM_HEAD_DIM ** -0.5)
    p = jax.nn.softmax(scores, axis=-1).astype(v.dtype)
    o = jnp.einsum('bhsm,bmhe->bshe', p, v).reshape(b, s, D_MODEL)
    return o @ w_o

def hierarchical_moe(hx, w_group, b_group, w_router, b_router, w_gate, w_up, w_down):
    b, s, d = hx.shape
    n = b * s
    hf = hx.reshape(n, d)
    g_prob = jax.nn.softmax((hf @ w_group).astype(F32) + b_group.astype(F32), axis=-1)
    g_p, g_idx = lax.top_k(g_prob, 1)
    e_logits = ((hf @ w_router).astype(F32) + b_router.astype(F32)).reshape(n, N_GROUPS, EXPERTS_PER_GROUP)
    e_logits = jnp.take_along_axis(e_logits, g_idx[:, :, None], axis=1)[:, 0]
    e_p, e_loc = lax.top_k(jax.nn.softmax(e_logits, axis=-1), TOP_K)
    gate_w = g_p * e_p / jnp.sum(e_p, axis=-1, keepdims=True)
    expert = g_idx * EXPERTS_PER_GROUP + e_loc
    a = n * TOP_K
    flat_e = expert.reshape(a)
    order = jnp.argsort(flat_e)
    e_sorted = flat_e[order]
    tok_sorted = (order // TOP_K).astype(jnp.int32)
    w_sorted = gate_w.reshape(a)[order]
    counts = jax.ops.segment_sum(jnp.ones((a,), jnp.int32), flat_e, num_segments=N_EXPERTS)
    padded = (counts + MOE_BLOCK - 1) // MOE_BLOCK * MOE_BLOCK
    pad_end = jnp.cumsum(padded)
    pad_start = pad_end - padded
    start = jnp.cumsum(counts) - counts
    dest = pad_start[e_sorted] + jnp.arange(a, dtype=jnp.int32) - start[e_sorted]
    cap = a + N_EXPERTS * MOE_BLOCK
    n_blocks = cap // MOE_BLOCK
    buf_tok = jnp.zeros((cap,), jnp.int32).at[dest].set(tok_sorted)
    buf_w = jnp.zeros((cap,), F32).at[dest].set(w_sorted)
    blk_start = jnp.arange(n_blocks, dtype=jnp.int32) * MOE_BLOCK
    blk_expert = jnp.minimum(jnp.searchsorted(pad_end, blk_start, side='right'), N_EXPERTS - 1)

    def expert_block(args):
        tok, wt, e = args
        xb = hf[tok]
        y = (jax.nn.silu(xb @ w_gate[e]) * (xb @ w_up[e])) @ w_down[e]
        return y * wt[:, None].astype(y.dtype)

    ys = lax.map(expert_block, (buf_tok.reshape(n_blocks, MOE_BLOCK), buf_w.reshape(n_blocks, MOE_BLOCK), blk_expert))
    out = jax.ops.segment_sum(ys.reshape(cap, d), buf_tok, num_segments=n)
    return out.reshape(b, s, d)

def setup_inputs(seed: int = 0) -> dict:
    key = jax.random.key(seed)
    k = jax.random.split(key, 28)
    L, D, W, H = DEPTH, D_MODEL, MIXER_WIDTH, MIXER_HEADS

    def nrm(i, shape, scale):
        return jax.random.normal(k[i], shape, F32) * scale

    def gain(i, shape):
        return 1.0 + 0.05 * jax.random.normal(k[i], shape, F32)

    dt = jnp.exp(jax.random.uniform(k[10], (L, 2, H), F32, math.log(1e-3), math.log(1e-1)))
    return {
        'x': nrm(0, (BATCH, SEQ, D), 1.0),
        'mem': nrm(1, (BATCH, N_MEM, D), 1.0),
        'mix_norm_g': gain(2, (L, D)),
        'w_in': nrm(3, (L, D, P_IN), D ** -0.5),
        'na_rpb': nrm(4, (L, H, 2 * NA_KH_MAX - 1, 2 * NA_KW - 1), 0.1),
        'ret_norm_g': gain(5, (L, W)),
        'pool_w': nrm(6, (L, len(POOL_WINDOWS), POOL_GROUP, POOL_GROUP), POOL_GROUP ** -0.5),
        'pool_scale': gain(7, (L, W)),
        'gdn_conv_w': nrm(8, (L, CONV_K, 3 * W), CONV_K ** -0.5),
        'gdn_a_log': jnp.log(jax.random.uniform(k[9], (L, 2, H), F32, 1.0, 16.0)),
        'gdn_dt_bias': dt + jnp.log(-jnp.expm1(-dt)),
        'gdn_norm_g': gain(11, (L, HEAD_DIM)),
        'w_out': nrm(12, (L, D_MIX, D), D_MIX ** -0.5),
        'mem_q_norm_g': gain(13, (L, D)),
        'mem_kv_norm_g': gain(14, (L, D)),
        'mem_w_q': nrm(15, (L, D, D), D ** -0.5),
        'mem_w_k': nrm(16, (L, D, D), D ** -0.5),
        'mem_w_v': nrm(17, (L, D, D), D ** -0.5),
        'mem_w_o': nrm(18, (L, D, D), D ** -0.5),
        'ffn_norm_g': gain(19, (L, D)),
        'w_group': nrm(20, (L, D, N_GROUPS), D ** -0.5),
        'b_group': nrm(21, (L, N_GROUPS), 0.01),
        'w_router': nrm(22, (L, D, N_EXPERTS), D ** -0.5),
        'b_router': nrm(23, (L, N_EXPERTS), 0.01),
        'w_gate': nrm(24, (L, N_EXPERTS, D, D_EXPERT), D ** -0.5),
        'w_up': nrm(25, (L, N_EXPERTS, D, D_EXPERT), D ** -0.5),
        'w_down': nrm(26, (L, N_EXPERTS, D_EXPERT, D), D_EXPERT ** -0.5),
        'final_norm_g': gain(27, (D,)),
    }

def reference(x, mem, mix_norm_g, w_in, na_rpb, ret_norm_g, pool_w, pool_scale, gdn_conv_w,
              gdn_a_log, gdn_dt_bias, gdn_norm_g, w_out, mem_q_norm_g, mem_kv_norm_g, mem_w_q,
              mem_w_k, mem_w_v, mem_w_o, ffn_norm_g, w_group, b_group, w_router, b_router,
              w_gate, w_up, w_down, final_norm_g):
    W = MIXER_WIDTH
    for l in range(DEPTH):
        h = rmsnorm(x, mix_norm_g[l])
        proj = h @ w_in[l]
        p_a, p_b, p_c, p_d, p_ab = jnp.split(proj, IN_SPLITS, axis=-1)
        qa, ka, va = jnp.split(p_a, 3, axis=-1)
        y_a = neighbourhood_attention(qa, ka, va, na_rpb[l])
        qb, kb, vb, gb = jnp.split(p_b, 4, axis=-1)
        y_b = retention_mixer(qb, kb, vb, gb, ret_norm_g[l])
        y_c = multiscale_pool(p_c, pool_w[l], pool_scale[l])
        y_d = gated_deltanet_mixer(p_d[..., :3 * W], p_d[..., 3 * W:], p_ab, gdn_conv_w[l],
                                   gdn_a_log[l], gdn_dt_bias[l], gdn_norm_g[l])
        x = x + jnp.concatenate([y_a, y_b, y_c, y_d], axis=-1) @ w_out[l]
        x = x + memory_cross_attention(rmsnorm(x, mem_q_norm_g[l]), rmsnorm(mem, mem_kv_norm_g[l]),
                                       mem_w_q[l], mem_w_k[l], mem_w_v[l], mem_w_o[l])
        x = x + hierarchical_moe(rmsnorm(x, ffn_norm_g[l]), w_group[l], b_group[l], w_router[l],
                                 b_router[l], w_gate[l], w_up[l], w_down[l])
    return rmsnorm(x, final_norm_g)


_drawn_inputs = setup_inputs


def setup_inputs(seed=0):
    import zlib

    import numpy as np

    out = dict(_drawn_inputs(seed))
    spreads = {}
    factors = {'na_rpb': 3.076, 'mem_q_norm_g': 2.876, 'b_group': 8.0, 'b_router': 3.359}
    for name, (base, spread) in spreads.items():
        noise = np.random.default_rng([zlib.crc32(name.encode()), seed]).standard_normal(out[name].shape)
        drawn = base * np.exp(spread * noise) if base else spread * noise
        out[name] = jnp.asarray(drawn.astype(out[name].dtype))
    for name, factor in factors.items():
        out[name] = (out[name] * factor).astype(out[name].dtype)
    return out
```

```python
from contextlib import ExitStack

import numpy as np
import concourse.bass as bass
from concourse import mybir

F32 = mybir.dt.float32
I32 = mybir.dt.int32
U32 = mybir.dt.uint32
ALU = mybir.AluOpType
ACT = mybir.ActivationFunctionType
AX = mybir.AxisListType.X

P = 128
D = 1024
T = 256
TT = T // P
DC = D // P
DEPTH = 2
GRID_W = 64
ROWS = T // GRID_W
HD = 64
NH = 4
W = NH * HD
RPB_H, RPB_W = 15, 31
NE = 32
EPG = 8
NG = 4
DE = 512
CHUNK = 64
LEVELS = 6
QUAD = 4
SLOTS = 32
NQ = NE // QUAD
NSLOT = 6
P_IN = 12 * W + 4 * NH
EPS = 1e-6
POOL_WINDOWS = (2, 4, 8, 16)
NEG = -1e30

PV_A, PQ_B, PK_B, PV_B, PG_B, PU_C, PG_D, PAB = 0, 256, 512, 768, 1024, 1280, 1536, 1792
PW = PAB + 4 * NH

CONSTS = {}
_at = 0
for _name, _width in (("ident", P), ("anti", P), ("band", T), ("tri", 2 * P), ("level", LEVELS * 2 * P),
                      ("blocks", P), ("ones", P), ("before", P), ("rot_a", TT * HD), ("rot_b", TT * HD),
                      ("slot", SLOTS), ("eight", EPG), ("halves", 2)):
    CONSTS[_name] = (_at, _width)
    _at += _width
NCONST = _at


def constant_tables():
    c = np.zeros((P, NCONST), np.float32)

    def put(name, value):
        at, width = CONSTS[name]
        c[:, at:at + width] = np.asarray(value, np.float32).reshape(P, width)

    p = np.arange(P)
    j, i = p[:, None], p[None, :]
    put("ident", j == i)
    put("anti", (j // 64 == i // 64) & (j % 64 == 63 - i % 64))
    qc, kc = (p % GRID_W)[:, None], (np.arange(T) % GRID_W)[None, :]
    lo = np.clip(qc - 8, 0, GRID_W - 16)
    put("band", np.where((kc >= lo) & (kc < lo + 16), 0.0, NEG))
    same = j // CHUNK == i // CHUNK
    put("tri", np.stack([same & (j <= i), same & (j >= i)], 1))
    levels = []
    for n in range(LEVELS):
        b = 1 << n
        pair = j // (2 * b) == i // (2 * b)
        levels += [pair & (j // b % 2 == 0) & (i // b % 2 == 1), pair & (j // b % 2 == 1) & (i // b % 2 == 0)]
    put("level", np.stack(levels, 1))
    put("blocks", same)
    put("ones", np.ones((P, P)))
    put("before", j < i)
    inv = np.float32(10000.0) ** (-np.arange(HD // 2, dtype=np.float32) / np.float32(HD // 2))
    ang = (np.arange(T, dtype=np.float32)[:, None] * inv[None, :]).astype(np.float32)
    cos, sin = np.cos(ang), np.sin(ang)
    tiled = lambda a: a.reshape(TT, P, HD).transpose(1, 0, 2)
    put("rot_a", tiled(np.concatenate([cos, cos], 1)))
    put("rot_b", tiled(np.concatenate([-sin, sin], 1)))
    put("slot", np.broadcast_to(np.arange(SLOTS), (P, SLOTS)))
    put("eight", np.broadcast_to(np.arange(EPG), (P, EPG)))
    put("halves", np.stack([p < 64, p >= 64], 1))

    t = np.arange(T)
    diff = (t[None, :] - t[:, None]).astype(np.float64)
    lg = np.log1p(-np.exp2(-5.0 - np.arange(NH)))
    decay = np.stack([np.where(diff >= 0, np.exp(lg[h] * np.maximum(diff, 0)),
                               np.exp(lg[::-1][h] * np.maximum(-diff, 0))) for h in range(NH)]) * HD ** -0.5
    pools = []
    for w in POOL_WINDOWS:
        a, b = np.clip(t - w // 2, 0, T), np.clip(t + w // 2, 0, T)
        inside = (t[:, None] >= a[None, :]) & (t[:, None] < b[None, :])
        pools.append(inside / (b - a)[None, :] - (t[:, None] == t[None, :]))
    fold = lambda m: np.stack(m).reshape(4, TT, P, T).transpose(2, 0, 1, 3).reshape(P, 4 * TT * T)
    big = np.concatenate([fold(decay), fold(pools)], 1).astype(np.float32)
    return c, big


def encoder(nc, a, out, taps):
    ctx = ExitStack()
    with ctx:
        sb = lambda name, shape, dt=F32: ctx.enter_context(nc.sbuf_tensor(name, shape, dt))

        def wide(ap, n):
            return ap.rearrange("p (k o) -> p k o", o=1).to_broadcast([ap.shape[0], ap.shape[1], n])

        def again(ap, n):
            return ap.rearrange("p (o k) -> p o k", o=1).to_broadcast([ap.shape[0], n, ap.shape[1]])

        ring = sb("ring", [P, NSLOT, 4096])
        x = sb("x", [P, TT, D])
        xn = sb("xn", [P, TT, D])
        xnT = sb("xnT", [P, DC, T])
        rpb = sb("rpb", [P, 2048])
        m1, m2, m3, m4 = (sb(f"m{k}", [P, 2048]) for k in (1, 2, 3, 4))
        yT = sb("yT", [P, DC, T])
        proj = sb("proj", [P, TT * PW])
        conv_in = sb("conv_in", [P, 6, T + 3])
        const = sb("const", [P, NCONST])
        gains = sb("gains", [P, 5, DC])
        cols = sb("cols", [P, 8])
        conv_w = sb("conv_w", [P, 4, 6])
        rows = sb("rows", [P, 16 + 4 + NE])
        pool_w = sb("pool_w", [HD, 4, HD])
        router_w = sb("router_w", [P, DC, NG + NE])
        ss = sb("ss", [P, 4])
        rstd = sb("rstd", [P, 4])
        mhalf = sb("mhalf", [P, 16])
        small = sb("small", [P, 512])
        npi = sb("npi", [1, 1], I32)
        idx = sb("idx", [P, 2, TT, 8], U32)
        val = sb("val", [P, 2, TT, 8])
        rank_q = sb("rank_q", [P, TT, QUAD])
        gate_q = sb("gate_q", [P, TT, QUAD])
        ranks = sb("ranks", [P, TT, NE])
        gates = sb("gates", [P, TT, NE])
        print("sbuf left", nc.sbuf_bytes_remaining() if callable(nc.sbuf_bytes_remaining) else nc.sbuf_bytes_remaining)

        def c(name):
            at, width = CONSTS[name]
            return const[:, at:at + width]

        ident, anti, ones, blocks, before = c("ident"), c("anti"), c("ones"), c("blocks"), c("before")
        tri = c("tri").rearrange("p (d k) -> p d k", d=2)
        level = c("level").rearrange("p (n d k) -> p n d k", n=LEVELS, d=2)
        rot_a = c("rot_a").rearrange("p (t k) -> p t k", t=TT)
        rot_b = c("rot_b").rearrange("p (t k) -> p t k", t=TT)
        halves = c("halves")
        projv = proj[:, :].rearrange("p (t k) -> p t k", t=TT)

        aqkT = m3[:, 1024:2048].rearrange("p (c t) -> p c t", c=4)
        prob = m1[:, :].rearrange("p (h t k) -> p h t k", h=NH, t=TT)
        probT = m2[:, :].rearrange("p (h c q) -> p h c q", h=NH, c=2)
        bias = rpb[:, :].rearrange("p (t h k) -> p t h k", t=TT, h=NH)
        rot1 = m4[:, 0:1024].rearrange("p (t k) -> p t k", t=TT)
        rot2 = m4[:, 1024:2048].rearrange("p (t k) -> p t k", t=TT)
        bqkT = m3[:, 0:1024].rearrange("p (c t) -> p c t", c=4)
        retS = xn[:, :, :].rearrange("p t (u k) -> p (t u) k", k=512)
        ret_o = m4[:, 0:512]
        ret_s = m4[:, 512:1024]
        ret_g = m4[:, 1024:1536]
        diffT = m3[0:HD, 1024:2048].rearrange("p (g t) -> p g t", g=4)
        units = lambda m: m.rearrange("p (u k) -> p u k", k=P)
        decay, lT, inv, invT = (units(m[:, :]) for m in (m1, m2, m3, m4))
        low = units(xn[:, :, :].rearrange("p t k -> p (t k)"))
        prod = units(rpb[:, :])
        qkv = conv_in[:, :, :].rearrange("p c t -> p (c t)")[:, 0:TT * 768].rearrange("p (t k) -> p t k", t=TT)
        qkT = xnT
        wT = m2[:, 0:1024].rearrange("p (d t f k) -> p d t f k", d=2, t=TT, f=2)
        qdT = m2[:, 1024:2048].rearrange("p (d t f k) -> p d t f k", d=2, t=TT, f=2)
        uval = m3[:, 0:1024].rearrange("p (u k) -> p u k", k=HD)
        vbeta = m3[:, 1024:2048].rearrange("p (u k) -> p u k", k=HD)
        kdec = rpb[:, 0:1024].rearrange("p (u k) -> p u k", k=HD)
        kstate = rpb[:, 1024:2048].rearrange("p (u k) -> p u k", k=HD)
        xnf = xn[:, :, :].rearrange("p t k -> p (t k)")
        qdec = xnf[:, 0:1024].rearrange("p (u k) -> p u k", k=HD)
        gdn_o = xnf[:, 1024:2048]
        state = small[:, 0:256].rearrange("p (d f e) -> p d f e", d=2, f=2)
        vnew = small[:, 256:512].rearrange("p (a f e) -> p a f e", a=2, f=2)
        dsm = sb("dsm", [P, 16 * 16])
        dcol = lambda k, n=16: dsm[:, 16 * k:16 * k + n]
        unit_col = lambda k: dcol(k).rearrange("p (t d h) -> p t d h", t=TT, d=2)
        G, BETA, GC, GL, EGC, ESL, T0, T1, T2, T3 = range(10)
        gmask = dsm[:, 160:192].rearrange("p (v u) -> p v u", v=2)
        egl = dsm[:, 192:208]
        stat = dsm[:, 208:224]
        stat2 = dsm[:, 224:240]
        gdn_q = sb("gdn_q", [P, 2, 2, HD])
        mem_tok, mem_n, memT = m1[:, :].rearrange("p (t k) -> p t k", t=TT), m2[:, :].rearrange("p (t k) -> p t k", t=TT), m3[:, :].rearrange("p (c t) -> p c t", c=DC)
        memK = m4[:, :].rearrange("p (c t) -> p c t", c=DC)
        memV = proj[:, 0:2048].rearrange("p (t k) -> p t k", t=TT)
        memQ = yT
        attT = m3[:, :].rearrange("p (c t) -> p c t", c=DC)
        sel = m1[:, 0:256].rearrange("p (t s) -> p t s", t=TT)
        selw = m1[:, 256:512].rearrange("p (t s) -> p t s", t=TT)
        selwT = m1[:, 512:768].rearrange("p (t k) -> p t k", t=TT)
        xg = m2[:, 0:1024].rearrange("p (c s) -> p c s", c=DC)
        xn_by_row = xn[:, :, :].rearrange("p t (k c) -> p t c k", c=DC)
        silu_g, hid = m3[:, 0:512], m3[:, 512:1024]
        hid_by_row = hid.rearrange("p (k c) -> p c k", c=4)
        hidT = m3[:, 1024:1536].rearrange("p (c s) -> p c s", c=4)
        y_e = m4[:, 0:1024]
        logit = small[:, 0:TT * 36].rearrange("p (t k) -> p t k", t=TT)

        bank = [ctx.enter_context(nc.psum_tensor(f"bank{k}", [P, 512], F32)) for k in range(8)]

        sem = lambda name: ctx.enter_context(nc.semaphore(name))
        const_in, x_in, preset, layer_go = sem("const_in"), sem("x_in"), sem("preset"), sem("layer_go")
        stored, final_in = sem("stored"), sem("final_in")
        last_sq, last_mean, last_rstd, last_out = sem("last_sq"), sem("last_mean"), sem("last_rstd"), sem("last_out")
        layer_seen, pass_seen = sem("layer_seen"), sem("pass_seen")
        layer_sems = []

        def lsem(name):
            s = sem(name)
            layer_sems.append(s)
            return s

        unit_in = [lsem(f"unit_in{k}") for k in range(NSLOT)]
        params_in, rpb_in, mem_in = lsem("params_in"), lsem("rpb_in"), lsem("mem_in")
        vec_full, vec_evac, act_full, act_evac = lsem("vec_full"), lsem("vec_evac"), lsem("act_full"), lsem("act_evac")
        vec_step, act_step, pool_step = lsem("vec_step"), lsem("act_step"), lsem("pool_step")
        squares, means, rstds, normed = lsem("squares"), lsem("means"), lsem("rstds"), lsem("normed")
        maxed, exped, probs_ready = lsem("maxed"), lsem("exped"), lsem("probs_ready")
        rotated, ret_silu, ret_var, ret_rstd, ret_done = lsem("rotated"), lsem("ret_silu"), lsem("ret_var"), lsem("ret_rstd"), lsem("ret_done")
        conved, conv_silu, qk_sums, qk_rstd, qk_ready = lsem("conved"), lsem("conv_silu"), lsem("qk_sums"), lsem("qk_rstd"), lsem("qk_ready")
        gate_in, gate_exp, gate_in2, gate_ln, g_ready = lsem("gate_in"), lsem("gate_exp"), lsem("gate_in2"), lsem("gate_ln"), lsem("g_ready")
        gdiff, gexp, dec_exp, dec_masked, low_ready = lsem("gdiff"), lsem("gexp"), lsem("dec_exp"), lsem("dec_masked"), lsem("low_ready")
        lT_ready, inv0_ready, scaled, vnew_ready = lsem("lT_ready"), lsem("inv0_ready"), lsem("scaled"), lsem("vnew_ready")
        state_ready, gdn_var, gdn_rstd, gdn_silu, gdn_done = lsem("state_ready"), lsem("gdn_var"), lsem("gdn_rstd"), lsem("gdn_silu"), lsem("gdn_done")
        r_max, r_exp, ind_ready, np_ready = lsem("r_max"), lsem("r_exp"), lsem("ind_ready"), lsem("np_ready")
        sel_built, sel_turned, selwT_ready, x_added = lsem("sel_built"), lsem("sel_turned"), lsem("selwT_ready"), lsem("x_added")
        gathered, xg_ready = [lsem(f"gathered{k}") for k in range(2)], [lsem(f"xg_ready{k}") for k in range(2)]
        gate_full, up_full, silu_ready, hid_ready = lsem("gate_full"), lsem("up_full"), lsem("silu_ready"), lsem("hid_ready")
        hid_turned, hidT_ready, y_full = lsem("hid_turned"), lsem("hidT_ready"), [lsem(f"y_full{k}") for k in range(2)]
        y_ready, scattered = [lsem(f"y_ready{k}") for k in range(2)], [lsem(f"scattered{k}") for k in range(4)]
        units_free = lsem("units_free")
        layer_done, quad_ready = lsem("layer_done"), lsem("quad_ready")
        ranks_moved = lsem("ranks_moved")

        PRE_UNITS = 18
        slot = lambda n: n % NSLOT
        landed = lambda n: 16 * (n // NSLOT + 1)
        U_AQK, U_TOK, U_GATE, U_DQK, U_DV, U_CONST, U_OUT, U_MK, U_MV, U_MQ, U_MO = 0, 1, 4, 5, 6, 7, 8, 10, 12, 14, 16
        last_reader = {}
        done = {}
        filled = {}

        ring3 = lambda n, k: ring[:, slot(n), 0:DC * k].rearrange("p (c k) -> p c k", k=k)

        block = ctx.enter_context(nc.Block())

        @block.tensor
        def _(pe):
            pe.wait_ge(const_in, 16)
            pe.wait_ge(preset, 2)
            with pe.Fori(0, DEPTH) as l:
                count = {"v": 0, "a": 0}
                evac = {"v": vec_evac, "a": act_evac}
                full = {"v": vec_full, "a": act_full}

                def fill(r):
                    n = count[r]
                    if n >= 4:
                        pe.wait_ge(evac[r], n - 3)
                    return bank[(0 if r == "v" else 4) + n % 4]

                def end(r, mm, name=None, units=()):
                    mm.then_inc(full[r], 1)
                    count[r] += 1
                    if name:
                        done[name] = (evac[r], count[r])
                        filled[name] = (full[r], count[r])
                    for u in units:
                        last_reader[u] = (full[r], count[r])

                def need(name):
                    pe.wait_ge(*done[name])

                def unit(n):
                    pe.wait_ge(unit_in[slot(n)], landed(n))

                def turn_x(name, src, k):
                    pe.wait_ge(normed, 2 * (k + 1))
                    for t in range(TT):
                        for g in range(2):
                            b = fill("v")
                            for q in range(4):
                                mm = pe.transpose(b[:, q * P:(q + 1) * P], src[:, t, (4 * g + q) * P:(4 * g + q + 1) * P], ident)
                            end("v", mm, name)

                def feature_major(n, chunks, rhsT, r, name, k=512):
                    w = ring3(n, k)
                    for f in range(0, chunks, 2):
                        b = fill(r)
                        for q in range(2):
                            for ch in range(DC):
                                mm = pe.matmul(b[:, q * T:(q + 1) * T], w[:, ch, (f + q) * P:(f + q + 1) * P], rhsT[:, ch, :],
                                               start=ch == 0, stop=ch == DC - 1)
                        end(r, mm, f"{name}{f // 2}", (n,))

                def token_major(n, k, lhsT, rs, name):
                    w = ring3(n, k)
                    for t in range(TT):
                        b = fill(rs[t])
                        for ch in range(DC):
                            mm = pe.matmul(b[:, 0:k], lhsT[:, ch, t * P:(t + 1) * P], w[:, ch, :], start=ch == 0, stop=ch == DC - 1)
                        end(rs[t], mm, f"{name}{t}", (n,))

                def turn_probs(k):
                    for h in range(NH):
                        pe.wait_ge(probs_ready, NH * k + h + 1)
                        b = fill("a")
                        for kc in range(2):
                            for t in range(TT):
                                mm = pe.transpose(b[:, (2 * kc + t) * P:(2 * kc + t + 1) * P], prob[:, h, t, kc * P:(kc + 1) * P], ident)
                        end("a", mm, f"probT{k}{h}")

                turn_x("xnT", xn, 0)
                need("xnT")
                unit(U_AQK)
                feature_major(U_AQK, 4, xnT, "a", "aqk")
                for n in range(3):
                    unit(U_TOK + n)
                    token_major(U_TOK + n, 512, xnT, "av", f"tok{n}")
                unit(U_GATE)
                token_major(U_GATE, W + 4 * NH, xnT, "aa", "gate")
                unit(U_DQK)
                feature_major(U_DQK, 4, xnT, "v", "dqk")
                unit(U_DV)
                feature_major(U_DV, 2, xnT, "v", "dv", k=256)

                need("aqk1")
                pe.wait_ge(rpb_in, 16 * 16)
                for h in range(NH):
                    b = fill("v")
                    r0 = (h % 2) * HD
                    for t in range(TT):
                        o = b[:, t * T:(t + 1) * T]
                        pe.matmul(o, aqkT[r0:r0 + HD, h // 2, t * P:(t + 1) * P], aqkT[r0:r0 + HD, 2 + h // 2, :], start=True, stop=False)
                        mm = pe.matmul(o, anti, bias[:, t, h, :], start=False, stop=True)
                    end("v", mm, f"ascore{h}")
                turn_probs(0)
                need("probT03")
                need("tok01")
                need("tok00")
                b = fill("a")
                for h in range(NH):
                    for kc in range(2):
                        mm = pe.matmul(b[(h % 2) * HD:(h % 2 + 1) * HD, (h // 2) * T:(h // 2 + 1) * T],
                                       projv[:, kc, PV_A + h * HD:PV_A + (h + 1) * HD], probT[:, h, kc, :], start=kc == 0, stop=kc == 1)
                end("a", mm, "yA")

                pe.wait_ge(rotated, 2)
                for t in range(TT):
                    b = fill("a")
                    for q in range(4):
                        mm = pe.transpose(b[:, q * P:(q + 1) * P], rot1[:, t, q * P:(q + 1) * P], ident)
                    end("a", mm, "bqkT")
                need("bqkT")
                for h in range(NH):
                    b = fill("v")
                    r0 = (h % 2) * HD
                    for jt in range(TT):
                        mm = pe.matmul(b[:, jt * T:(jt + 1) * T], bqkT[r0:r0 + HD, 2 + h // 2, jt * P:(jt + 1) * P],
                                       bqkT[r0:r0 + HD, h // 2, :], start=True, stop=True)
                    end("v", mm, f"retS{h}")
                need("retS3")
                for n in range(1, 3):
                    for t in range(TT):
                        need(f"tok{n}{t}")
                b = fill("v")
                for t in range(TT):
                    for h in range(NH):
                        for jt in range(TT):
                            mm = pe.matmul(b[:, t * W + h * HD:t * W + (h + 1) * HD], retS[:, h, jt * T + t * P:jt * T + (t + 1) * P],
                                           projv[:, jt, PV_B + h * HD:PV_B + (h + 1) * HD], start=jt == 0, stop=jt == TT - 1)
                end("v", mm, "ret_o")

                unit(U_CONST)
                pools = ring[:, slot(U_CONST), 2048:4096].rearrange("p (g s t) -> p g s t", g=4, s=TT)
                for f in range(2):
                    b = fill("a")
                    for q in range(2):
                        g = 2 * f + q
                        for st in range(TT):
                            mm = pe.matmul(b[0:HD, q * T:(q + 1) * T], projv[:, st, PU_C + g * HD:PU_C + (g + 1) * HD],
                                           pools[:, g, st, :], start=st == 0, stop=st == TT - 1)
                    end("a", mm, "diffT")
                need("diffT")
                b = fill("v")
                for g in range(4):
                    mm = pe.matmul(b[(g % 2) * HD:(g % 2 + 1) * HD, (g // 2) * T:(g // 2 + 1) * T], pool_w[:, g, :], diffT[:, g, :],
                                   start=True, stop=True)
                end("v", mm, "yC")

                pe.wait_ge(ret_done, 1)
                b = fill("v")
                for f in range(2):
                    for t in range(TT):
                        mm = pe.transpose(b[:, f * T + t * P:f * T + (t + 1) * P], ret_o[:, t * W + f * P:t * W + (f + 1) * P], ident)
                end("v", mm, "yB")

                pe.wait_ge(conv_silu, 6)
                for t in range(TT):
                    b = fill("v")
                    for q in range(4):
                        mm = pe.transpose(b[:, q * P:(q + 1) * P], xnT[:, q, t * P:(t + 1) * P], ident)
                    end("v", mm)
                    b = fill("v")
                    for q in range(2):
                        mm = pe.transpose(b[:, q * P:(q + 1) * P], xnT[:, 4 + q, t * P:(t + 1) * P], ident)
                    end("v", mm)
                pe.wait_ge(g_ready, 1)
                b = fill("v")
                g4 = unit_col(G)
                for d in range(2):
                    for t in range(TT):
                        pe.matmul(b[:, 8 * t + 4 * d:8 * t + 4 * d + 4], tri[:, d, :], g4[:, t, d, :], start=True, stop=True)
                pe.matmul(b[:, 16:32], blocks, dcol(G), start=True, stop=True)
                gm = gmask.rearrange("p v (u h) -> p (v u) h", h=NH)
                for par in range(2):
                    mm = pe.matmul(b[par * HD:(par + 1) * HD, 32:48], ones[:, 0:HD], gm[:, :, par::2], start=True, stop=True)
                end("v", mm, "gc")
                for d in range(2):
                    for par in range(2):
                        b = fill("v")
                        for t in range(TT):
                            for f in range(2):
                                k = 2 * t + f
                                mm = pe.matmul(b[:, k * P:(k + 1) * P], g4[:, t, d, 2 * f + par:2 * f + par + 1].to_broadcast([P, P]), tri[:, d, :],
                                               start=True, stop=True)
                        end("v", mm)
                pe.wait_ge(qk_ready, 2)
                for t in range(TT):
                    b = fill("a")
                    for q in range(4):
                        mm = pe.transpose(b[:, q * P:(q + 1) * P], qkv[:, t, q * P:(q + 1) * P], ident)
                    end("a", mm, "qkT")
                need("qkT")
                for which in (2, 0):
                    for par in range(2):
                        b = fill("v")
                        r0 = par * HD
                        for t in range(TT):
                            for f in range(2):
                                k = 2 * t + f
                                mm = pe.matmul(b[:, k * P:(k + 1) * P], qkT[r0:r0 + HD, 2 + f, t * P:(t + 1) * P],
                                               qkT[r0:r0 + HD, which + f, t * P:(t + 1) * P], start=True, stop=True)
                        end("v", mm)
                b4 = unit_col(BETA)
                for d in range(2):
                    for par in range(2):
                        b = fill("v")
                        for t in range(TT):
                            for f in range(2):
                                k = 2 * t + f
                                mm = pe.matmul(b[:, k * P:(k + 1) * P], b4[:, t, d, 2 * f + par:2 * f + par + 1].to_broadcast([P, P]), ident,
                                               start=True, stop=True)
                        end("v", mm)
                for q in range(4):
                    pe.wait_ge(inv0_ready, q + 1)
                    b = fill("a")
                    for k in range(4):
                        mm = pe.transpose(b[:, k * P:(k + 1) * P], invT[:, 4 * q + k, :], ident)
                    end("a", mm, f"inv{q}")
                    done[f"inv0{q}"] = done[f"inv{q}"]
                for n in range(1, LEVELS):
                    pe.wait_ge(low_ready, 2 * n)
                    for q in range(4):
                        need(f"inv{q}")
                        b = fill("a")
                        for k in range(4):
                            u = 4 * q + k
                            mm = pe.matmul(b[:, k * P:(k + 1) * P], low[:, u, :], inv[:, u, :], start=True, stop=True)
                        end("a", mm, f"prod{q}")
                        if q == 3:
                            filled[f"low_used{n}"] = filled["prod3"]
                    for q in range(4):
                        need(f"prod{q}")
                        if n > 1:
                            need(f"invT{q}")
                        if n < LEVELS - 1:
                            b = fill("v")
                            for k in range(4):
                                u = 4 * q + k
                                mm = pe.matmul(b[:, k * P:(k + 1) * P], invT[:, u, :], prod[:, u, :], start=True, stop=True)
                            end("v", mm, f"inv{q}")
                        b = fill("v")
                        for k in range(4):
                            u = 4 * q + k
                            mm = pe.matmul(b[:, k * P:(k + 1) * P], prod[:, u, :], invT[:, u, :], start=True, stop=True)
                        end("v", mm, f"invT{q}")
                filled["prod_used"] = filled["invT3"]
                pe.wait_ge(scaled, 4)
                need("invT3")
                for d in range(2):
                    b = fill("a")
                    for k in range(8):
                        u = 8 * d + k
                        mm = pe.matmul(b[:, k * HD:(k + 1) * HD], invT[:, u, :], vbeta[:, u, :], start=True, stop=True)
                    end("a", mm, "uval")
                for d in range(2):
                    b = fill("a")
                    for par in range(2):
                        for t in range(TT):
                            for f in range(2):
                                u = ((2 * d + par) * TT + t) * 2 + f
                                mm = pe.matmul(b[par * HD:(par + 1) * HD, (2 * t + f) * P:(2 * t + f + 1) * P], kdec[:, u, :], invT[:, u, :],
                                               start=True, stop=True)
                    end("a", mm, "wT")
                for d in range(2):
                    b = fill("a")
                    for t in range(TT):
                        for f in range(2):
                            u0 = (2 * d + t) * NH + 2 * f
                            mm = pe.transpose(b[:, (2 * t + f) * P:(2 * t + f + 1) * P],
                                              qdec[:, u0:u0 + 2, :].rearrange("p u k -> p (u k)"), ident)
                    end("a", mm, "qdT")
                need("qdT")
                for s in range(4):
                    where = [(d, (s if d == 0 else 3 - s) // 2, (s if d == 0 else 3 - s) % 2) for d in range(2)]
                    if s:
                        pe.wait_ge(state_ready, 4 * s)
                        for par in range(2):
                            b = fill("v")
                            for d, t, hf in where:
                                for f in range(2):
                                    mm = pe.matmul(b[hf * HD:(hf + 1) * HD, f * HD:(f + 1) * HD],
                                                   wT[par * HD:(par + 1) * HD, d, t, f, hf * HD:(hf + 1) * HD],
                                                   state[par * HD:(par + 1) * HD, d, f, :], start=True, stop=True)
                            end("v", mm)
                        for par in range(2):
                            b = fill("a")
                            for d, t, hf in where:
                                for f in range(2):
                                    mm = pe.matmul(b[hf * HD:(hf + 1) * HD, f * HD:(f + 1) * HD],
                                                   qdT[par * HD:(par + 1) * HD, d, t, f, hf * HD:(hf + 1) * HD],
                                                   state[par * HD:(par + 1) * HD, d, f, :], start=True, stop=True)
                            end("a", mm, f"gdn_q{s}")
                    pe.wait_ge(vnew_ready, 4 * (s + 1))
                    b = fill("v")
                    for d, t, hf in where:
                        for par in range(2):
                            for f in range(2):
                                u = ((2 * d + par) * TT + t) * 2 + f
                                mm = pe.matmul(b[hf * HD:(hf + 1) * HD, (2 * par + f) * HD:(2 * par + f + 1) * HD],
                                               decay[hf * HD:(hf + 1) * HD, u, hf * HD:(hf + 1) * HD],
                                               vnew[hf * HD:(hf + 1) * HD, par, f, :], start=True, stop=True)
                    end("v", mm)
                    if s < 3:
                        for d, t, hf in where:
                            b = fill("v")
                            for par in range(2):
                                for f in range(2):
                                    u = ((2 * d + par) * TT + t) * 2 + f
                                    mm = pe.matmul(b[par * HD:(par + 1) * HD, f * HD:(f + 1) * HD],
                                                   kstate[hf * HD:(hf + 1) * HD, u, :], vnew[hf * HD:(hf + 1) * HD, par, f, :],
                                                   start=True, stop=True)
                            end("v", mm)
                pe.wait_ge(gdn_done, 1)
                b = fill("v")
                for f in range(2):
                    for t in range(TT):
                        mm = pe.transpose(b[:, f * T + t * P:f * T + (t + 1) * P], gdn_o[:, t * W + f * P:t * W + (f + 1) * P], ident)
                end("v", mm, "yD")

                for name in ("yA", "yB", "yC", "yD"):
                    need(name)
                for n in range(2):
                    unit(U_OUT + n)
                    token_major(U_OUT + n, 512, yT, "vv", "x_mix")

                turn_x("memT", mem_n, 1)
                need("memT")
                for n in range(2):
                    unit(U_MK + n)
                    feature_major(U_MK + n, 4, memT, "a", f"memK{n}")
                for n in range(2):
                    unit(U_MV + n)
                    token_major(U_MV + n, 512, memT, "aa", f"memV{n}")
                turn_x("xnT", xn, 2)
                need("xnT")
                for n in range(2):
                    unit(U_MQ + n)
                    feature_major(U_MQ + n, 4, xnT, "a", f"memQ{n}")
                need("memQ11")
                for h in range(NH):
                    b = fill("v")
                    for t in range(TT):
                        for ch in range(2):
                            mm = pe.matmul(b[:, t * T:(t + 1) * T], memQ[:, 2 * h + ch, t * P:(t + 1) * P], memK[:, 2 * h + ch, :],
                                           start=ch == 0, stop=ch == 1)
                    end("v", mm)
                turn_probs(1)
                for h in range(NH):
                    need(f"probT1{h}")
                    b = fill("a")
                    for ch in range(2):
                        for kc in range(2):
                            mm = pe.matmul(b[:, ch * T:(ch + 1) * T], memV[:, kc, h * T + ch * P:h * T + (ch + 1) * P], probT[:, h, kc, :],
                                           start=kc == 0, stop=kc == 1)
                    end("a", mm, "attT")
                need("attT")
                for n in range(2):
                    unit(U_MO + n)
                    token_major(U_MO + n, 512, attT, "vv", "x_mem")

                turn_x("xnT", xn, 3)
                need("xnT")
                pe.wait_ge(params_in, 16 * N_PARAMS)
                b = fill("v")
                for t in range(TT):
                    for ch in range(DC):
                        mm = pe.matmul(b[:, 36 * t:36 * t + 36], xnT[:, ch, t * P:(t + 1) * P], router_w[:, ch, :], start=ch == 0, stop=ch == DC - 1)
                end("v", mm)
                pe.wait_ge(ind_ready, 1)
                b = fill("v")
                pe.matmul(b[:, 0:NE], before, ranks[:, 0, :], start=True, stop=True)
                pe.matmul(b[:, NE:2 * NE], ones, ranks[:, 0, :], start=True, stop=False)
                pe.matmul(b[:, NE:2 * NE], before, ranks[:, 1, :], start=False, stop=True)
                pe.matmul(b[:, 2 * NE:3 * NE], ones, ranks[:, 0, :], start=True, stop=False)
                mm = pe.matmul(b[:, 2 * NE:3 * NE], ones, ranks[:, 1, :], start=False, stop=True)
                end("v", mm, "ranks")
                pe.wait_ge(np_ready, 1)
                rounds = pe.value_load(npi[0:1, 0:1], min_val=1, max_val=T // SLOTS)

                def expert_pass(it, use):
                    def unit(n):
                        pe.wait_ge(unit_in[n % NSLOT], 16 * (PRE_UNITS // NSLOT + n // NSLOT + 1) + 32 * use)
                        return ring[:, n % NSLOT, :].rearrange("p (e k) -> p e k", e=QUAD)

                    pe.wait_ge(sel_built, 2 * it)
                    for g in range(2):
                        for q in range(4):
                            for t in range(TT):
                                mm = pe.matmul(bank[g][:, q * P:(q + 1) * P], xn_by_row[:, t, 4 * g + q, :], sel[:, t, :],
                                               start=t == 0, stop=t == TT - 1)
                        mm.then_inc(gathered[g], 1)
                    for t in range(TT):
                        mm = pe.transpose(bank[2][:, t * P:(t + 1) * P], selw[:, t, :], ident)
                    mm.then_inc(sel_turned, 1)
                    pe.wait_ge(xg_ready[0], it)
                    pe.wait_ge(xg_ready[1], it)
                    for part in range(2):
                        for n in range(4):
                            w = unit(4 * part + n)
                            for q in range(2):
                                ch = 2 * n + q
                                for e in range(QUAD):
                                    mm = pe.matmul(bank[3 + part][e * SLOTS:(e + 1) * SLOTS, :], xg[:, ch, e * SLOTS:(e + 1) * SLOTS],
                                                   w[:, e, q * DE:(q + 1) * DE], start=ch == 0, stop=ch == DC - 1)
                            mm.then_inc((gate_full, up_full)[part] if n == 3 else units_free, 1)
                    pe.wait_ge(hid_ready, it)
                    for c4 in range(4):
                        mm = pe.transpose(bank[5][:, c4 * P:(c4 + 1) * P], hid_by_row[:, c4, :], ident)
                    mm.then_inc(hid_turned, 1)
                    pe.wait_ge(hidT_ready, it)
                    for c4 in range(4):
                        w = unit(8 + c4)
                        for n in range(2):
                            for e in range(QUAD):
                                mm = pe.matmul(bank[6 + n][e * SLOTS:(e + 1) * SLOTS, :], hidT[:, c4, e * SLOTS:(e + 1) * SLOTS],
                                               w[:, e, n * 512:(n + 1) * 512], start=c4 == 0, stop=c4 == 3)
                            if c4 == 3:
                                mm.then_inc(y_full[n], 1)
                            elif n == 1:
                                mm.then_inc(units_free, 1)
                    pe.drain().then_inc(units_free, 1)
                    pe.wait_ge(selwT_ready, it)
                    for n in range(2):
                        pe.wait_ge(y_ready[n], it)
                        for t in range(TT):
                            pe.matmul(bank[(0, 1, 2, 5)[2 * n + t]][:, :], selwT[:, t, :], y_e[:, n * 512:(n + 1) * 512],
                                      start=True, stop=True).then_inc(scattered[2 * n + t], 1)

                pe.wait_ge(vec_evac, count["v"])
                pe.wait_ge(act_evac, count["a"])
                with pe.Fori(0, rounds) as k:
                    with pe.Fori(0, NQ) as q:
                        expert_pass(NQ * k + q + 1, NQ * k + q)
                pe.drain().then_inc(layer_done, 1)
                pe.wait_ge(layer_go, l + 1)
                pe.sem_inc(layer_seen, 1)

        @block.vector
        def _(v):
            v.memset(mhalf[:], -0.5).then_inc(preset, 1)
            v.memset(small[:], 0.0).then_inc(preset, 1)
            v.wait_ge(preset, 2)
            v.wait_ge(const_in, 16)
            v.wait_ge(x_in, 16)

            with v.Fori(0, DEPTH) as l:
                n_own = [0]
                n_in = [0]

                def own(ins):
                    n_own[0] += 1
                    ins.then_inc(vec_step, 1)
                    v.wait_ge(vec_step, n_own[0])

                def take():
                    v.wait_ge(vec_full, n_in[0] + 1)
                    return bank[n_in[0] % 4]

                def taken(ins):
                    n_in[0] += 1
                    ins.then_inc(vec_evac, 1)
                    v.wait_ge(vec_evac, n_in[0])

                def norm(src, dst, k, gain):
                    v.wait_ge(squares, 2 * (k + 1))
                    v.tensor_scalar(ss[:, 2:4], ss[:, 0:2], 1.0 / D, EPS, ALU.mult, ALU.add).then_inc(means, 1)
                    v.wait_ge(rstds, k + 1)
                    for t in range(TT):
                        v.tensor_scalar(dst[:, t, :], src[:, t, :], rstd[:, t:t + 1], None, ALU.mult).then_inc(normed, 1)

                def take_turned(dstT, k):
                    for t in range(TT):
                        for g in range(2):
                            b = take()
                            taken(v.tensor_tensor(dstT[:, 4 * g:4 * g + 4, t * P:(t + 1) * P], b[:, :].rearrange("p (c k) -> p c k", c=4),
                                                  wide(gains[:, k, 4 * g:4 * g + 4], P), ALU.mult))

                def softmax(k, mask):
                    mx = dsm[:, 240:248].rearrange("p (h t) -> p h t", t=TT)
                    for h in range(NH):
                        b = take()
                        bv = b[:, :].rearrange("p (t k) -> p t k", t=TT)
                        if mask:
                            taken(v.tensor_tensor(prob[:, h], bv, again(c("band"), TT), ALU.add))
                        else:
                            taken(v.tensor_copy(prob[:, h], bv))
                        own(v.tensor_reduce(mx[:, h, :], prob[:, h], AX, ALU.max))
                        v.tensor_scalar(mx[:, h, :], mx[:, h, :], -1.0, None, ALU.mult).then_inc(maxed, 1)
                    for h in range(NH):
                        v.wait_ge(exped, 2 * (NH * k + h + 1))
                        own(v.reciprocal(stat[:, 2 * h:2 * h + 2], stat2[:, 2 * h:2 * h + 2]))
                        v.tensor_tensor(prob[:, h], prob[:, h], wide(stat[:, 2 * h:2 * h + 2], T), ALU.mult).then_inc(probs_ready, 1)

                v.wait_ge(params_in, 16 * N_PARAMS)
                norm(x, xn, 0, 0)
                take_turned(xnT, 0)
                for n in range(3):
                    b = take()
                    taken(v.tensor_copy(projv[:, 1, n * 512:(n + 1) * 512], b[:, :]))
                own(v.memset(conv_in[:, :, 0:2], 0.0))
                own(v.memset(conv_in[:, :, T + 2:T + 3], 0.0))
                for f in range(3):
                    b = take()
                    taken(v.tensor_copy(conv_in[:, 2 * f:2 * f + 2, 2:T + 2], b[:, :].rearrange("p (c t) -> p c t", c=2)))
                softmax(0, True)

                for n in range(2):
                    v.wait_ge(*done[f"tok{n}0"])
                for t in range(TT):
                    src = projv[:, t, PQ_B:PQ_B + 512].rearrange("p (h k) -> p h k", k=HD)
                    r1 = rot1[:, t, :].rearrange("p (h k) -> p h k", k=HD)
                    r2 = rot2[:, t, :].rearrange("p (h k) -> p h k", k=HD)
                    own(v.tensor_tensor(r1, src, again(rot_a[:, t, :], 8), ALU.mult))
                    own(v.tensor_tensor(r2[:, :, 0:32], src[:, :, 32:64], again(rot_b[:, t, 0:32], 8), ALU.mult))
                    own(v.tensor_tensor(r2[:, :, 32:64], src[:, :, 0:32], again(rot_b[:, t, 32:64], 8), ALU.mult))
                    v.tensor_tensor(r1, r1, r2, ALU.add).then_inc(rotated, 1)
                v.wait_ge(unit_in[slot(U_CONST)], landed(U_CONST))
                decays = ring[:, slot(U_CONST), 0:2048].rearrange("p (h k) -> p h k", h=NH)
                for h in range(NH):
                    b = take()
                    taken(v.tensor_tensor(retS[:, h, :], b[:, :], decays[:, h, :], ALU.mult))
                b = take()
                taken(v.tensor_copy(ret_o, b[:, :]))
                o3 = ret_o.rearrange("p (u k) -> p u k", k=HD)
                s3 = ret_s.rearrange("p (u k) -> p u k", k=HD)
                own(v.tensor_reduce(stat[:, 0:8], o3, AX, ALU.add))
                own(v.tensor_scalar(stat[:, 0:8], stat[:, 0:8], 1.0 / HD, None, ALU.mult))
                own(v.tensor_tensor(o3, o3, wide(stat[:, 0:8], HD), ALU.subtract))
                own(v.tensor_tensor(s3, o3, o3, ALU.mult))
                own(v.tensor_reduce(stat[:, 0:8], s3, AX, ALU.add))
                v.tensor_scalar(stat[:, 8:16], stat[:, 0:8], 1.0 / HD, EPS, ALU.mult, ALU.add).then_inc(ret_var, 1)
                v.wait_ge(ret_rstd, 1)
                own(v.tensor_tensor(o3, o3, wide(stat[:, 0:8], HD), ALU.mult))
                v.wait_ge(ret_silu, 1)
                v.tensor_tensor(ret_o, ret_o, ret_g, ALU.mult).then_inc(ret_done, 1)
                b = take()
                taken(v.tensor_tensor(yT[:, 4:6, :], b[:, :].rearrange("p (c t) -> p c t", c=2), wide(cols[:, 2:4], T), ALU.mult))
                b = take()
                taken(v.tensor_tensor(yT[:, 2:4, :], b[:, :].rearrange("p (c t) -> p c t", c=2), wide(cols[:, 0:2], T), ALU.mult))

                for ch in range(6):
                    o = xnT[:, ch, :]
                    own(v.tensor_scalar(o, conv_in[:, ch, 0:T], conv_w[:, 0, ch:ch + 1], None, ALU.mult))
                    for k in range(1, 4):
                        ins = v.scalar_tensor_tensor(out=o, in0=conv_in[:, ch, k:k + T], scalar=conv_w[:, k, ch:ch + 1], in1=o, op0=ALU.mult, op1=ALU.add)
                        if k < 3:
                            own(ins)
                        else:
                            ins.then_inc(conved, 1)
                v.wait_ge(conved, 6)
                for t in range(TT):
                    v.wait_ge(*done[f"gate{t}"])
                ab = projv[:, :, PAB:PAB + 16]
                t16 = lambda k: dcol(k).rearrange("p (t u) -> p t u", t=TT)
                own(v.tensor_tensor(t16(T0), ab[:, :, 0:8], again(rows[:, 8:16], TT), ALU.add))
                own(v.tensor_scalar(t16(T1), t16(T0), -1.0, None, ALU.mult))
                own(v.tensor_tensor(t16(T1), t16(T1), t16(T0), ALU.min))
                own(v.tensor_scalar(t16(T0), t16(T0), 0.0, None, ALU.max))
                v.tensor_copy(t16(T2), ab[:, :, 8:16]).then_inc(gate_in, 1)
                for t in range(TT):
                    b = take()
                    taken(v.tensor_copy(qkv[:, t, 0:512], b[:, :]))
                    b = take()
                    taken(v.tensor_copy(qkv[:, t, 512:768], b[:, 0:256]))
                for t in range(TT):
                    own(v.tensor_tensor(m4[:, 512 * t:512 * (t + 1)], qkv[:, t, 0:512], qkv[:, t, 0:512], ALU.mult))
                own(v.tensor_reduce(stat, m4[:, 0:1024].rearrange("p (u k) -> p u k", k=HD), AX, ALU.add))
                v.tensor_scalar(stat2, stat, EPS, None, ALU.add).then_inc(qk_sums, 1)
                v.wait_ge(gate_exp, 3)
                own(v.tensor_scalar(t16(T2), t16(T2), 1.0, None, ALU.add))
                own(v.reciprocal(dcol(BETA), dcol(T2)))
                v.wait_ge(gate_ln, 1)
                own(v.tensor_tensor(t16(T0), t16(T0), t16(T1), ALU.add))
                own(v.tensor_tensor(t16(T0), t16(T0), again(dcol(T3, 8), TT), ALU.mult))
                own(v.tensor_scalar(dcol(G), dcol(T0), -1.0, None, ALU.mult))
                own(v.tensor_scalar(gmask[:, 0, :], dcol(G), halves[:, 0:1], None, ALU.mult))
                v.tensor_scalar(gmask[:, 1, :], dcol(G), halves[:, 1:2], None, ALU.mult).then_inc(g_ready, 1)
                v.wait_ge(qk_rstd, 1)
                stat_t = stat.rearrange("p (t u) -> p t u", t=TT)
                own(v.tensor_scalar(stat_t[:, :, 0:4], stat_t[:, :, 0:4], HD ** -0.5, None, ALU.mult))
                for t in range(TT):
                    q3 = qkv[:, t, 0:512].rearrange("p (u k) -> p u k", k=HD)
                    v.tensor_tensor(q3, q3, wide(stat[:, 8 * t:8 * t + 8], HD), ALU.mult).then_inc(qk_ready, 1)
                b = take()
                own(v.tensor_copy(dsm[:, 16 * GC:16 * GC + 32], b[:, 0:32]))
                own(v.tensor_tensor(dcol(T0), dcol(GL), dcol(GC), ALU.subtract))
                taken(v.tensor_copy(egl, b[:, 32:48]))
                v.tensor_copy(dcol(T1), dcol(GC)).then_inc(gdiff, 1)
                gc4 = unit_col(GC)
                for d in range(2):
                    for par in range(2):
                        b = take()
                        for k in range(4):
                            t, f = k // 2, k % 2
                            ins = v.tensor_scalar(decay[:, (2 * d + par) * 4 + k, :], b[:, k * P:(k + 1) * P],
                                                  gc4[:, t, d, 2 * f + par:2 * f + par + 1], 0.0, ALU.subtract, ALU.min)
                        taken(ins)
                v.wait_ge(dec_masked, 4)
                kk = [None, None]
                for par in range(2):
                    b = take()
                    for d in range(2):
                        u0 = (2 * d + par) * 4
                        ins = v.tensor_tensor(lT[:, u0:u0 + 4, :], b[:, :].rearrange("p (u k) -> p u k", u=4), decay[:, u0:u0 + 4, :], ALU.mult)
                    taken(ins)
                for par in range(2):
                    b = take()
                    for d in range(2):
                        u0 = (2 * d + par) * 4
                        ins = v.tensor_tensor(decay[:, u0:u0 + 4, :], b[:, :].rearrange("p (u k) -> p u k", u=4), decay[:, u0:u0 + 4, :], ALU.mult)
                    taken(ins)
                for q in range(4):
                    b = take()
                    taken(v.tensor_tensor(lT[:, 4 * q:4 * q + 4, :], b[:, :].rearrange("p (u k) -> p u k", u=4), lT[:, 4 * q:4 * q + 4, :], ALU.mult))
                own(v.tensor_copy(stat2, stat))
                v.tensor_copy(stat, stat2).then_inc(lT_ready, 1)
                for q in range(4):
                    d = q // 2
                    o = invT[:, 4 * q:4 * q + 4, :]
                    own(v.tensor_tensor(o, lT[:, 4 * q:4 * q + 4, :], again(level[:, 0, d, :], 4), ALU.mult))
                    v.tensor_tensor(o, again(ident, 4), o, ALU.subtract).then_inc(inv0_ready, 1)
                for n in range(1, LEVELS):
                    for q in range(4):
                        for m in ((inv, invT) if n < LEVELS - 1 else (invT,)):
                            if n == 1 and m is inv:
                                v.wait_ge(*done[f"inv0{q}"])
                            b = take()
                            o = m[:, 4 * q:4 * q + 4, :]
                            taken(v.tensor_tensor(o, o, b[:, :].rearrange("p (u k) -> p u k", u=4), ALU.subtract))
                v.wait_ge(gexp, 3)
                v.wait_ge(*filled["prod_used"])
                b4, e4, s4 = unit_col(BETA), unit_col(EGC), unit_col(ESL)
                own(v.tensor_tensor(dcol(T0), dcol(BETA), dcol(EGC), ALU.mult))
                be4 = unit_col(T0)
                for d in range(2):
                    for par in range(2):
                        for t in range(TT):
                            u0 = ((2 * d + par) * TT + t) * 2
                            v4 = qkv[:, t, :].rearrange("p (w f a k) -> p w a f k", w=3, f=2, a=2)
                            for dst, w, col in ((vbeta, 2, b4), (kdec, 1, be4), (kstate, 1, s4)):
                                ins = v.tensor_tensor(dst[:, u0:u0 + 2, :], v4[:, w, par], wide(col[:, t, d, par::2], HD), ALU.mult)
                                if d == 1 and par == 1 and t == 1:
                                    ins.then_inc(scaled, 1)
                for d in range(2):
                    for t in range(TT):
                        ins = v.tensor_tensor(qdec[:, (2 * d + t) * NH:(2 * d + t + 1) * NH, :], qkv[:, t, 0:W].rearrange("p (h k) -> p h k", h=NH),
                                              wide(e4[:, t, d, :], HD), ALU.mult)
                ins.then_inc(scaled, 1)
                v.wait_ge(*done["uval"])
                v.wait_ge(*done["qdT"])
                ov = gdn_o.rearrange("p (d t f a e) -> p d t a f e", d=2, t=TT, f=2, a=2)
                u6 = uval.rearrange("p (d a t f) e -> p d a t f e", d=2, a=2, t=TT)
                for s in range(4):
                    where = [(d, (s if d == 0 else 3 - s) // 2, (s if d == 0 else 3 - s) % 2) for d in range(2)]
                    for par in range(2):
                        if s:
                            b = take()
                        for d, t, hf in where:
                            r = slice(hf * HD, (hf + 1) * HD)
                            if s:
                                ins = v.tensor_tensor(vnew[r, par], u6[r, d, par, t], b[r, 0:P].rearrange("p (f e) -> p f e", f=2), ALU.subtract)
                            else:
                                ins = v.tensor_copy(vnew[r, par], u6[r, d, par, t])
                            if d == 0 or not s:
                                ins.then_inc(vnew_ready, 1)
                            else:
                                ins.then_inc(vnew_ready, 1)
                        if s:
                            own(v.tensor_copy(stat2[:, 0:1], stat2[:, 1:2]))
                            taken(v.tensor_copy(stat2[:, 0:1], b[:, 0:1]))
                    if s:
                        v.wait_ge(*done[f"gdn_q{s}"])
                    b = take()
                    for d, t, hf in where:
                        r = slice(hf * HD, (hf + 1) * HD)
                        bv = b[r, 0:256].rearrange("p (a f e) -> p a f e", a=2, f=2)
                        for par in range(2):
                            if s:
                                ins = v.tensor_tensor(ov[r, d, t, par], gdn_q[r, par], bv[:, par], ALU.add)
                            else:
                                ins = v.tensor_copy(ov[r, d, t, par], bv[:, par])
                    taken(ins)
                    if s < 3:
                        for d, t, hf in where:
                            b = take()
                            for f in range(2):
                                k = ((hf * TT + t) * 2 + d) * 2 + f
                                if s:
                                    v.scalar_tensor_tensor(out=state[:, d, f, :], in0=state[:, d, f, :], scalar=egl[:, k:k + 1],
                                                           in1=b[:, f * HD:(f + 1) * HD], op0=ALU.mult, op1=ALU.add).then_inc(state_ready, 1)
                                else:
                                    v.tensor_copy(state[:, d, f, :], b[:, f * HD:(f + 1) * HD]).then_inc(state_ready, 1)
                            own(v.tensor_copy(stat2[:, 0:1], stat2[:, 1:2]))
                            taken(v.tensor_copy(stat2[:, 0:1], b[:, 0:1]))
                        v.wait_ge(state_ready, 4 * (s + 1))
                g3 = gdn_o[:, 0:512].rearrange("p (u k) -> p u k", k=HD)
                own(v.tensor_tensor(gdn_o[:, 0:512], gdn_o[:, 0:512], gdn_o[:, 512:1024], ALU.add))
                own(v.tensor_tensor(gdn_o[:, 512:1024], gdn_o[:, 0:512], gdn_o[:, 0:512], ALU.mult))
                own(v.tensor_reduce(stat[:, 0:8], gdn_o[:, 512:1024].rearrange("p (u k) -> p u k", k=HD), AX, ALU.add))
                v.tensor_scalar(stat[:, 8:16], stat[:, 0:8], 1.0 / HD, EPS, ALU.mult, ALU.add).then_inc(gdn_var, 1)
                v.wait_ge(gdn_rstd, 1)
                own(v.tensor_tensor(g3, g3, wide(stat[:, 0:8], HD), ALU.mult))
                v.wait_ge(gdn_silu, 1)
                v.tensor_tensor(gdn_o[:, 0:512].rearrange("p (t k) -> p t k", t=TT), gdn_o[:, 0:512].rearrange("p (t k) -> p t k", t=TT),
                                projv[:, :, PG_D:PG_D + W], ALU.mult).then_inc(gdn_done, 1)
                b = take()
                taken(v.tensor_scalar(yT[:, 6:8, :], b[:, :].rearrange("p (c t) -> p c t", c=2), cols[:, 4:5], None, ALU.mult))

                def add_to_x():
                    for n in range(2):
                        for t in range(TT):
                            b = take()
                            o = x[:, t, n * 512:(n + 1) * 512]
                            taken(v.tensor_tensor(o, o, b[:, :], ALU.add))

                add_to_x()
                norm(mem_tok, mem_n, 1, 2)
                take_turned(memT, 2)
                norm(x, xn, 2, 1)
                take_turned(xnT, 1)
                softmax(1, False)
                add_to_x()
                norm(x, xn, 3, 3)
                take_turned(xnT, 3)

                b = take()
                taken(v.tensor_tensor(logit, b[:, 0:72].rearrange("p (t k) -> p t k", t=TT), again(rows[:, 16:52], TT), ALU.add))
                rt = lambda k: small[:, 80 + 16 * k:96 + 16 * k].rearrange("p (t k) -> p t k", t=TT)
                GP, EL, E1, OH1, OH2, GOH, DF, W1, W2 = (rt(k) for k in range(9))
                own(v.tensor_scalar(GP, logit[:, :, 0:8], 0.0, NEG, ALU.mult, ALU.add))
                own(v.tensor_copy(GP[:, :, 0:4], logit[:, :, 0:4]))
                for t in range(TT):
                    own(v.max(val[:, 0, t, :], GP[:, t, :]))
                    own(v.max_index(idx[:, 0, t, :], val[:, 0, t, :], GP[:, t, :]))
                g1 = DF[:, :, 0:1]
                own(v.tensor_copy(g1, idx[:, 0, :, 0:1]))
                for t in range(TT):
                    own(v.tensor_scalar(GOH[:, t, :], c("eight"), g1[:, t, :], None, ALU.is_equal))
                for t in range(TT):
                    own(v.tensor_scalar(W1[:, t, 0:4], GP[:, t, 0:4], val[:, 0, t, 0:1], None, ALU.subtract))
                for t in range(TT):
                    own(v.tensor_scalar(EL[:, t, :], logit[:, t, 4:12], GOH[:, t, 0:1], None, ALU.mult))
                    for g in range(1, NG):
                        own(v.scalar_tensor_tensor(out=EL[:, t, :], in0=logit[:, t, 4 + 8 * g:12 + 8 * g], scalar=GOH[:, t, g:g + 1], in1=EL[:, t, :],
                                                   op0=ALU.mult, op1=ALU.add))
                    own(v.max(val[:, 1, t, :], EL[:, t, :]))
                    own(v.max_index(idx[:, 1, t, :], val[:, 1, t, :], EL[:, t, :]))
                own(v.tensor_copy(DF[:, :, 0:2], idx[:, 1, :, 0:2]))
                for t in range(TT):
                    own(v.tensor_scalar(OH1[:, t, :], c("eight"), DF[:, t, 0:1], None, ALU.is_equal))
                    own(v.tensor_scalar(OH2[:, t, :], c("eight"), DF[:, t, 1:2], None, ALU.is_equal))
                v.tensor_tensor(W1[:, :, 4:5], val[:, 1, :, 1:2], val[:, 1, :, 0:1], ALU.subtract).then_inc(r_max, 1)
                v.wait_ge(r_exp, 1)
                own(v.tensor_reduce(DF[:, :, 2], W2[:, :, 0:4], AX, ALU.add))
                own(v.tensor_scalar(DF[:, :, 3:4], W2[:, :, 4:5], 1.0, None, ALU.add))
                own(v.tensor_tensor(DF[:, :, 4:5], DF[:, :, 2:3], DF[:, :, 3:4], ALU.mult))
                own(v.reciprocal(DF[:, :, 5:6], DF[:, :, 4:5]))
                own(v.tensor_tensor(DF[:, :, 6:7], DF[:, :, 5:6], W2[:, :, 4:5], ALU.mult))
                for t in range(TT):
                    own(v.tensor_tensor(E1[:, t, :], OH1[:, t, :], OH2[:, t, :], ALU.add))
                    own(v.tensor_scalar(W1[:, t, :], OH1[:, t, :], DF[:, t, 5:6], None, ALU.mult))
                    own(v.scalar_tensor_tensor(out=W1[:, t, :], in0=OH2[:, t, :], scalar=DF[:, t, 6:7], in1=W1[:, t, :], op0=ALU.mult, op1=ALU.add))
                    for g in range(NG):
                        own(v.tensor_scalar(gates[:, t, 8 * g:8 * g + 8], W1[:, t, :], GOH[:, t, g:g + 1], None, ALU.mult))
                        own(v.tensor_scalar(ranks[:, t, 8 * g:8 * g + 8], E1[:, t, :], GOH[:, t, g:g + 1], None, ALU.mult))
                own(v.tensor_copy(stat, stat2))
                v.tensor_copy(stat2, stat).then_inc(ind_ready, 1)
                b = take()
                ind = small[:, 256:320].rearrange("p (t e) -> p t e", t=TT)
                own(v.tensor_copy(ind, ranks[:, :, :]))
                own(v.scalar_tensor_tensor(out=ranks[:, :, :], in0=b[:, 0:2 * NE].rearrange("p (t e) -> p t e", t=TT), scalar=1.0, in1=ind,
                                           op0=ALU.add, op1=ALU.mult))
                own(v.tensor_scalar(ranks[:, :, :], ranks[:, :, :], -1.0, None, ALU.add))
                taken(v.tensor_reduce(stat[:, 0:1], b[:, 2 * NE:3 * NE], AX, ALU.max))
                own(v.tensor_scalar(stat[:, 1:2], stat[:, 0:1], 0.0, None, ALU.mult))
                for k in range(1, T // SLOTS):
                    own(v.scalar_tensor_tensor(out=stat[:, 1:2], in0=stat[:, 0:1], scalar=float(k * SLOTS), in1=stat[:, 1:2], op0=ALU.is_gt, op1=ALU.add))
                v.tensor_scalar(npi[0:1, 0:1], stat[0:1, 1:2], 1.0, None, ALU.add).then_inc(np_ready, 1)
                v.wait_ge(np_ready, 1)
                rounds = v.value_load(npi[0:1, 0:1], min_val=1, max_val=T // SLOTS)

                def expert_pass(it, before_it, q):
                    v.tensor_copy(rank_q[:], ranks[:, :, bass.ds(QUAD * q, QUAD)]).then_inc(quad_ready, 1)
                    v.tensor_copy(gate_q[:], gates[:, :, bass.ds(QUAD * q, QUAD)]).then_inc(quad_ready, 1)
                    v.wait_ge(quad_ready, 2 * it)
                    s3 = sel.rearrange("p t (e s) -> p (t e) s", e=QUAD)
                    w3 = selw.rearrange("p t (e s) -> p (t e) s", e=QUAD)
                    slots8 = again(c("slot"), TT * QUAD)
                    v.tensor_tensor(s3, slots8, wide(rank_q[:].rearrange("p t e -> p (t e)"), SLOTS), ALU.is_equal).then_inc(sel_built, 1)
                    v.wait_ge(sel_built, 2 * before_it + 1)
                    v.tensor_tensor(w3, s3, wide(gate_q[:].rearrange("p t e -> p (t e)"), SLOTS), ALU.mult).then_inc(sel_built, 1)
                    for g in range(2):
                        v.wait_ge(gathered[g], it)
                        v.tensor_tensor(xg[:, 4 * g:4 * g + 4, :], bank[g][:, :].rearrange("p (c s) -> p c s", c=4),
                                        wide(gains[:, 4, 4 * g:4 * g + 4], P), ALU.mult).then_inc(xg_ready[g], 1)
                    v.wait_ge(silu_ready, it)
                    v.wait_ge(up_full, it)
                    v.tensor_tensor(hid, silu_g, bank[4][:, :], ALU.mult).then_inc(hid_ready, 1)
                    for n in range(2):
                        for t in range(TT):
                            v.wait_ge(scattered[2 * n + t], it)
                            o = x[:, t, n * 512:(n + 1) * 512]
                            v.tensor_tensor(o, o, bank[(0, 1, 2, 5)[2 * n + t]][:, :], ALU.add).then_inc(x_added, 1)
                    v.wait_ge(x_added, 4 * it)
                    v.sem_inc(pass_seen, 1)

                with v.Fori(0, rounds) as k:
                    with v.Fori(0, NQ) as q:
                        expert_pass(NQ * k + q + 1, NQ * k + q, q)
                    v.tensor_scalar(ranks[:, :, :], ranks[:, :, :], -float(SLOTS), None, ALU.add).then_inc(ranks_moved, 1)
                    v.wait_ge(ranks_moved, k + 1)
                    v.sem_inc(pass_seen, 1)
                v.drain().then_inc(layer_done, 1)
                v.wait_ge(layer_go, l + 1)
                v.sem_inc(layer_seen, 1)

            v.wait_ge(last_sq, 2)
            v.tensor_scalar(ss[:, 2:4], ss[:, 0:2], 1.0 / D, EPS, ALU.mult, ALU.add).then_inc(last_mean, 1)
            v.wait_ge(last_rstd, 1)
            v.wait_ge(final_in, 16)
            for t in range(TT):
                v.scalar_tensor_tensor(out=xn[:, t, :], in0=x[:, t, :], scalar=rstd[:, t:t + 1], in1=m1[:, 0:D], op0=ALU.mult, op1=ALU.mult).then_inc(last_out, 1)

        @block.scalar
        def _(s):
            s.wait_ge(x_in, 16)
            with s.Fori(0, DEPTH) as l:
                n_in = [0]

                def take():
                    s.wait_ge(act_full, n_in[0] + 1)
                    return bank[4 + n_in[0] % 4]

                def taken(ins):
                    n_in[0] += 1
                    ins.then_inc(act_evac, 1)

                def squares_of(src, junk):
                    for t in range(TT):
                        s.activation(junk[:, t, :], src[:, t, :], ACT.Square, accum_out=ss[:, t:t + 1]).then_inc(squares, 1)

                def exps(k):
                    for h in range(NH):
                        s.wait_ge(maxed, NH * k + h + 1)
                        for t in range(TT):
                            s.activation(prob[:, h, t, :], prob[:, h, t, :], ACT.Exp, bias=dsm[:, 240 + 2 * h + t:241 + 2 * h + t],
                                         accum_out=stat2[:, 2 * h + t:2 * h + t + 1]).then_inc(exped, 1)

                squares_of(x, xn)
                b = take()
                taken(s.mul(aqkT[:, 0:2, :], b[:, :].rearrange("p (c t) -> p c t", c=2), HD ** -0.5))
                b = take()
                taken(s.copy(aqkT[:, 2:4, :], b[:, :].rearrange("p (c t) -> p c t", c=2)))
                for n in range(3):
                    b = take()
                    taken(s.copy(projv[:, 0, n * 512:(n + 1) * 512], b[:, :]))
                for t in range(TT):
                    b = take()
                    taken(s.copy(projv[:, t, PG_D:PW], b[:, 0:PW - PG_D]))
                exps(0)
                for h in range(NH):
                    b = take()
                    taken(s.copy(probT[:, h].rearrange("p c q -> p (c q)"), b[:, :]))
                b = take()
                taken(s.copy(yT[:, 0:2, :], b[:, :].rearrange("p (c t) -> p c t", c=2)))
                for t in range(TT):
                    b = take()
                    taken(s.copy(bqkT[:, :, t * P:(t + 1) * P], b[:, :].rearrange("p (c k) -> p c k", c=4)))
                s.wait_ge(*done["tok21"])
                s.wait_ge(*done["tok20"])
                s.wait_ge(*filled["bqkT"])
                s.wait_ge(rotated, 2)
                s.activation(ret_g.rearrange("p (t k) -> p t k", t=TT), projv[:, :, PG_B:PG_B + W], ACT.Silu).then_inc(ret_silu, 1)
                for f in range(2):
                    b = take()
                    taken(s.copy(diffT[:, 2 * f:2 * f + 2, :], b[0:HD, :].rearrange("p (c t) -> p c t", c=2)))
                for ch in range(6):
                    s.wait_ge(conved, ch + 1)
                    s.activation(xnT[:, ch, :], xnT[:, ch, :], ACT.Silu).then_inc(conv_silu, 1)
                s.wait_ge(*done["gate1"])
                s.activation(projv[:, :, PG_D:PG_D + W], projv[:, :, PG_D:PG_D + W], ACT.Silu).then_inc(gdn_silu, 1)
                s.wait_ge(gate_in, 1)
                s.wait_ge(params_in, 16 * N_PARAMS)
                s.activation(dcol(T1), dcol(T1), ACT.Exp).then_inc(gate_exp, 1)
                s.activation(dcol(T2), dcol(T2), ACT.Exp, scale=-1.0).then_inc(gate_exp, 1)
                s.activation(dcol(T3, 8), rows[:, 0:8], ACT.Exp).then_inc(gate_exp, 1)
                s.wait_ge(gate_exp, 3)
                s.activation(dcol(T1), dcol(T1), ACT.Ln, bias=1.0).then_inc(gate_ln, 1)
                for t in range(TT):
                    b = take()
                    taken(s.copy(qkT[:, 0:4, t * P:(t + 1) * P], b[:, :].rearrange("p (c k) -> p c k", c=4)))
                s.wait_ge(gdiff, 1)
                s.activation(dcol(EGC), dcol(T1), ACT.Exp).then_inc(gexp, 1)
                s.activation(dcol(ESL), dcol(T0), ACT.Exp).then_inc(gexp, 1)
                s.wait_ge(*done["gc"])
                s.activation(egl, egl, ACT.Exp).then_inc(gexp, 1)
                for q in range(4):
                    s.wait_ge(vec_evac, done["gc"][1] + q + 1)
                    o = decay[:, 4 * q:4 * q + 4, :]
                    s.activation(o, o, ACT.Exp).then_inc(dec_exp, 1)
                for q in range(4):
                    b = take()
                    taken(s.copy(inv[:, 4 * q:4 * q + 4, :], b[:, :].rearrange("p (u k) -> p u k", u=4)))
                for n in range(1, LEVELS):
                    for q in range(4):
                        b = take()
                        taken(s.copy(prod[:, 4 * q:4 * q + 4, :], b[:, :].rearrange("p (u k) -> p u k", u=4)))
                for d in range(2):
                    b = take()
                    taken(s.copy(uval[:, 8 * d:8 * d + 8, :], b[:, :].rearrange("p (u k) -> p u k", u=8)))
                for dst in (wT, qdT):
                    for d in range(2):
                        b = take()
                        taken(s.copy(dst[:, d].rearrange("p t f k -> p (t f) k"), b[:, :].rearrange("p (u k) -> p u k", u=4)))
                for step in range(1, 4):
                    for par in range(2):
                        b = take()
                        if step > 1:
                            s.wait_ge(state_ready, 4 * step)
                        taken(s.copy(gdn_q[:, par], b[:, 0:P].rearrange("p (f e) -> p f e", f=2)))
                s.wait_ge(mem_in, 16)
                squares_of(mem_tok, mem_n)
                for n in range(2):
                    for f in range(2):
                        b = take()
                        taken(s.copy(memK[:, 4 * n + 2 * f:4 * n + 2 * f + 2, :], b[:, :].rearrange("p (c t) -> p c t", c=2)))
                for n in range(2):
                    for t in range(TT):
                        b = take()
                        taken(s.copy(memV[:, t, n * 512:(n + 1) * 512], b[:, :]))
                s.wait_ge(vec_evac, done["x_mix1"][1])
                s.wait_ge(normed, 4)
                squares_of(x, xn)
                for n in range(2):
                    for f in range(2):
                        b = take()
                        taken(s.mul(memQ[:, 4 * n + 2 * f:4 * n + 2 * f + 2, :], b[:, :].rearrange("p (c t) -> p c t", c=2), 256 ** -0.5))
                exps(1)
                for h in range(NH):
                    b = take()
                    taken(s.copy(probT[:, h].rearrange("p c q -> p (c q)"), b[:, :]))
                for h in range(NH):
                    b = take()
                    taken(s.copy(attT[:, 2 * h:2 * h + 2, :], b[:, :].rearrange("p (c t) -> p c t", c=2)))
                s.wait_ge(*done["x_mem1"])
                squares_of(x, xn)
                s.wait_ge(r_max, 1)
                rw = small[:, 80 + 16 * 7:80 + 16 * 9].rearrange("p (w t k) -> p w t k", w=2, t=TT)
                s.activation(rw[:, 1, :, 0:5], rw[:, 0, :, 0:5], ACT.Exp).then_inc(r_exp, 1)
                s.wait_ge(np_ready, 1)
                rounds = s.value_load(npi[0:1, 0:1], min_val=1, max_val=T // SLOTS)

                def expert_pass(it):
                    s.wait_ge(sel_turned, it)
                    s.copy(selwT, bank[2][:, 0:T].rearrange("p (t k) -> p t k", t=TT)).then_inc(selwT_ready, 1)
                    s.wait_ge(gate_full, it)
                    s.activation(silu_g, bank[3][:, :], ACT.Silu).then_inc(silu_ready, 1)
                    s.wait_ge(hid_turned, it)
                    s.copy(hidT, bank[5][:, :].rearrange("p (c s) -> p c s", c=4)).then_inc(hidT_ready, 1)
                    for n in range(2):
                        s.wait_ge(y_full[n], it)
                        s.copy(y_e[:, n * 512:(n + 1) * 512], bank[6 + n][:, :]).then_inc(y_ready[n], 1)

                with s.Fori(0, rounds) as k:
                    with s.Fori(0, NQ) as q:
                        expert_pass(NQ * k + q + 1)
                s.drain().then_inc(layer_done, 1)
                s.wait_ge(layer_go, l + 1)
                s.sem_inc(layer_seen, 1)
            for t in range(TT):
                s.activation(xn[:, t, :], x[:, t, :], ACT.Square, accum_out=ss[:, t:t + 1]).then_inc(last_sq, 1)

        @block.gpsimd
        def _(g):
            g.wait_ge(preset, 2)
            g.wait_ge(const_in, 16)
            with g.Fori(0, DEPTH) as l:
                def root(k):
                    g.wait_ge(means, k + 1)
                    g.tensor_tensor(rstd[:, 0:2], ss[:, 2:4], mhalf[:, 0:2], ALU.pow).then_inc(rstds, 1)

                root(0)
                g.wait_ge(ret_var, 1)
                g.tensor_tensor(stat[:, 0:8], stat[:, 8:16], mhalf[:, 0:8], ALU.pow).then_inc(ret_rstd, 1)
                g.wait_ge(qk_sums, 1)
                g.tensor_tensor(stat, stat2, mhalf[:], ALU.pow).then_inc(qk_rstd, 1)
                for q in range(4):
                    g.wait_ge(dec_exp, q + 1)
                    o = decay[:, 4 * q:4 * q + 4, :]
                    g.tensor_tensor(o, o, again(tri[:, q // 2, :], 4), ALU.mult).then_inc(dec_masked, 1)
                g.wait_ge(lT_ready, 1)
                for n in range(1, LEVELS):
                    if n > 1:
                        g.wait_ge(*filled[f"low_used{n - 1}"])
                    for d in range(2):
                        g.tensor_tensor(low[:, 8 * d:8 * d + 8, :], lT[:, 8 * d:8 * d + 8, :], again(level[:, n, d, :], 8), ALU.mult).then_inc(low_ready, 1)
                g.wait_ge(gdn_var, 1)
                g.tensor_tensor(stat[:, 0:8], stat[:, 8:16], mhalf[:, 0:8], ALU.pow).then_inc(gdn_rstd, 1)
                for k in range(1, 4):
                    root(k)
                g.drain().then_inc(layer_done, 1)
                g.wait_ge(layer_go, l + 1)
                g.sem_inc(layer_seen, 1)
            g.wait_ge(last_mean, 1)
            g.tensor_tensor(rstd[:, 0:2], ss[:, 2:4], mhalf[:, 0:2], ALU.pow).then_inc(last_rstd, 1)

        @block.sync
        def _(sp):
            sp.dma_start(const[:], a["consts"]).then_inc(const_in, 16)
            sp.dma_start(x[:], a["x"].rearrange("b (t p) d -> p (b t) d", p=P)).then_inc(x_in, 16)
            with sp.Fori(0, DEPTH) as l:
                lay = lambda name: a[name][bass.ds(l, 1)]
                n_par = [0]

                def param(dst, src):
                    sp.dma_start(dst, src, allow_slow_non_contiguous=True).then_inc(params_in, 16)
                    n_par[0] += 1

                for k, name in enumerate(("mix_norm_g", "mem_q_norm_g", "mem_kv_norm_g", "ffn_norm_g")):
                    param(gains[:, k, :], lay(name).rearrange("l (c p) -> p (l c)", p=P))
                param(gains[:, 4, :], lay("ffn_norm_g").rearrange("l (p c) -> p (l c)", p=P))

                def load(n, dst, src):
                    if n >= NSLOT:
                        sp.wait_ge(*last_reader[n - NSLOT])
                    sp.dma_start(dst, src).then_inc(unit_in[slot(n)], 16)

                w_in = lambda lo, hi: lay("w_in")[:, :, lo:hi].rearrange("l (c p) n -> p (l c) n", p=P)
                part = lambda n, k: ring[:, slot(n), 0:DC * k].rearrange("p (c k) -> p c k", c=DC)
                half = lambda name, n: lay(name)[:, :, 512 * n:512 * (n + 1)].rearrange("l (c p) n -> p (l c) n", p=P)
                load(U_AQK, part(U_AQK, 512), w_in(0, 512))
                for n in range(3):
                    load(U_TOK + n, part(U_TOK + n, 512), w_in(512 + 512 * n, 1024 + 512 * n))
                load(U_GATE, part(U_GATE, 272), w_in(2816, 3088))
                load(U_DQK, part(U_DQK, 512), w_in(2048, 2560))
                for t in range(TT):
                    for r in range(2):
                        for h in range(NH):
                            row = 2 * t + r
                            src = bass.AP(a["na_rpb"].tensor, l * (NH * RPB_H * RPB_W) + ((7 - row) * RPB_W + 15 - 63 + RPB_H * RPB_W * h),
                                          [[1, GRID_W], [RPB_W, ROWS], [1, GRID_W]])
                            sp.dma_start(bias[GRID_W * r:GRID_W * (r + 1), t, h, :].rearrange("p (r k) -> p r k", r=ROWS), src).then_inc(rpb_in, 16)
                param(cols[:, 0:2], lay("ret_norm_g").rearrange("l (c p) -> p (l c)", p=P))
                param(cols[:, 2:4], lay("pool_scale").rearrange("l (c p) -> p (l c)", p=P))
                for k in range(2):
                    param(cols[k * HD:(k + 1) * HD, 4:5], lay("gdn_norm_g").rearrange("l p -> p l"))
                for k in range(4):
                    param(conv_w[:, k, :], lay("gdn_conv_w")[:, k, :].rearrange("l (c p) -> p (l c)", p=P))
                param(rows[:, 0:8], lay("gdn_a_log").rearrange("l d h -> l (d h)").to_broadcast([P, 8]))
                param(rows[:, 8:16], lay("gdn_dt_bias").rearrange("l d h -> l (d h)").to_broadcast([P, 8]))
                param(rows[:, 16:20], lay("b_group").to_broadcast([P, 4]))
                param(rows[:, 20:52], lay("b_router").to_broadcast([P, NE]))
                param(pool_w[:], lay("pool_w").rearrange("l g c e -> c (l g) e"))
                param(router_w[:, :, 0:NG], lay("w_group").rearrange("l (c p) n -> p (l c) n", p=P))
                param(router_w[:, :, NG:NG + NE], lay("w_router").rearrange("l (c p) n -> p (l c) n", p=P))
                assert n_par[0] == N_PARAMS, n_par

                load(U_DV, part(U_DV, 256), w_in(2560, 2816))
                sp.wait_ge(*last_reader[U_CONST - NSLOT])
                sp.dma_start(ring[:, slot(U_CONST), :], a["big_consts"]).then_inc(unit_in[slot(U_CONST)], 16)
                for n in range(2):
                    load(U_OUT + n, part(U_OUT + n, 512), half("w_out", n))
                for n in range(2):
                    load(U_MK + n, part(U_MK + n, 512), half("mem_w_k", n))
                for n in range(2):
                    if n == 1:
                        sp.wait_ge(*done["retS3"])
                        sp.wait_ge(*filled["diffT"])
                        sp.dma_start(part(U_MV + n, 512), half("mem_w_v", n)).then_inc(unit_in[slot(U_MV + n)], 16)
                    else:
                        load(U_MV + n, part(U_MV + n, 512), half("mem_w_v", n))
                sp.wait_ge(gdn_done, 1)
                sp.wait_ge(*filled["yD"])
                sp.dma_start(mem_tok, a["mem"].rearrange("b (t p) d -> p (b t) d", p=P)).then_inc(mem_in, 16)
                for n in range(2):
                    load(U_MQ + n, part(U_MQ + n, 512), half("mem_w_q", n))
                for n in range(2):
                    load(U_MO + n, part(U_MO + n, 512), half("mem_w_o", n))

                def expert_unit(n, first):
                    name, k = (("w_gate", n), ("w_up", n - 4), ("w_down", n - 8))[n // 4]
                    rows_of = a[name].rearrange("l e (p c) f -> (l e) p (c f)", p=P)[bass.ds(first, QUAD)]
                    sp.dma_start(ring[:, n % NSLOT, :].rearrange("p (e k) -> p e k", e=QUAD),
                                 rows_of[:, :, 1024 * k:1024 * (k + 1)].rearrange("e p k -> p e k")).then_inc(unit_in[n % NSLOT], 16)

                RELEASE = (1, 2, 3, 4, 4, 5, 6, 7, 7, 8, 9, 10)

                def units(q, lo, released):
                    first = sp.snap(l * NE + QUAD * q)
                    for n in range(lo, lo + NSLOT):
                        sp.wait_ge(units_free, released + RELEASE[(n + NSLOT) % 12])
                        if n % 4 == 0:
                            sp.sem_inc(pass_seen, 1)
                        expert_unit(n, first)

                for n in range(NSLOT):
                    sp.wait_ge(*last_reader[PRE_UNITS - NSLOT + n])
                    expert_unit(n, l * NE)
                with sp.Fori(0, NQ - 1) as q:
                    units(q, NSLOT, 10 * q)
                    units(q + 1, 0, 10 * q)
                units(NQ - 1, NSLOT, 10 * (NQ - 1))
                sp.wait_ge(np_ready, 1)
                rounds = sp.value_load(npi[0:1, 0:1], min_val=1, max_val=T // SLOTS)
                with sp.If(rounds > 1):
                    with sp.Fori(0, rounds - 1) as k:
                        with sp.Fori(0, NQ) as q:
                            units(q, 0, 10 * (NQ * k + q) + 10 * (NQ - 1))
                            units(q, NSLOT, 10 * (NQ * k + q) + 10 * NQ)
                sp.wait_ge(layer_done, 4)
                for q in layer_sems:
                    sp.sem_clear(q)
                sp.sem_inc(layer_go, 1)
            sp.dma_start(m1[:, 0:D], a["final_norm_g"].rearrange("(o d) -> o d", o=1).to_broadcast([P, D])).then_inc(final_in, 16)
            sp.wait_ge(last_out, 2)
            sp.dma_start(out.rearrange("b (t p) d -> p (b t) d", p=P), xn[:]).then_inc(stored, 16)
            sp.wait_ge(stored, 16)


N_PARAMS = 20
_INS = ("x", "mem", "mix_norm_g", "w_in", "na_rpb", "ret_norm_g", "pool_w", "pool_scale", "gdn_conv_w", "gdn_a_log", "gdn_dt_bias",
        "gdn_norm_g", "w_out", "mem_q_norm_g", "mem_kv_norm_g", "mem_w_q", "mem_w_k", "mem_w_v", "mem_w_o", "ffn_norm_g", "w_group",
        "b_group", "w_router", "b_router", "w_gate", "w_up", "w_down", "final_norm_g")


def kernel(**inputs):
    import concourse.bacc as _bacc
    from concourse.bass_utils import run_bass_kernel_spmd as _run

    nc = _bacc.Bacc("TRN2", target_bir_lowering=False, num_devices=1)
    small_tables, big_tables = constant_tables()
    arrays = {name: np.ascontiguousarray(inputs[name]) for name in _INS}
    arrays["consts"], arrays["big_consts"] = small_tables, big_tables
    a = {name: nc.dram_tensor(f"in_{name}", v.shape, F32, kind="ExternalInput").ap() for name, v in arrays.items()}
    out = nc.dram_tensor("out_0", (1, T, D), F32, kind="ExternalOutput").ap()
    encoder(nc, a, out, {})
    r = _run(nc, [{f"in_{name}": v for name, v in arrays.items()}], core_ids=[0])
    return r.results[0]["out_0"]
```

```python
from contextlib import ExitStack

import numpy as np
import concourse.bass as bass
from concourse import mybir

F32 = mybir.dt.float32
I32 = mybir.dt.int32
U32 = mybir.dt.uint32
ALU = mybir.AluOpType
ACT = mybir.ActivationFunctionType
AX = mybir.AxisListType.X

P = 128
D = 1024
T = 256
TT = T // P
DC = D // P
DEPTH = 2
GRID_W = 64
ROWS = T // GRID_W
HD = 64
NH = 4
W = NH * HD
RPB_H, RPB_W = 15, 31
NE = 32
EPG = 8
NG = 4
DE = 512
CHUNK = 64
LEVELS = 6
QUAD = 4
SLOTS = 32
NQ = NE // QUAD
NSLOT = 4
P_IN = 12 * W + 4 * NH
EPS = 1e-6
POOL_WINDOWS = (2, 4, 8, 16)
NEG = -1e30

PV_A, PQ_B, PK_B, PV_B, PG_B, PU_C, PG_D, PAB = 0, 256, 512, 768, 1024, 1280, 1536, 1792
PW = PAB + 4 * NH

CONSTS = {}
_at = 0
for _name, _width in (("ident", P), ("anti", P), ("band", T), ("tri", 2 * P), ("level", LEVELS * 2 * P),
                      ("blocks", P), ("ones", P), ("before", P), ("rot_a", TT * HD), ("rot_b", TT * HD),
                      ("slot", SLOTS), ("eight", EPG), ("halves", 2)):
    CONSTS[_name] = (_at, _width)
    _at += _width
NCONST = _at


def constant_tables():
    c = np.zeros((P, NCONST), np.float32)

    def put(name, value):
        at, width = CONSTS[name]
        c[:, at:at + width] = np.asarray(value, np.float32).reshape(P, width)

    p = np.arange(P)
    j, i = p[:, None], p[None, :]
    put("ident", j == i)
    put("anti", (j // 64 == i // 64) & (j % 64 == 63 - i % 64))
    qc, kc = (p % GRID_W)[:, None], (np.arange(T) % GRID_W)[None, :]
    lo = np.clip(qc - 8, 0, GRID_W - 16)
    put("band", np.where((kc >= lo) & (kc < lo + 16), 0.0, NEG))
    same = j // CHUNK == i // CHUNK
    put("tri", np.stack([same & (j <= i), same & (j >= i)], 1))
    levels = []
    for n in range(LEVELS):
        b = 1 << n
        pair = j // (2 * b) == i // (2 * b)
        levels += [pair & (j // b % 2 == 0) & (i // b % 2 == 1), pair & (j // b % 2 == 1) & (i // b % 2 == 0)]
    put("level", np.stack(levels, 1))
    put("blocks", same)
    put("ones", np.ones((P, P)))
    put("before", j < i)
    inv = np.float32(10000.0) ** (-np.arange(HD // 2, dtype=np.float32) / np.float32(HD // 2))
    ang = (np.arange(T, dtype=np.float32)[:, None] * inv[None, :]).astype(np.float32)
    cos, sin = np.cos(ang), np.sin(ang)
    tiled = lambda a: a.reshape(TT, P, HD).transpose(1, 0, 2)
    put("rot_a", tiled(np.concatenate([cos, cos], 1)))
    put("rot_b", tiled(np.concatenate([-sin, sin], 1)))
    put("slot", np.broadcast_to(np.arange(SLOTS), (P, SLOTS)))
    put("eight", np.broadcast_to(np.arange(EPG), (P, EPG)))
    put("halves", np.stack([p < 64, p >= 64], 1))

    t = np.arange(T)
    diff = (t[None, :] - t[:, None]).astype(np.float64)
    lg = np.log1p(-np.exp2(-5.0 - np.arange(NH)))
    decay = np.stack([np.where(diff >= 0, np.exp(lg[h] * np.maximum(diff, 0)),
                               np.exp(lg[::-1][h] * np.maximum(-diff, 0))) for h in range(NH)]) * HD ** -0.5
    pools = []
    for w in POOL_WINDOWS:
        a, b = np.clip(t - w // 2, 0, T), np.clip(t + w // 2, 0, T)
        inside = (t[:, None] >= a[None, :]) & (t[:, None] < b[None, :])
        pools.append(inside / (b - a)[None, :] - (t[:, None] == t[None, :]))
    fold = lambda m: np.stack(m).reshape(4, TT, P, T).transpose(2, 0, 1, 3).reshape(P, 4 * TT * T)
    big = np.concatenate([fold(decay), fold(pools)], 1).astype(np.float32)
    return c, big


def encoder(nc, a, out, taps):
    ctx = ExitStack()
    with ctx:
        sb = lambda name, shape, dt=F32: ctx.enter_context(nc.sbuf_tensor(name, shape, dt))

        def wide(ap, n):
            return ap.rearrange("p (k o) -> p k o", o=1).to_broadcast([ap.shape[0], ap.shape[1], n])

        def again(ap, n):
            return ap.rearrange("p (o k) -> p o k", o=1).to_broadcast([ap.shape[0], n, ap.shape[1]])

        ring = sb("ring", [P, NSLOT, 4096])
        x = sb("x", [P, TT, D])
        xn = sb("xn", [P, TT, D])
        xnT = sb("xnT", [P, DC, T])
        rpb = sb("rpb", [P, 2048])
        m1, m2, m3, m4 = (sb(f"m{k}", [P, 2048]) for k in (1, 2, 3, 4))
        yT = sb("yT", [P, DC, T])
        proj = sb("proj", [P, TT * PW])
        conv_in = sb("conv_in", [P, 6, T + 3])
        const = sb("const", [P, NCONST])
        gains = sb("gains", [P, 5, DC])
        cols = sb("cols", [P, 8])
        conv_w = sb("conv_w", [P, 4, 6])
        rows = sb("rows", [P, 16 + 4 + NE])
        pool_w = sb("pool_w", [HD, 4, HD])
        router_w = sb("router_w", [P, DC, NG + NE])
        w_ab = sb("w_ab", [P, DC, 4 * NH])
        tables = sb("tables", [P, 4096])
        memT = sb("memT", [P, DC, T])
        memK = sb("memK", [P, DC, T])
        ss = sb("ss", [P, 4, 4])
        rstd = sb("rstd", [P, 4, 2])
        mhalf = sb("mhalf", [P, 16])
        small = sb("small", [P, 512])
        npi = sb("npi", [1, 2], I32)
        idx = sb("idx", [P, 2, TT, 8], U32)
        val = sb("val", [P, 2, TT, 8])
        rank_q = sb("rank_q", [P, TT, QUAD])
        gate_q = sb("gate_q", [P, TT, QUAD])
        ranks = sb("ranks", [P, TT, NE])
        gates = sb("gates", [P, TT, NE])

        def c(name):
            at, width = CONSTS[name]
            return const[:, at:at + width]

        ident, anti, ones, blocks, before = c("ident"), c("anti"), c("ones"), c("blocks"), c("before")
        tri = c("tri").rearrange("p (d k) -> p d k", d=2)
        level = c("level").rearrange("p (n d k) -> p n d k", n=LEVELS, d=2)
        rot_a = c("rot_a").rearrange("p (t k) -> p t k", t=TT)
        rot_b = c("rot_b").rearrange("p (t k) -> p t k", t=TT)
        halves = c("halves")
        projv = proj[:, :].rearrange("p (t k) -> p t k", t=TT)

        aqkT = m3[:, 1024:2048].rearrange("p (c t) -> p c t", c=4)
        prob = m1[:, :].rearrange("p (h t k) -> p h t k", h=NH, t=TT)
        probT = m2[:, :].rearrange("p (h c q) -> p h c q", h=NH, c=2)
        bias = rpb[:, :].rearrange("p (t h k) -> p t h k", t=TT, h=NH)
        rot1 = m4[:, 0:1024].rearrange("p (t k) -> p t k", t=TT)
        rot2 = m4[:, 1024:2048].rearrange("p (t k) -> p t k", t=TT)
        bqkT = m3[:, 0:1024].rearrange("p (c t) -> p c t", c=4)
        retS = xn[:, :, :].rearrange("p t (u k) -> p (t u) k", k=512)
        ret_o = m4[:, 0:512]
        ret_s = m4[:, 512:1024]
        diffT = m3[0:HD, 1024:2048].rearrange("p (g t) -> p g t", g=4)
        units = lambda m: m.rearrange("p (u k) -> p u k", k=P)
        decay, lT, inv, invT = (units(m[:, :]) for m in (m1, m2, m3, m4))
        low = units(xn[:, :, :].rearrange("p t k -> p (t k)"))
        prod = units(rpb[:, :])
        qkv = conv_in[:, :, :].rearrange("p c t -> p (c t)")[:, 0:TT * 768].rearrange("p (t k) -> p t k", t=TT)
        qkT = xnT
        wT = m2[:, 0:1024].rearrange("p (d t f k) -> p d t f k", d=2, t=TT, f=2)
        qdT = m2[:, 1024:2048].rearrange("p (d t f k) -> p d t f k", d=2, t=TT, f=2)
        uval = m3[:, 0:1024].rearrange("p (u k) -> p u k", k=HD)
        decays = tables[:, 0:2048].rearrange("p (h k) -> p h k", h=NH)
        pools = tables[:, 2048:4096].rearrange("p (g s t) -> p g s t", g=4, s=TT)
        vbeta, kdec, kstate, qdec = (tables[:, 1024 * k:1024 * (k + 1)].rearrange("p (u k) -> p u k", k=HD) for k in range(4))
        xnf = xn[:, :, :].rearrange("p t k -> p (t k)")
        gdn_o = xnf[:, 1024:2048]
        state = small[:, 0:256].rearrange("p (d f e) -> p d f e", d=2, f=2)
        vnew = small[:, 256:512].rearrange("p (a f e) -> p a f e", a=2, f=2)
        dsm = sb("dsm", [P, 16 * 16])
        dcol = lambda k, n=16: dsm[:, 16 * k:16 * k + n]
        unit_col = lambda k: dcol(k).rearrange("p (t d h) -> p t d h", t=TT, d=2)
        G, BETA, GC, GL, EGC, ESL, T0, T1, T2, T3 = range(10)
        gmask = dsm[:, 160:192].rearrange("p (v u) -> p v u", v=2)
        egl = dsm[:, 192:208]
        stat = dsm[:, 208:224]
        stat2 = dsm[:, 224:240]
        gdn_q = xnf[:, 0:256].rearrange("p (a f e) -> p a f e", a=2, f=2)
        mem_tok, mem_n = (m[:, :].rearrange("p (t k) -> p t k", t=TT) for m in (m1, m2))
        memV = projv[:, :, 0:D]
        convT = yT
        memQ = yT
        attT = m3[:, :].rearrange("p (c t) -> p c t", c=DC)
        sel = m1[:, 0:256].rearrange("p (t s) -> p t s", t=TT)
        selw = m1[:, 256:512].rearrange("p (t s) -> p t s", t=TT)
        selwT = m1[:, 512:768].rearrange("p (t k) -> p t k", t=TT)
        xg = m2[:, 0:1024].rearrange("p (c s) -> p c s", c=DC)
        xn_by_row = xn[:, :, :].rearrange("p t (k c) -> p t c k", c=DC)
        silu_g, hid = m3[:, 0:512], m3[:, 512:1024]
        hid_by_row = hid.rearrange("p (k c) -> p c k", c=4)
        hidT = m3[:, 1024:1536].rearrange("p (c s) -> p c s", c=4)
        y_e = m4[:, 0:1024]
        logit = small[:, 0:TT * 36].rearrange("p (t k) -> p t k", t=TT)

        bank = [ctx.enter_context(nc.psum_tensor(f"bank{k}", [P, 512], F32)) for k in range(8)]

        sem = lambda name: ctx.enter_context(nc.semaphore(name))
        const_in, x_in, preset, layer_go = sem("const_in"), sem("x_in"), sem("preset"), sem("layer_go")
        stored, final_in = sem("stored"), sem("final_in")
        last_sq, last_mean, last_rstd, last_out = sem("last_sq"), sem("last_mean"), sem("last_rstd"), sem("last_out")
        layer_seen, pass_seen = sem("layer_seen"), sem("pass_seen")
        layer_sems = []

        def lsem(name):
            s = sem(name)
            layer_sems.append(s)
            return s

        first_in = [sem(f"first_in{k}") for k in range(NSLOT)]
        unit_in = [lsem(f"unit_in{k}") for k in range(NSLOT)]
        params_in, rpb_in, mem_in = lsem("params_in"), lsem("rpb_in"), lsem("mem_in")
        gains_in, tables_in = lsem("gains_in"), lsem("tables_in")
        vec_full, vec_evac, act_full, act_evac = lsem("vec_full"), lsem("vec_evac"), lsem("act_full"), lsem("act_evac")
        vec_step, act_step, pool_step = lsem("vec_step"), lsem("act_step"), lsem("pool_step")
        squares, means, rstds, normed = lsem("squares"), lsem("means"), lsem("rstds"), lsem("normed")
        maxed, exped, probs_ready = lsem("maxed"), lsem("exped"), lsem("probs_ready")
        rotated, ret_silu, ret_var, ret_rstd, ret_done = lsem("rotated"), lsem("ret_silu"), lsem("ret_var"), lsem("ret_rstd"), lsem("ret_done")
        conved, conv_silu, qk_sums, qk_rstd, qk_ready = lsem("conved"), lsem("conv_silu"), lsem("qk_sums"), lsem("qk_rstd"), lsem("qk_ready")
        gate_in, gate_exp, gate_in2, gate_ln, g_ready = lsem("gate_in"), lsem("gate_exp"), lsem("gate_in2"), lsem("gate_ln"), lsem("g_ready")
        gdiff, gexp, dec_exp, dec_masked, low_ready = lsem("gdiff"), lsem("gexp"), lsem("dec_exp"), lsem("dec_masked"), lsem("low_ready")
        lT_ready, inv0_ready, scaled, vnew_ready = lsem("lT_ready"), lsem("inv0_ready"), lsem("scaled"), lsem("vnew_ready")
        state_ready, gdn_var, gdn_rstd, gdn_silu, gdn_done = lsem("state_ready"), lsem("gdn_var"), lsem("gdn_rstd"), lsem("gdn_silu"), lsem("gdn_done")
        r_max, r_exp, ind_ready, np_ready = lsem("r_max"), lsem("r_exp"), lsem("ind_ready"), lsem("np_ready")
        sel_built, sel_turned, selwT_ready, x_added = lsem("sel_built"), lsem("sel_turned"), lsem("selwT_ready"), lsem("x_added")
        gathered, xg_ready = [lsem(f"gathered{k}") for k in range(2)], [lsem(f"xg_ready{k}") for k in range(2)]
        gate_full, up_full, silu_ready, hid_ready = lsem("gate_full"), lsem("up_full"), lsem("silu_ready"), lsem("hid_ready")
        hid_turned, hidT_ready, y_full = lsem("hid_turned"), lsem("hidT_ready"), [lsem(f"y_full{k}") for k in range(2)]
        y_ready, scattered = [lsem(f"y_ready{k}") for k in range(2)], [lsem(f"scattered{k}") for k in range(4)]
        units_free = lsem("units_free")
        layer_done, quad_ready = lsem("layer_done"), lsem("quad_ready")
        ranks_moved = lsem("ranks_moved")

        PRE_UNITS = 16
        slot = lambda n: n % NSLOT
        U_DQK, U_DVG, U_TOK, U_AQK, U_MK, U_MV, U_OUT, U_MQ, U_MO = 0, 1, 2, 5, 6, 8, 10, 12, 14
        last_reader = {}
        done = {}
        filled = {}
        gdn_read = {}

        ring3 = lambda n, k: ring[:, slot(n), 0:DC * k].rearrange("p (c k) -> p c k", k=k)

        block = ctx.enter_context(nc.Block())

        @block.tensor
        def _(pe):
            pe.wait_ge(const_in, 16)
            pe.wait_ge(preset, 2)
            with pe.Fori(0, DEPTH) as l:
                count = {"v": 0, "a": 0}
                evac = {"v": vec_evac, "a": act_evac}
                full = {"v": vec_full, "a": act_full}

                def fill(r):
                    n = count[r]
                    if n >= 4:
                        pe.wait_ge(evac[r], n - 3)
                    return bank[(0 if r == "v" else 4) + n % 4]

                def end(r, mm, name=None, units=()):
                    mm.then_inc(full[r], 1)
                    count[r] += 1
                    if name:
                        done[name] = (evac[r], count[r])
                        filled[name] = (full[r], count[r])
                    for u in units:
                        last_reader[u] = (full[r], count[r])

                def need(name):
                    pe.wait_ge(*done[name])

                def unit(n):
                    if n < NSLOT:
                        pe.wait_ge(first_in[n], 16 * l + 16)
                    else:
                        pe.wait_ge(unit_in[slot(n)], 16 * (n // NSLOT))

                def turn_x(name, src, k):
                    pe.wait_ge(normed, 2 * (k + 1))
                    for t in range(TT):
                        for g in range(2):
                            b = fill("v")
                            for q in range(4):
                                mm = pe.transpose(b[:, q * P:(q + 1) * P], src[:, t, (4 * g + q) * P:(4 * g + q + 1) * P], ident)
                            end("v", mm, name)

                def feature_major(n, f, rhsT, r, name):
                    w = ring3(n, 512)
                    b = fill(r)
                    for q in range(2):
                        for ch in range(DC):
                            mm = pe.matmul(b[:, q * T:(q + 1) * T], w[:, ch, (f + q) * P:(f + q + 1) * P], rhsT[:, ch, :],
                                           start=ch == 0, stop=ch == DC - 1)
                    end(r, mm, name, (n,))

                def token_major(n, t, lhsT, r, name):
                    w = ring3(n, 512)
                    b = fill(r)
                    for ch in range(DC):
                        mm = pe.matmul(b[:, :], lhsT[:, ch, t * P:(t + 1) * P], w[:, ch, :], start=ch == 0, stop=ch == DC - 1)
                    end(r, mm, name, (n,))

                def memory_keys(n, f):
                    need("memT")
                    unit(U_MK + n)
                    feature_major(U_MK + n, f, memT, "a", "memK")

                def memory_values(n, t):
                    unit(U_MV + n)
                    token_major(U_MV + n, t, memT, "a", "memV")

                def turn_probs(k):
                    for h in range(NH):
                        pe.wait_ge(probs_ready, NH * k + h + 1)
                        b = fill("a")
                        for kc in range(2):
                            for t in range(TT):
                                mm = pe.transpose(b[:, (2 * kc + t) * P:(2 * kc + t + 1) * P], prob[:, h, t, kc * P:(kc + 1) * P], ident)
                        end("a", mm, f"probT{k}{h}")

                turn_x("xnT", xn, 0)
                need("xnT")
                unit(U_DQK)
                feature_major(U_DQK, 0, xnT, "v", "dqk0")
                feature_major(U_DQK, 2, xnT, "v", "dqk1")
                unit(U_DVG)
                feature_major(U_DVG, 0, xnT, "v", "dv")
                pe.wait_ge(params_in, 16 * N_PARAMS)
                wg = ring3(U_DVG, 512)
                for t in range(TT):
                    b = fill("a")
                    for ch in range(DC):
                        pe.matmul(b[:, 0:W], xnT[:, ch, t * P:(t + 1) * P], wg[:, ch, W:2 * W], start=ch == 0, stop=ch == DC - 1)
                    for ch in range(DC):
                        mm = pe.matmul(b[:, W:W + 16], xnT[:, ch, t * P:(t + 1) * P], w_ab[:, ch, :], start=ch == 0, stop=ch == DC - 1)
                    end("a", mm, f"gate{t}", (U_DVG,))
                turn_x("memT", mem_n, 1)
                for n in range(3):
                    unit(U_TOK + n)
                    for t in range(TT):
                        token_major(U_TOK + n, t, xnT, "av"[t], f"tok{n}{t}")
                unit(U_AQK)
                feature_major(U_AQK, 0, xnT, "a", "aqk0")
                feature_major(U_AQK, 2, xnT, "a", "aqk1")
                filled["projected"] = filled["aqk1"]

                pe.wait_ge(conv_silu, 6)
                for t in range(TT):
                    b = fill("v")
                    for q in range(4):
                        mm = pe.transpose(b[:, q * P:(q + 1) * P], convT[:, q, t * P:(t + 1) * P], ident)
                    end("v", mm)
                    b = fill("v")
                    for q in range(2):
                        mm = pe.transpose(b[:, q * P:(q + 1) * P], convT[:, 4 + q, t * P:(t + 1) * P], ident)
                    end("v", mm)

                need("aqk1")
                pe.wait_ge(rpb_in, 16 * 16)
                for h in range(NH):
                    b = fill("v")
                    r0 = (h % 2) * HD
                    for t in range(TT):
                        o = b[:, t * T:(t + 1) * T]
                        pe.matmul(o, aqkT[r0:r0 + HD, h // 2, t * P:(t + 1) * P], aqkT[r0:r0 + HD, 2 + h // 2, :], start=True, stop=False)
                        mm = pe.matmul(o, anti, bias[:, t, h, :], start=False, stop=True)
                    end("v", mm, f"ascore{h}")
                memory_keys(0, 0)
                pe.wait_ge(g_ready, 1)
                b = fill("v")
                g4 = unit_col(G)
                for d in range(2):
                    for t in range(TT):
                        pe.matmul(b[:, 8 * t + 4 * d:8 * t + 4 * d + 4], tri[:, d, :], g4[:, t, d, :], start=True, stop=True)
                pe.matmul(b[:, 16:32], blocks, dcol(G), start=True, stop=True)
                gm = gmask.rearrange("p v (u h) -> p (v u) h", h=NH)
                for par in range(2):
                    mm = pe.matmul(b[par * HD:(par + 1) * HD, 32:48], ones[:, 0:HD], gm[:, :, par::2], start=True, stop=True)
                end("v", mm, "gc")
                pe.wait_ge(qk_ready, 2)
                for t in range(TT):
                    b = fill("a")
                    for q in range(4):
                        mm = pe.transpose(b[:, q * P:(q + 1) * P], qkv[:, t, q * P:(q + 1) * P], ident)
                    end("a", mm, "qkT")
                turn_probs(0)
                pe.wait_ge(rotated, 2)
                for t in range(TT):
                    b = fill("a")
                    for q in range(4):
                        mm = pe.transpose(b[:, q * P:(q + 1) * P], rot1[:, t, q * P:(q + 1) * P], ident)
                    end("a", mm, "bqkT")
                for d in range(2):
                    for par in range(2):
                        b = fill("v")
                        for t in range(TT):
                            for f in range(2):
                                k = 2 * t + f
                                mm = pe.matmul(b[:, k * P:(k + 1) * P], g4[:, t, d, 2 * f + par:2 * f + par + 1].to_broadcast([P, P]), tri[:, d, :],
                                               start=True, stop=True)
                        end("v", mm)
                need("probT03")
                need("tok01")
                need("tok00")
                b = fill("a")
                for h in range(NH):
                    for kc in range(2):
                        mm = pe.matmul(b[(h % 2) * HD:(h % 2 + 1) * HD, (h // 2) * T:(h // 2 + 1) * T],
                                       projv[:, kc, PV_A + h * HD:PV_A + (h + 1) * HD], probT[:, h, kc, :], start=kc == 0, stop=kc == 1)
                end("a", mm, "yA")

                need("bqkT")
                for h in range(NH):
                    b = fill("v")
                    r0 = (h % 2) * HD
                    for jt in range(TT):
                        mm = pe.matmul(b[:, jt * T:(jt + 1) * T], bqkT[r0:r0 + HD, 2 + h // 2, jt * P:(jt + 1) * P],
                                       bqkT[r0:r0 + HD, h // 2, :], start=True, stop=True)
                    end("v", mm, f"retS{h}")
                memory_keys(0, 2)
                need("retS3")
                for n in range(1, 3):
                    for t in range(TT):
                        need(f"tok{n}{t}")
                b = fill("v")
                for t in range(TT):
                    for h in range(NH):
                        for jt in range(TT):
                            mm = pe.matmul(b[:, t * W + h * HD:t * W + (h + 1) * HD], retS[:, h, jt * T + t * P:jt * T + (t + 1) * P],
                                           projv[:, jt, PV_B + h * HD:PV_B + (h + 1) * HD], start=jt == 0, stop=jt == TT - 1)
                end("v", mm, "ret_o")

                pe.wait_ge(tables_in, 16)
                for f in range(2):
                    b = fill("a")
                    for q in range(2):
                        g = 2 * f + q
                        for st in range(TT):
                            mm = pe.matmul(b[0:HD, q * T:(q + 1) * T], projv[:, st, PU_C + g * HD:PU_C + (g + 1) * HD],
                                           pools[:, g, st, :], start=st == 0, stop=st == TT - 1)
                    end("a", mm, "diffT")
                need("qkT")
                for which in (2, 0):
                    for par in range(2):
                        b = fill("v")
                        r0 = par * HD
                        for t in range(TT):
                            for f in range(2):
                                k = 2 * t + f
                                mm = pe.matmul(b[:, k * P:(k + 1) * P], qkT[r0:r0 + HD, 2 + f, t * P:(t + 1) * P],
                                               qkT[r0:r0 + HD, which + f, t * P:(t + 1) * P], start=True, stop=True)
                        end("v", mm)
                b4 = unit_col(BETA)
                for d in range(2):
                    for par in range(2):
                        b = fill("v")
                        for t in range(TT):
                            for f in range(2):
                                k = 2 * t + f
                                mm = pe.matmul(b[:, k * P:(k + 1) * P], b4[:, t, d, 2 * f + par:2 * f + par + 1].to_broadcast([P, P]), ident,
                                               start=True, stop=True)
                        end("v", mm)
                need("diffT")
                b = fill("v")
                for g in range(4):
                    mm = pe.matmul(b[(g % 2) * HD:(g % 2 + 1) * HD, (g // 2) * T:(g // 2 + 1) * T], pool_w[:, g, :], diffT[:, g, :],
                                   start=True, stop=True)
                end("v", mm, "yC")
                pe.wait_ge(ret_done, 1)
                b = fill("v")
                for f in range(2):
                    for t in range(TT):
                        mm = pe.transpose(b[:, f * T + t * P:f * T + (t + 1) * P], ret_o[:, t * W + f * P:t * W + (f + 1) * P], ident)
                end("v", mm, "yB")
                memory_keys(1, 0)

                for q in range(4):
                    pe.wait_ge(inv0_ready, q + 1)
                    b = fill("a")
                    for k in range(4):
                        mm = pe.transpose(b[:, k * P:(k + 1) * P], invT[:, 4 * q + k, :], ident)
                    end("a", mm, f"inv{q}")
                    done[f"inv0{q}"] = done[f"inv{q}"]
                for n in range(1, LEVELS):
                    pe.wait_ge(low_ready, 2 * n)
                    for q in range(4):
                        need(f"inv{q}")
                        b = fill("a")
                        for k in range(4):
                            u = 4 * q + k
                            mm = pe.matmul(b[:, k * P:(k + 1) * P], low[:, u, :], inv[:, u, :], start=True, stop=True)
                        end("a", mm, f"prod{q}")
                        if q == 3:
                            filled[f"low_used{n}"] = filled["prod3"]
                    for q in range(4):
                        need(f"prod{q}")
                        if n > 1:
                            need(f"invT{q}")
                        if n < LEVELS - 1:
                            b = fill("v")
                            for k in range(4):
                                u = 4 * q + k
                                mm = pe.matmul(b[:, k * P:(k + 1) * P], invT[:, u, :], prod[:, u, :], start=True, stop=True)
                            end("v", mm, f"inv{q}")
                        b = fill("v")
                        for k in range(4):
                            u = 4 * q + k
                            mm = pe.matmul(b[:, k * P:(k + 1) * P], prod[:, u, :], invT[:, u, :], start=True, stop=True)
                        end("v", mm, f"invT{q}")
                pe.wait_ge(scaled, 4)
                for d in range(2):
                    b = fill("a")
                    for t in range(TT):
                        for f in range(2):
                            u0 = (2 * d + t) * NH + 2 * f
                            mm = pe.transpose(b[:, (2 * t + f) * P:(2 * t + f + 1) * P],
                                              qdec[:, u0:u0 + 2, :].rearrange("p u k -> p (u k)"), ident)
                    end("a", mm, "qdT")
                need("invT3")
                for d in range(2):
                    b = fill("a")
                    for k in range(8):
                        u = 8 * d + k
                        mm = pe.matmul(b[:, k * HD:(k + 1) * HD], invT[:, u, :], vbeta[:, u, :], start=True, stop=True)
                    end("a", mm, "uval")
                for d in range(2):
                    b = fill("a")
                    for par in range(2):
                        for t in range(TT):
                            for f in range(2):
                                u = ((2 * d + par) * TT + t) * 2 + f
                                mm = pe.matmul(b[par * HD:(par + 1) * HD, (2 * t + f) * P:(2 * t + f + 1) * P], kdec[:, u, :], invT[:, u, :],
                                               start=True, stop=True)
                    end("a", mm, "wT")
                need("wT")
                for s in range(4):
                    where = [(d, (s if d == 0 else 3 - s) // 2, (s if d == 0 else 3 - s) % 2) for d in range(2)]
                    if s:
                        pe.wait_ge(state_ready, 4 * s)
                        for par in range(2):
                            b = fill("v")
                            for d, t, hf in where:
                                for f in range(2):
                                    mm = pe.matmul(b[hf * HD:(hf + 1) * HD, f * HD:(f + 1) * HD],
                                                   wT[par * HD:(par + 1) * HD, d, t, f, hf * HD:(hf + 1) * HD],
                                                   state[par * HD:(par + 1) * HD, d, f, :], start=True, stop=True)
                            end("v", mm)
                        for par in range(2):
                            b = fill("a")
                            for d, t, hf in where:
                                for f in range(2):
                                    mm = pe.matmul(b[hf * HD:(hf + 1) * HD, f * HD:(f + 1) * HD],
                                                   qdT[par * HD:(par + 1) * HD, d, t, f, hf * HD:(hf + 1) * HD],
                                                   state[par * HD:(par + 1) * HD, d, f, :], start=True, stop=True)
                            end("a", mm, f"gdn_q{s}")
                    pe.wait_ge(vnew_ready, 4 * (s + 1))
                    if s < 3:
                        for d, t, hf in where:
                            b = fill("v")
                            for par in range(2):
                                for f in range(2):
                                    u = ((2 * d + par) * TT + t) * 2 + f
                                    mm = pe.matmul(b[par * HD:(par + 1) * HD, f * HD:(f + 1) * HD],
                                                   kstate[hf * HD:(hf + 1) * HD, u, :], vnew[hf * HD:(hf + 1) * HD, par, f, :],
                                                   start=True, stop=True)
                            end("v", mm)
                    b = fill("v")
                    for d, t, hf in where:
                        for par in range(2):
                            for f in range(2):
                                u = ((2 * d + par) * TT + t) * 2 + f
                                mm = pe.matmul(b[hf * HD:(hf + 1) * HD, (2 * par + f) * HD:(2 * par + f + 1) * HD],
                                               decay[hf * HD:(hf + 1) * HD, u, hf * HD:(hf + 1) * HD],
                                               vnew[hf * HD:(hf + 1) * HD, par, f, :], start=True, stop=True)
                    end("v", mm)
                    gdn_read[s] = count["v"]
                    if s == 1:
                        memory_keys(1, 2)
                    if s == 2:
                        memory_values(0, 0)
                memory_values(0, 1)
                memory_values(1, 0)
                pe.wait_ge(gdn_done, 1)
                b = fill("v")
                for f in range(2):
                    for t in range(TT):
                        mm = pe.transpose(b[:, f * T + t * P:f * T + (t + 1) * P], gdn_o[:, t * W + f * P:t * W + (f + 1) * P], ident)
                end("v", mm, "yD")
                memory_values(1, 1)

                for name in ("yA", "yB", "yC", "yD"):
                    need(name)
                for n in range(2):
                    unit(U_OUT + n)
                    for t in range(TT):
                        token_major(U_OUT + n, t, yT, "v", f"x_mix{n}")

                turn_x("xnT", xn, 2)
                need("xnT")
                for n in range(2):
                    unit(U_MQ + n)
                    for f in (0, 2):
                        feature_major(U_MQ + n, f, xnT, "a", "memQ")
                need("memQ")
                for h in range(NH):
                    b = fill("v")
                    for t in range(TT):
                        for ch in range(2):
                            mm = pe.matmul(b[:, t * T:(t + 1) * T], memQ[:, 2 * h + ch, t * P:(t + 1) * P], memK[:, 2 * h + ch, :],
                                           start=ch == 0, stop=ch == 1)
                    end("v", mm)
                turn_probs(1)
                for h in range(NH):
                    need(f"probT1{h}")
                    b = fill("a")
                    for ch in range(2):
                        for kc in range(2):
                            mm = pe.matmul(b[:, ch * T:(ch + 1) * T], memV[:, kc, h * T + ch * P:h * T + (ch + 1) * P], probT[:, h, kc, :],
                                           start=kc == 0, stop=kc == 1)
                    end("a", mm, "attT")
                need("attT")
                for n in range(2):
                    unit(U_MO + n)
                    for t in range(TT):
                        token_major(U_MO + n, t, attT, "v", f"x_mem{n}")

                turn_x("xnT", xn, 3)
                need("xnT")
                b = fill("v")
                for t in range(TT):
                    for ch in range(DC):
                        mm = pe.matmul(b[:, 36 * t:36 * t + 36], xnT[:, ch, t * P:(t + 1) * P], router_w[:, ch, :], start=ch == 0, stop=ch == DC - 1)
                end("v", mm)
                pe.wait_ge(ind_ready, 1)
                b = fill("v")
                pe.matmul(b[:, 0:NE], before, ranks[:, 0, :], start=True, stop=True)
                pe.matmul(b[:, NE:2 * NE], ones, ranks[:, 0, :], start=True, stop=False)
                pe.matmul(b[:, NE:2 * NE], before, ranks[:, 1, :], start=False, stop=True)
                pe.matmul(b[:, 2 * NE:3 * NE], ones, ranks[:, 0, :], start=True, stop=False)
                mm = pe.matmul(b[:, 2 * NE:3 * NE], ones, ranks[:, 1, :], start=False, stop=True)
                end("v", mm, "ranks")
                pe.wait_ge(np_ready, 2)
                rounds = pe.value_load(npi[0:1, 0:1], min_val=1, max_val=T // SLOTS)

                def expert_pass(it, use):
                    def unit(n):
                        pe.wait_ge(unit_in[n % NSLOT], 16 * (PRE_UNITS // NSLOT - 1 + n // NSLOT + 1) + 16 * (12 // NSLOT) * use)
                        return ring[:, n % NSLOT, :].rearrange("p (e k) -> p e k", e=QUAD)

                    pe.wait_ge(sel_built, 2 * it)
                    for g in range(2):
                        for q in range(4):
                            for t in range(TT):
                                mm = pe.matmul(bank[g][:, q * P:(q + 1) * P], xn_by_row[:, t, 4 * g + q, :], sel[:, t, :],
                                               start=t == 0, stop=t == TT - 1)
                        mm.then_inc(gathered[g], 1)
                    for t in range(TT):
                        mm = pe.transpose(bank[2][:, t * P:(t + 1) * P], selw[:, t, :], ident)
                    mm.then_inc(sel_turned, 1)
                    pe.wait_ge(xg_ready[0], it)
                    pe.wait_ge(xg_ready[1], it)
                    for part in range(2):
                        for n in range(4):
                            w = unit(4 * part + n)
                            for q in range(2):
                                ch = 2 * n + q
                                for e in range(QUAD):
                                    mm = pe.matmul(bank[3 + part][e * SLOTS:(e + 1) * SLOTS, :], xg[:, ch, e * SLOTS:(e + 1) * SLOTS],
                                                   w[:, e, q * DE:(q + 1) * DE], start=ch == 0, stop=ch == DC - 1)
                            mm.then_inc((gate_full, up_full)[part] if n == 3 else units_free, 1)
                    pe.wait_ge(hid_ready, it)
                    for c4 in range(4):
                        mm = pe.transpose(bank[5][:, c4 * P:(c4 + 1) * P], hid_by_row[:, c4, :], ident)
                    mm.then_inc(hid_turned, 1)
                    pe.wait_ge(hidT_ready, it)
                    for c4 in range(4):
                        w = unit(8 + c4)
                        for n in range(2):
                            for e in range(QUAD):
                                mm = pe.matmul(bank[6 + n][e * SLOTS:(e + 1) * SLOTS, :], hidT[:, c4, e * SLOTS:(e + 1) * SLOTS],
                                               w[:, e, n * 512:(n + 1) * 512], start=c4 == 0, stop=c4 == 3)
                            if c4 == 3:
                                mm.then_inc(y_full[n], 1)
                            elif n == 1:
                                mm.then_inc(units_free, 1)
                    pe.drain().then_inc(units_free, 1)
                    pe.wait_ge(selwT_ready, it)
                    for n in range(2):
                        pe.wait_ge(y_ready[n], it)
                        for t in range(TT):
                            pe.matmul(bank[(0, 1, 2, 5)[2 * n + t]][:, :], selwT[:, t, :], y_e[:, n * 512:(n + 1) * 512],
                                      start=True, stop=True).then_inc(scattered[2 * n + t], 1)

                pe.wait_ge(vec_evac, count["v"])
                pe.wait_ge(act_evac, count["a"])
                with pe.Fori(0, rounds) as k:
                    with pe.Fori(0, NQ) as q:
                        expert_pass(NQ * k + q + 1, NQ * k + q)
                pe.drain().then_inc(layer_done, 1)
                pe.wait_ge(layer_go, l + 1)
                pe.sem_inc(layer_seen, 1)

        @block.vector
        def _(v):
            v.memset(mhalf[:], -0.5).then_inc(preset, 1)
            v.memset(small[:], 0.0).then_inc(preset, 1)
            v.wait_ge(preset, 2)
            v.wait_ge(const_in, 16)
            v.wait_ge(x_in, 16)

            with v.Fori(0, DEPTH) as l:
                n_own = [0]
                n_in = [0]

                def own(ins):
                    n_own[0] += 1
                    ins.then_inc(vec_step, 1)
                    v.wait_ge(vec_step, n_own[0])

                def take():
                    v.wait_ge(vec_full, n_in[0] + 1)
                    return bank[n_in[0] % 4]

                def taken(ins):
                    n_in[0] += 1
                    ins.then_inc(vec_evac, 1)
                    v.wait_ge(vec_evac, n_in[0])

                def norm(src, dst, k):
                    v.wait_ge(squares, 2 * (k + 1))
                    v.tensor_scalar(ss[:, k, 2:4], ss[:, k, 0:2], 1.0 / D, EPS, ALU.mult, ALU.add).then_inc(means, 1)
                    v.wait_ge(rstds, k + 1)
                    for t in range(TT):
                        v.tensor_scalar(dst[:, t, :], src[:, t, :], rstd[:, k, t:t + 1], None, ALU.mult).then_inc(normed, 1)

                def take_turned(dstT, k):
                    for t in range(TT):
                        for g in range(2):
                            b = take()
                            taken(v.tensor_tensor(dstT[:, 4 * g:4 * g + 4, t * P:(t + 1) * P], b[:, :].rearrange("p (c k) -> p c k", c=4),
                                                  wide(gains[:, k, 4 * g:4 * g + 4], P), ALU.mult))

                mx = dsm[:, 240:248].rearrange("p (h t) -> p h t", t=TT)

                def scores(mask):
                    for h in range(NH):
                        b = take()
                        bv = b[:, :].rearrange("p (t k) -> p t k", t=TT)
                        if mask:
                            taken(v.tensor_tensor(prob[:, h], bv, again(c("band"), TT), ALU.add))
                        else:
                            taken(v.tensor_copy(prob[:, h], bv))
                        own(v.tensor_reduce(mx[:, h, :], prob[:, h], AX, ALU.max))
                        v.tensor_scalar(mx[:, h, :], mx[:, h, :], -1.0, None, ALU.mult).then_inc(maxed, 1)

                def weights(k):
                    for h in range(NH):
                        v.wait_ge(exped, 2 * (NH * k + h + 1))
                        own(v.reciprocal(stat[:, 2 * h:2 * h + 2], stat2[:, 2 * h:2 * h + 2]))
                        v.tensor_tensor(prob[:, h], prob[:, h], wide(stat[:, 2 * h:2 * h + 2], T), ALU.mult).then_inc(probs_ready, 1)

                v.wait_ge(gains_in, 16 * 5)
                norm(x, xn, 0)
                take_turned(xnT, 0)
                norm(mem_tok, mem_n, 1)
                own(v.memset(conv_in[:, :, 0:2], 0.0))
                own(v.memset(conv_in[:, :, T + 2:T + 3], 0.0))
                for f in range(3):
                    b = take()
                    taken(v.tensor_copy(conv_in[:, 2 * f:2 * f + 2, 2:T + 2], b[:, :].rearrange("p (c t) -> p c t", c=2)))
                take_turned(memT, 2)
                v.wait_ge(params_in, 16 * N_PARAMS)
                for k in range(4):
                    for ch in range(6):
                        o = convT[:, ch, :]
                        if k == 0:
                            ins = v.tensor_scalar(o, conv_in[:, ch, 0:T], conv_w[:, 0, ch:ch + 1], None, ALU.mult)
                        else:
                            ins = v.scalar_tensor_tensor(out=o, in0=conv_in[:, ch, k:k + T], scalar=conv_w[:, k, ch:ch + 1], in1=o, op0=ALU.mult, op1=ALU.add)
                        if k < 3:
                            n_own[0] += 1
                            ins.then_inc(vec_step, 1)
                        else:
                            ins.then_inc(conved, 1)
                        if k < 3 and ch == 5:
                            v.wait_ge(vec_step, n_own[0])
                for t in range(TT):
                    v.wait_ge(*done[f"gate{t}"])
                ab = projv[:, :, PAB:PAB + 16]
                t16 = lambda k: dcol(k).rearrange("p (t u) -> p t u", t=TT)
                own(v.tensor_tensor(t16(T0), ab[:, :, 0:8], again(rows[:, 8:16], TT), ALU.add))
                own(v.tensor_scalar(t16(T1), t16(T0), -1.0, None, ALU.mult))
                own(v.tensor_tensor(t16(T1), t16(T1), t16(T0), ALU.min))
                own(v.tensor_scalar(t16(T0), t16(T0), 0.0, None, ALU.max))
                v.tensor_copy(t16(T2), ab[:, :, 8:16]).then_inc(gate_in, 1)
                for n in range(3):
                    b = take()
                    taken(v.tensor_copy(projv[:, 1, n * 512:(n + 1) * 512], b[:, :]))
                v.wait_ge(gate_exp, 3)
                own(v.tensor_scalar(t16(T2), t16(T2), 1.0, None, ALU.add))
                own(v.reciprocal(dcol(BETA), dcol(T2)))
                v.wait_ge(gate_ln, 1)
                own(v.tensor_tensor(t16(T0), t16(T0), t16(T1), ALU.add))
                own(v.tensor_tensor(t16(T0), t16(T0), again(dcol(T3, 8), TT), ALU.mult))
                own(v.tensor_scalar(dcol(G), dcol(T0), -1.0, None, ALU.mult))
                own(v.tensor_scalar(gmask[:, 0, :], dcol(G), halves[:, 0:1], None, ALU.mult))
                v.tensor_scalar(gmask[:, 1, :], dcol(G), halves[:, 1:2], None, ALU.mult).then_inc(g_ready, 1)
                for n in range(2):
                    v.wait_ge(*done[f"tok{n}0"])
                for t in range(TT):
                    src = projv[:, t, PQ_B:PQ_B + 512].rearrange("p (h k) -> p h k", k=HD)
                    r1 = rot1[:, t, :].rearrange("p (h k) -> p h k", k=HD)
                    r2 = rot2[:, t, :].rearrange("p (h k) -> p h k", k=HD)
                    own(v.tensor_tensor(r1, src, again(rot_a[:, t, :], 8), ALU.mult))
                    own(v.tensor_tensor(r2[:, :, 0:32], src[:, :, 32:64], again(rot_b[:, t, 0:32], 8), ALU.mult))
                    own(v.tensor_tensor(r2[:, :, 32:64], src[:, :, 0:32], again(rot_b[:, t, 32:64], 8), ALU.mult))
                    v.tensor_tensor(r1, r1, r2, ALU.add).then_inc(rotated, 1)
                for t in range(TT):
                    b = take()
                    taken(v.tensor_copy(qkv[:, t, 0:512], b[:, :]))
                    b = take()
                    taken(v.tensor_copy(qkv[:, t, 512:768], b[:, 0:256]))
                for t in range(TT):
                    own(v.tensor_tensor(xnf[:, 512 * t:512 * (t + 1)], qkv[:, t, 0:512], qkv[:, t, 0:512], ALU.mult))
                own(v.tensor_reduce(stat, xnf[:, 0:1024].rearrange("p (u k) -> p u k", k=HD), AX, ALU.add))
                v.tensor_scalar(stat2, stat, EPS, None, ALU.add).then_inc(qk_sums, 1)
                v.wait_ge(qk_rstd, 1)
                stat_t = stat.rearrange("p (t u) -> p t u", t=TT)
                own(v.tensor_scalar(stat_t[:, :, 0:4], stat_t[:, :, 0:4], HD ** -0.5, None, ALU.mult))
                for t in range(TT):
                    q3 = qkv[:, t, 0:512].rearrange("p (u k) -> p u k", k=HD)
                    v.tensor_tensor(q3, q3, wide(stat[:, 8 * t:8 * t + 8], HD), ALU.mult).then_inc(qk_ready, 1)
                v.wait_ge(qk_ready, 2)
                scores(True)
                b = take()
                own(v.tensor_copy(dsm[:, 16 * GC:16 * GC + 32], b[:, 0:32]))
                own(v.tensor_tensor(dcol(T0), dcol(GL), dcol(GC), ALU.subtract))
                taken(v.tensor_copy(egl, b[:, 32:48]))
                v.tensor_copy(dcol(T1), dcol(GC)).then_inc(gdiff, 1)
                weights(0)
                v.wait_ge(*filled["probT03"])
                gc4 = unit_col(GC)
                for d in range(2):
                    for par in range(2):
                        b = take()
                        for k in range(4):
                            t, f = k // 2, k % 2
                            ins = v.tensor_scalar(decay[:, (2 * d + par) * 4 + k, :], b[:, k * P:(k + 1) * P],
                                                  gc4[:, t, d, 2 * f + par:2 * f + par + 1], 0.0, ALU.subtract, ALU.min)
                        taken(ins)
                v.wait_ge(tables_in, 16)
                for h in range(NH):
                    b = take()
                    taken(v.tensor_tensor(retS[:, h, :], b[:, :], decays[:, h, :], ALU.mult))
                b = take()
                taken(v.tensor_copy(ret_o, b[:, :]))
                o3 = ret_o.rearrange("p (u k) -> p u k", k=HD)
                s3 = ret_s.rearrange("p (u k) -> p u k", k=HD)
                own(v.tensor_reduce(stat[:, 0:8], o3, AX, ALU.add))
                own(v.tensor_scalar(stat[:, 0:8], stat[:, 0:8], 1.0 / HD, None, ALU.mult))
                own(v.tensor_tensor(o3, o3, wide(stat[:, 0:8], HD), ALU.subtract))
                own(v.tensor_tensor(s3, o3, o3, ALU.mult))
                own(v.tensor_reduce(stat[:, 0:8], s3, AX, ALU.add))
                v.tensor_scalar(stat[:, 8:16], stat[:, 0:8], 1.0 / HD, EPS, ALU.mult, ALU.add).then_inc(ret_var, 1)
                v.wait_ge(dec_masked, 4)
                v.wait_ge(*filled["probT03"])
                for par in range(2):
                    b = take()
                    for d in range(2):
                        u0 = (2 * d + par) * 4
                        ins = v.tensor_tensor(lT[:, u0:u0 + 4, :], b[:, :].rearrange("p (u k) -> p u k", u=4), decay[:, u0:u0 + 4, :], ALU.mult)
                    taken(ins)
                for par in range(2):
                    b = take()
                    for d in range(2):
                        u0 = (2 * d + par) * 4
                        ins = v.tensor_tensor(decay[:, u0:u0 + 4, :], b[:, :].rearrange("p (u k) -> p u k", u=4), decay[:, u0:u0 + 4, :], ALU.mult)
                    taken(ins)
                v.wait_ge(ret_rstd, 1)
                own(v.tensor_tensor(o3, o3, wide(stat[:, 0:8], HD), ALU.mult))
                v.wait_ge(ret_silu, 1)
                v.tensor_tensor(ret_o.rearrange("p (t k) -> p t k", t=TT), ret_o.rearrange("p (t k) -> p t k", t=TT),
                                projv[:, :, PG_B:PG_B + W], ALU.mult).then_inc(ret_done, 1)
                for q in range(4):
                    b = take()
                    taken(v.tensor_tensor(lT[:, 4 * q:4 * q + 4, :], b[:, :].rearrange("p (u k) -> p u k", u=4), lT[:, 4 * q:4 * q + 4, :], ALU.mult))
                b = take()
                taken(v.tensor_tensor(yT[:, 4:6, :], b[:, :].rearrange("p (c t) -> p c t", c=2), wide(cols[:, 2:4], T), ALU.mult))
                b = take()
                taken(v.tensor_tensor(yT[:, 2:4, :], b[:, :].rearrange("p (c t) -> p c t", c=2), wide(cols[:, 0:2], T), ALU.mult))
                for q in range(4):
                    d = q // 2
                    o = invT[:, 4 * q:4 * q + 4, :]
                    own(v.tensor_tensor(o, lT[:, 4 * q:4 * q + 4, :], again(level[:, 0, d, :], 4), ALU.mult))
                    v.tensor_tensor(o, again(ident, 4), o, ALU.subtract).then_inc(inv0_ready, 1)
                b4, e4, s4 = unit_col(BETA), unit_col(EGC), unit_col(ESL)
                be4 = unit_col(T0)

                def scale_rows(dst, w, col):
                    for d in range(2):
                        for par in range(2):
                            for t in range(TT):
                                u0 = ((2 * d + par) * TT + t) * 2
                                v4 = qkv[:, t, :].rearrange("p (w f a k) -> p w a f k", w=3, f=2, a=2)
                                ins = v.tensor_tensor(dst[:, u0:u0 + 2, :], v4[:, w, par], wide(col[:, t, d, par::2], HD), ALU.mult)
                    ins.then_inc(scaled, 1)

                for n in range(1, LEVELS):
                    for q in range(4):
                        for m in ((inv, invT) if n < LEVELS - 1 else (invT,)):
                            if n == 1 and m is inv:
                                v.wait_ge(*done[f"inv0{q}"])
                            b = take()
                            o = m[:, 4 * q:4 * q + 4, :]
                            taken(v.tensor_tensor(o, o, b[:, :].rearrange("p (u k) -> p u k", u=4), ALU.subtract))
                    if n == 1:
                        v.wait_ge(gexp, 3)
                        v.wait_ge(*filled["diffT"])
                        own(v.tensor_tensor(dcol(T0), dcol(BETA), dcol(EGC), ALU.mult))
                        scale_rows(vbeta, 2, b4)
                    if n == 2:
                        scale_rows(kdec, 1, be4)
                    if n == 3:
                        scale_rows(kstate, 1, s4)
                        for d in range(2):
                            for t in range(TT):
                                ins = v.tensor_tensor(qdec[:, (2 * d + t) * NH:(2 * d + t + 1) * NH, :], qkv[:, t, 0:W].rearrange("p (h k) -> p h k", h=NH),
                                                      wide(e4[:, t, d, :], HD), ALU.mult)
                        ins.then_inc(scaled, 1)
                v.wait_ge(*done["uval"])
                ov = gdn_o.rearrange("p (d t f a e) -> p d t a f e", d=2, t=TT, f=2, a=2)
                u6 = uval.rearrange("p (d a t f) e -> p d a t f e", d=2, a=2, t=TT)
                for s in range(4):
                    where = [(d, (s if d == 0 else 3 - s) // 2, (s if d == 0 else 3 - s) % 2) for d in range(2)]
                    for par in range(2):
                        if s:
                            b = take()
                        for d, t, hf in where:
                            r = slice(hf * HD, (hf + 1) * HD)
                            if s:
                                v.tensor_tensor(vnew[r, par], u6[r, d, par, t], b[r, 0:P].rearrange("p (f e) -> p f e", f=2), ALU.subtract).then_inc(vnew_ready, 1)
                            else:
                                v.tensor_copy(vnew[r, par], u6[r, d, par, t]).then_inc(vnew_ready, 1)
                        if s:
                            taken(v.tensor_copy(stat2[:, 0:1], b[:, 0:1]))
                    if s < 3:
                        for d, t, hf in where:
                            b = take()
                            for f in range(2):
                                k = ((hf * TT + t) * 2 + d) * 2 + f
                                if s:
                                    v.scalar_tensor_tensor(out=state[:, d, f, :], in0=state[:, d, f, :], scalar=egl[:, k:k + 1],
                                                           in1=b[:, f * HD:(f + 1) * HD], op0=ALU.mult, op1=ALU.add).then_inc(state_ready, 1)
                                else:
                                    v.tensor_copy(state[:, d, f, :], b[:, f * HD:(f + 1) * HD]).then_inc(state_ready, 1)
                            taken(v.tensor_copy(stat2[:, 0:1], b[:, 0:1]))
                        v.wait_ge(state_ready, 4 * (s + 1))
                    if s:
                        v.wait_ge(*done[f"gdn_q{s}"])
                    b = take()
                    for d, t, hf in where:
                        r = slice(hf * HD, (hf + 1) * HD)
                        bv = b[r, 0:256].rearrange("p (a f e) -> p a f e", a=2, f=2)
                        for par in range(2):
                            if s:
                                ins = v.tensor_tensor(ov[r, d, t, par], gdn_q[r, par], bv[:, par], ALU.add)
                            else:
                                ins = v.tensor_copy(ov[r, d, t, par], bv[:, par])
                    taken(ins)
                g3 = gdn_o[:, 0:512].rearrange("p (u k) -> p u k", k=HD)
                own(v.tensor_tensor(gdn_o[:, 0:512], gdn_o[:, 0:512], gdn_o[:, 512:1024], ALU.add))
                own(v.tensor_tensor(gdn_o[:, 512:1024], gdn_o[:, 0:512], gdn_o[:, 0:512], ALU.mult))
                own(v.tensor_reduce(stat[:, 0:8], gdn_o[:, 512:1024].rearrange("p (u k) -> p u k", k=HD), AX, ALU.add))
                v.tensor_scalar(stat[:, 8:16], stat[:, 0:8], 1.0 / HD, EPS, ALU.mult, ALU.add).then_inc(gdn_var, 1)
                v.wait_ge(gdn_rstd, 1)
                own(v.tensor_tensor(g3, g3, wide(stat[:, 0:8], HD), ALU.mult))
                v.wait_ge(gdn_silu, 1)
                v.tensor_tensor(gdn_o[:, 0:512].rearrange("p (t k) -> p t k", t=TT), gdn_o[:, 0:512].rearrange("p (t k) -> p t k", t=TT),
                                projv[:, :, PG_D:PG_D + W], ALU.mult).then_inc(gdn_done, 1)
                b = take()
                taken(v.tensor_scalar(yT[:, 6:8, :], b[:, :].rearrange("p (c t) -> p c t", c=2), cols[:, 4:5], None, ALU.mult))

                def add_to_x():
                    for n in range(2):
                        for t in range(TT):
                            b = take()
                            o = x[:, t, n * 512:(n + 1) * 512]
                            taken(v.tensor_tensor(o, o, b[:, :], ALU.add))

                add_to_x()
                norm(x, xn, 2)
                take_turned(xnT, 1)
                scores(False)
                weights(1)
                add_to_x()
                norm(x, xn, 3)
                take_turned(xnT, 3)

                b = take()
                taken(v.tensor_tensor(logit, b[:, 0:72].rearrange("p (t k) -> p t k", t=TT), again(rows[:, 16:52], TT), ALU.add))
                rt = lambda k: small[:, 80 + 16 * k:96 + 16 * k].rearrange("p (t k) -> p t k", t=TT)
                GP, EL, E1, OH1, OH2, GOH, DF, W1, W2 = (rt(k) for k in range(9))
                own(v.tensor_scalar(GP, logit[:, :, 0:8], 0.0, NEG, ALU.mult, ALU.add))
                own(v.tensor_copy(GP[:, :, 0:4], logit[:, :, 0:4]))
                for t in range(TT):
                    own(v.max(val[:, 0, t, :], GP[:, t, :]))
                    own(v.max_index(idx[:, 0, t, :], val[:, 0, t, :], GP[:, t, :]))
                g1 = DF[:, :, 0:1]
                own(v.tensor_copy(g1, idx[:, 0, :, 0:1]))
                for t in range(TT):
                    own(v.tensor_scalar(GOH[:, t, :], c("eight"), g1[:, t, :], None, ALU.is_equal))
                for t in range(TT):
                    own(v.tensor_scalar(W1[:, t, 0:4], GP[:, t, 0:4], val[:, 0, t, 0:1], None, ALU.subtract))
                for t in range(TT):
                    own(v.tensor_scalar(EL[:, t, :], logit[:, t, 4:12], GOH[:, t, 0:1], None, ALU.mult))
                    for g in range(1, NG):
                        own(v.scalar_tensor_tensor(out=EL[:, t, :], in0=logit[:, t, 4 + 8 * g:12 + 8 * g], scalar=GOH[:, t, g:g + 1], in1=EL[:, t, :],
                                                   op0=ALU.mult, op1=ALU.add))
                    own(v.max(val[:, 1, t, :], EL[:, t, :]))
                    own(v.max_index(idx[:, 1, t, :], val[:, 1, t, :], EL[:, t, :]))
                own(v.tensor_copy(DF[:, :, 0:2], idx[:, 1, :, 0:2]))
                for t in range(TT):
                    own(v.tensor_scalar(OH1[:, t, :], c("eight"), DF[:, t, 0:1], None, ALU.is_equal))
                    own(v.tensor_scalar(OH2[:, t, :], c("eight"), DF[:, t, 1:2], None, ALU.is_equal))
                v.tensor_tensor(W1[:, :, 4:5], val[:, 1, :, 1:2], val[:, 1, :, 0:1], ALU.subtract).then_inc(r_max, 1)
                v.wait_ge(r_exp, 1)
                own(v.tensor_reduce(DF[:, :, 2], W2[:, :, 0:4], AX, ALU.add))
                own(v.tensor_scalar(DF[:, :, 3:4], W2[:, :, 4:5], 1.0, None, ALU.add))
                own(v.tensor_tensor(DF[:, :, 4:5], DF[:, :, 2:3], DF[:, :, 3:4], ALU.mult))
                own(v.reciprocal(DF[:, :, 5:6], DF[:, :, 4:5]))
                own(v.tensor_tensor(DF[:, :, 6:7], DF[:, :, 5:6], W2[:, :, 4:5], ALU.mult))
                for t in range(TT):
                    own(v.tensor_tensor(E1[:, t, :], OH1[:, t, :], OH2[:, t, :], ALU.add))
                    own(v.tensor_scalar(W1[:, t, :], OH1[:, t, :], DF[:, t, 5:6], None, ALU.mult))
                    own(v.scalar_tensor_tensor(out=W1[:, t, :], in0=OH2[:, t, :], scalar=DF[:, t, 6:7], in1=W1[:, t, :], op0=ALU.mult, op1=ALU.add))
                    for g in range(NG):
                        own(v.tensor_scalar(gates[:, t, 8 * g:8 * g + 8], W1[:, t, :], GOH[:, t, g:g + 1], None, ALU.mult))
                        own(v.tensor_scalar(ranks[:, t, 8 * g:8 * g + 8], E1[:, t, :], GOH[:, t, g:g + 1], None, ALU.mult))
                own(v.tensor_copy(stat, stat2))
                v.tensor_copy(stat2, stat).then_inc(ind_ready, 1)
                b = take()
                ind = small[:, 256:320].rearrange("p (t e) -> p t e", t=TT)
                own(v.tensor_copy(ind, ranks[:, :, :]))
                own(v.scalar_tensor_tensor(out=ranks[:, :, :], in0=b[:, 0:2 * NE].rearrange("p (t e) -> p t e", t=TT), scalar=1.0, in1=ind,
                                           op0=ALU.add, op1=ALU.mult))
                own(v.tensor_scalar(ranks[:, :, :], ranks[:, :, :], -1.0, None, ALU.add))
                taken(v.tensor_reduce(stat[:, 0:1], b[:, 2 * NE:3 * NE], AX, ALU.max))
                own(v.tensor_scalar(stat[:, 1:2], stat[:, 0:1], 0.0, None, ALU.mult))
                for k in range(1, T // SLOTS):
                    own(v.scalar_tensor_tensor(out=stat[:, 1:2], in0=stat[:, 0:1], scalar=float(k * SLOTS), in1=stat[:, 1:2], op0=ALU.is_gt, op1=ALU.add))
                v.tensor_scalar(npi[0:1, 0:1], stat[0:1, 1:2], 1.0, None, ALU.add).then_inc(np_ready, 1)
                v.tensor_copy(npi[0:1, 1:2], stat[0:1, 1:2]).then_inc(np_ready, 1)
                v.wait_ge(np_ready, 2)
                rounds = v.value_load(npi[0:1, 0:1], min_val=1, max_val=T // SLOTS)

                def expert_pass(it, before_it, q):
                    v.tensor_copy(rank_q[:], ranks[:, :, bass.ds(QUAD * q, QUAD)]).then_inc(quad_ready, 1)
                    v.tensor_copy(gate_q[:], gates[:, :, bass.ds(QUAD * q, QUAD)]).then_inc(quad_ready, 1)
                    v.wait_ge(quad_ready, 2 * it)
                    s3 = sel.rearrange("p t (e s) -> p (t e) s", e=QUAD)
                    w3 = selw.rearrange("p t (e s) -> p (t e) s", e=QUAD)
                    slots8 = again(c("slot"), TT * QUAD)
                    v.tensor_tensor(s3, slots8, wide(rank_q[:].rearrange("p t e -> p (t e)"), SLOTS), ALU.is_equal).then_inc(sel_built, 1)
                    v.wait_ge(sel_built, 2 * before_it + 1)
                    v.tensor_tensor(w3, s3, wide(gate_q[:].rearrange("p t e -> p (t e)"), SLOTS), ALU.mult).then_inc(sel_built, 1)
                    for g in range(2):
                        v.wait_ge(gathered[g], it)
                        v.tensor_tensor(xg[:, 4 * g:4 * g + 4, :], bank[g][:, :].rearrange("p (c s) -> p c s", c=4),
                                        wide(gains[:, 4, 4 * g:4 * g + 4], P), ALU.mult).then_inc(xg_ready[g], 1)
                    v.wait_ge(silu_ready, it)
                    v.wait_ge(up_full, it)
                    v.tensor_tensor(hid, silu_g, bank[4][:, :], ALU.mult).then_inc(hid_ready, 1)
                    for n in range(2):
                        for t in range(TT):
                            v.wait_ge(scattered[2 * n + t], it)
                            o = x[:, t, n * 512:(n + 1) * 512]
                            v.tensor_tensor(o, o, bank[(0, 1, 2, 5)[2 * n + t]][:, :], ALU.add).then_inc(x_added, 1)
                    v.wait_ge(x_added, 4 * it)
                    v.sem_inc(pass_seen, 1)

                with v.Fori(0, rounds) as k:
                    with v.Fori(0, NQ) as q:
                        expert_pass(NQ * k + q + 1, NQ * k + q, q)
                    v.tensor_scalar(ranks[:, :, :], ranks[:, :, :], -float(SLOTS), None, ALU.add).then_inc(ranks_moved, 1)
                    v.wait_ge(ranks_moved, k + 1)
                    v.sem_inc(pass_seen, 1)
                v.drain().then_inc(layer_done, 1)
                v.wait_ge(layer_go, l + 1)
                v.sem_inc(layer_seen, 1)

            v.wait_ge(last_sq, 2)
            v.tensor_scalar(ss[:, 0, 2:4], ss[:, 0, 0:2], 1.0 / D, EPS, ALU.mult, ALU.add).then_inc(last_mean, 1)
            v.wait_ge(last_rstd, 1)
            v.wait_ge(final_in, 16)
            for t in range(TT):
                v.scalar_tensor_tensor(out=xn[:, t, :], in0=x[:, t, :], scalar=rstd[:, 0, t:t + 1], in1=m1[:, 0:D], op0=ALU.mult, op1=ALU.mult).then_inc(last_out, 1)

        @block.scalar
        def _(s):
            s.wait_ge(x_in, 16)
            with s.Fori(0, DEPTH) as l:
                n_in = [0]

                def take():
                    s.wait_ge(act_full, n_in[0] + 1)
                    return bank[4 + n_in[0] % 4]

                def taken(ins):
                    n_in[0] += 1
                    ins.then_inc(act_evac, 1)

                def squares_of(src, junk, k):
                    for t in range(TT):
                        s.activation(junk[:, t, :], src[:, t, :], ACT.Square, accum_out=ss[:, k, t:t + 1]).then_inc(squares, 1)

                def exps(k):
                    for h in range(NH):
                        s.wait_ge(maxed, NH * k + h + 1)
                        for t in range(TT):
                            s.activation(prob[:, h, t, :], prob[:, h, t, :], ACT.Exp, bias=dsm[:, 240 + 2 * h + t:241 + 2 * h + t],
                                         accum_out=stat2[:, 2 * h + t:2 * h + t + 1]).then_inc(exped, 1)

                def memory_keys(n, f):
                    b = take()
                    taken(s.copy(memK[:, 4 * n + f:4 * n + f + 2, :], b[:, :].rearrange("p (c t) -> p c t", c=2)))

                def memory_values(n, t):
                    b = take()
                    taken(s.copy(memV[:, t, n * 512:(n + 1) * 512], b[:, :]))

                squares_of(x, xn, 0)
                s.wait_ge(mem_in, 16)
                squares_of(mem_tok, mem_n, 1)
                for t in range(TT):
                    b = take()
                    taken(s.copy(projv[:, t, PG_D:PW], b[:, 0:PW - PG_D]))
                b = take()
                taken(s.copy(projv[:, 0, 0:512], b[:, :]))
                for ch in range(6):
                    s.wait_ge(conved, ch + 1)
                    s.activation(convT[:, ch, :], convT[:, ch, :], ACT.Silu).then_inc(conv_silu, 1)
                s.wait_ge(*done["gate1"])
                s.activation(projv[:, :, PG_D:PG_D + W], projv[:, :, PG_D:PG_D + W], ACT.Silu).then_inc(gdn_silu, 1)
                s.wait_ge(gate_in, 1)
                s.wait_ge(params_in, 16 * N_PARAMS)
                s.activation(dcol(T1), dcol(T1), ACT.Exp).then_inc(gate_exp, 1)
                s.activation(dcol(T2), dcol(T2), ACT.Exp, scale=-1.0).then_inc(gate_exp, 1)
                s.activation(dcol(T3, 8), rows[:, 0:8], ACT.Exp).then_inc(gate_exp, 1)
                s.wait_ge(gate_exp, 3)
                s.activation(dcol(T1), dcol(T1), ACT.Ln, bias=1.0).then_inc(gate_ln, 1)
                for n in range(1, 3):
                    b = take()
                    taken(s.copy(projv[:, 0, n * 512:(n + 1) * 512], b[:, :]))
                s.wait_ge(*done["tok21"])
                s.wait_ge(*done["tok20"])
                s.activation(projv[:, :, PG_B:PG_B + W], projv[:, :, PG_B:PG_B + W], ACT.Silu).then_inc(ret_silu, 1)
                b = take()
                taken(s.mul(aqkT[:, 0:2, :], b[:, :].rearrange("p (c t) -> p c t", c=2), HD ** -0.5))
                b = take()
                taken(s.copy(aqkT[:, 2:4, :], b[:, :].rearrange("p (c t) -> p c t", c=2)))
                exps(0)
                memory_keys(0, 0)
                for t in range(TT):
                    b = take()
                    taken(s.copy(qkT[:, 0:4, t * P:(t + 1) * P], b[:, :].rearrange("p (c k) -> p c k", c=4)))
                s.wait_ge(gdiff, 1)
                s.activation(dcol(EGC), dcol(T1), ACT.Exp).then_inc(gexp, 1)
                s.activation(dcol(ESL), dcol(T0), ACT.Exp).then_inc(gexp, 1)
                s.wait_ge(*done["gc"])
                s.activation(egl, egl, ACT.Exp).then_inc(gexp, 1)
                for h in range(NH):
                    b = take()
                    taken(s.copy(probT[:, h].rearrange("p c q -> p (c q)"), b[:, :]))
                for t in range(TT):
                    b = take()
                    taken(s.copy(bqkT[:, :, t * P:(t + 1) * P], b[:, :].rearrange("p (c k) -> p c k", c=4)))
                b = take()
                taken(s.copy(yT[:, 0:2, :], b[:, :].rearrange("p (c t) -> p c t", c=2)))
                for q in range(4):
                    s.wait_ge(vec_evac, done["gc"][1] + q + 1)
                    o = decay[:, 4 * q:4 * q + 4, :]
                    s.activation(o, o, ACT.Exp).then_inc(dec_exp, 1)
                memory_keys(0, 2)
                for f in range(2):
                    b = take()
                    taken(s.copy(diffT[:, 2 * f:2 * f + 2, :], b[0:HD, :].rearrange("p (c t) -> p c t", c=2)))
                memory_keys(1, 0)
                for q in range(4):
                    b = take()
                    taken(s.copy(inv[:, 4 * q:4 * q + 4, :], b[:, :].rearrange("p (u k) -> p u k", u=4)))
                for n in range(1, LEVELS):
                    for q in range(4):
                        b = take()
                        taken(s.copy(prod[:, 4 * q:4 * q + 4, :], b[:, :].rearrange("p (u k) -> p u k", u=4)))
                for d in range(2):
                    b = take()
                    taken(s.copy(qdT[:, d].rearrange("p t f k -> p (t f) k"), b[:, :].rearrange("p (u k) -> p u k", u=4)))
                for d in range(2):
                    b = take()
                    taken(s.copy(uval[:, 8 * d:8 * d + 8, :], b[:, :].rearrange("p (u k) -> p u k", u=8)))
                for d in range(2):
                    b = take()
                    taken(s.copy(wT[:, d].rearrange("p t f k -> p (t f) k"), b[:, :].rearrange("p (u k) -> p u k", u=4)))
                for step in range(1, 4):
                    for par in range(2):
                        b = take()
                        if step > 1:
                            s.wait_ge(vec_evac, gdn_read[step - 1])
                        taken(s.copy(gdn_q[:, par], b[:, 0:P].rearrange("p (f e) -> p f e", f=2)))
                    if step == 1:
                        memory_keys(1, 2)
                    if step == 2:
                        memory_values(0, 0)
                memory_values(0, 1)
                memory_values(1, 0)
                memory_values(1, 1)
                s.wait_ge(*done["x_mix1"])
                squares_of(x, xn, 2)
                for n in range(2):
                    for f in range(2):
                        b = take()
                        taken(s.mul(memQ[:, 4 * n + 2 * f:4 * n + 2 * f + 2, :], b[:, :].rearrange("p (c t) -> p c t", c=2), 256 ** -0.5))
                exps(1)
                for h in range(NH):
                    b = take()
                    taken(s.copy(probT[:, h].rearrange("p c q -> p (c q)"), b[:, :]))
                for h in range(NH):
                    b = take()
                    taken(s.copy(attT[:, 2 * h:2 * h + 2, :], b[:, :].rearrange("p (c t) -> p c t", c=2)))
                s.wait_ge(*done["x_mem1"])
                squares_of(x, xn, 3)
                s.wait_ge(r_max, 1)
                rw = small[:, 80 + 16 * 7:80 + 16 * 9].rearrange("p (w t k) -> p w t k", w=2, t=TT)
                s.activation(rw[:, 1, :, 0:5], rw[:, 0, :, 0:5], ACT.Exp).then_inc(r_exp, 1)
                s.wait_ge(np_ready, 2)
                rounds = s.value_load(npi[0:1, 0:1], min_val=1, max_val=T // SLOTS)

                def expert_pass(it):
                    s.wait_ge(sel_turned, it)
                    s.copy(selwT, bank[2][:, 0:T].rearrange("p (t k) -> p t k", t=TT)).then_inc(selwT_ready, 1)
                    s.wait_ge(gate_full, it)
                    s.activation(silu_g, bank[3][:, :], ACT.Silu).then_inc(silu_ready, 1)
                    s.wait_ge(hid_turned, it)
                    s.copy(hidT, bank[5][:, :].rearrange("p (c s) -> p c s", c=4)).then_inc(hidT_ready, 1)
                    for n in range(2):
                        s.wait_ge(y_full[n], it)
                        s.copy(y_e[:, n * 512:(n + 1) * 512], bank[6 + n][:, :]).then_inc(y_ready[n], 1)

                with s.Fori(0, rounds) as k:
                    with s.Fori(0, NQ) as q:
                        expert_pass(NQ * k + q + 1)
                s.drain().then_inc(layer_done, 1)
                s.wait_ge(layer_go, l + 1)
                s.sem_inc(layer_seen, 1)
            for t in range(TT):
                s.activation(xn[:, t, :], x[:, t, :], ACT.Square, accum_out=ss[:, 0, t:t + 1]).then_inc(last_sq, 1)

        @block.gpsimd
        def _(g):
            g.wait_ge(preset, 2)
            g.wait_ge(const_in, 16)
            with g.Fori(0, DEPTH) as l:
                def root(k):
                    g.wait_ge(means, k + 1)
                    g.tensor_tensor(rstd[:, k, :], ss[:, k, 2:4], mhalf[:, 0:2], ALU.pow).then_inc(rstds, 1)

                root(0)
                root(1)
                g.wait_ge(qk_sums, 1)
                g.tensor_tensor(stat, stat2, mhalf[:], ALU.pow).then_inc(qk_rstd, 1)
                for q in range(4):
                    g.wait_ge(dec_exp, q + 1)
                    o = decay[:, 4 * q:4 * q + 4, :]
                    g.tensor_tensor(o, o, again(tri[:, q // 2, :], 4), ALU.mult).then_inc(dec_masked, 1)
                g.wait_ge(ret_var, 1)
                g.tensor_tensor(stat[:, 0:8], stat[:, 8:16], mhalf[:, 0:8], ALU.pow).then_inc(ret_rstd, 1)
                g.wait_ge(inv0_ready, 4)
                for n in range(1, LEVELS):
                    if n > 1:
                        g.wait_ge(*filled[f"low_used{n - 1}"])
                    for d in range(2):
                        g.tensor_tensor(low[:, 8 * d:8 * d + 8, :], lT[:, 8 * d:8 * d + 8, :], again(level[:, n, d, :], 8), ALU.mult).then_inc(low_ready, 1)
                g.wait_ge(gdn_var, 1)
                g.tensor_tensor(stat[:, 0:8], stat[:, 8:16], mhalf[:, 0:8], ALU.pow).then_inc(gdn_rstd, 1)
                root(2)
                root(3)
                g.drain().then_inc(layer_done, 1)
                g.wait_ge(layer_go, l + 1)
                g.sem_inc(layer_seen, 1)
            g.wait_ge(last_mean, 1)
            g.tensor_tensor(rstd[:, 0, :], ss[:, 0, 2:4], mhalf[:, 0:2], ALU.pow).then_inc(last_rstd, 1)

        @block.sync
        def _(sp):
            def unit_source(layer, n):
                names = {U_DQK: ("w_in", 2048), U_DVG: ("w_in", 2560), U_TOK: ("w_in", 512), U_TOK + 1: ("w_in", 1024),
                         U_TOK + 2: ("w_in", 1536), U_AQK: ("w_in", 0)}
                for u, name in ((U_MK, "mem_w_k"), (U_MV, "mem_w_v"), (U_OUT, "w_out"), (U_MQ, "mem_w_q"), (U_MO, "mem_w_o")):
                    names[u], names[u + 1] = (name, 0), (name, 512)
                name, lo = names[n]
                w = a[name][layer:layer + 1] if isinstance(layer, int) else a[name][bass.ds(layer, 1)]
                return w[:, :, lo:lo + 512].rearrange("l (c p) n -> p (l c) n", p=P)

            def unit_tile(n):
                return ring[:, slot(n), :].rearrange("p (c k) -> p c k", c=DC)

            sp.dma_start(x[:], a["x"].rearrange("b (t p) d -> p (b t) d", p=P)).then_inc(x_in, 16)
            sp.dma_start(const[:], a["consts"]).then_inc(const_in, 16)
            for n in range(NSLOT):
                sp.dma_start(unit_tile(n), unit_source(0, n)).then_inc(first_in[n], 16)
            with sp.Fori(0, DEPTH) as l:
                lay = lambda name: a[name][bass.ds(l, 1)]
                n_par = [0]

                def param(dst, src, signal=params_in):
                    sp.dma_start(dst, src, allow_slow_non_contiguous=True).then_inc(signal, 16)
                    n_par[0] += signal is params_in

                for k, name in enumerate(("mix_norm_g", "mem_q_norm_g", "mem_kv_norm_g", "ffn_norm_g")):
                    param(gains[:, k, :], lay(name).rearrange("l (c p) -> p (l c)", p=P), gains_in)
                param(gains[:, 4, :], lay("ffn_norm_g").rearrange("l (p c) -> p (l c)", p=P), gains_in)
                sp.dma_start(mem_tok, a["mem"].rearrange("b (t p) d -> p (b t) d", p=P)).then_inc(mem_in, 16)
                param(w_ab[:], lay("w_in")[:, :, 3072:3088].rearrange("l (c p) n -> p (l c) n", p=P))
                for k in range(4):
                    param(conv_w[:, k, :], lay("gdn_conv_w")[:, k, :].rearrange("l (c p) -> p (l c)", p=P))
                param(rows[:, 0:8], lay("gdn_a_log").rearrange("l d h -> l (d h)").to_broadcast([P, 8]))
                param(rows[:, 8:16], lay("gdn_dt_bias").rearrange("l d h -> l (d h)").to_broadcast([P, 8]))
                param(rows[:, 16:20], lay("b_group").to_broadcast([P, 4]))
                param(rows[:, 20:52], lay("b_router").to_broadcast([P, NE]))
                param(cols[:, 0:2], lay("ret_norm_g").rearrange("l (c p) -> p (l c)", p=P))
                param(cols[:, 2:4], lay("pool_scale").rearrange("l (c p) -> p (l c)", p=P))
                for k in range(2):
                    param(cols[k * HD:(k + 1) * HD, 4:5], lay("gdn_norm_g").rearrange("l p -> p l"))
                param(pool_w[:], lay("pool_w").rearrange("l g c e -> c (l g) e"))
                param(router_w[:, :, 0:NG], lay("w_group").rearrange("l (c p) n -> p (l c) n", p=P))
                param(router_w[:, :, NG:NG + NE], lay("w_router").rearrange("l (c p) n -> p (l c) n", p=P))
                assert n_par[0] == N_PARAMS, n_par
                for t in range(TT):
                    for r in range(2):
                        for h in range(NH):
                            row = 2 * t + r
                            src = bass.AP(a["na_rpb"].tensor, l * (NH * RPB_H * RPB_W) + ((7 - row) * RPB_W + 15 - 63 + RPB_H * RPB_W * h),
                                          [[1, GRID_W], [RPB_W, ROWS], [1, GRID_W]])
                            sp.dma_start(bias[GRID_W * r:GRID_W * (r + 1), t, h, :].rearrange("p (r k) -> p r k", r=ROWS), src).then_inc(rpb_in, 16)
                sp.dma_start(tables[:], a["big_consts"]).then_inc(tables_in, 16)

                for n in range(NSLOT, PRE_UNITS):
                    sp.wait_ge(*last_reader[n - NSLOT])
                    sp.dma_start(unit_tile(n), unit_source(l, n)).then_inc(unit_in[slot(n)], 16)

                def expert_unit(n, first):
                    name, k = (("w_gate", n), ("w_up", n - 4), ("w_down", n - 8))[n // 4]
                    rows_of = a[name].rearrange("l e (p c) f -> (l e) p (c f)", p=P)[bass.ds(first, QUAD)]
                    sp.dma_start(ring[:, n % NSLOT, :].rearrange("p (e k) -> p e k", e=QUAD),
                                 rows_of[:, :, 1024 * k:1024 * (k + 1)].rearrange("e p k -> p e k")).then_inc(unit_in[n % NSLOT], 16)

                RELEASE = (1, 2, 3, 4, 4, 5, 6, 7, 7, 8, 9, 10)

                def units(q, lo, hi, released):
                    first = sp.snap(l * NE + QUAD * q)
                    for n in range(lo, hi):
                        sp.wait_ge(units_free, released + RELEASE[(n + 12 - NSLOT) % 12])
                        if n % 4 == 0:
                            sp.sem_inc(pass_seen, 1)
                        expert_unit(n, first)

                for n in range(NSLOT):
                    sp.wait_ge(*last_reader[PRE_UNITS - NSLOT + n])
                    expert_unit(n, l * NE)
                with sp.Fori(0, NQ - 1) as q:
                    units(q, NSLOT, 12, 10 * q)
                    units(q + 1, 0, NSLOT, 10 * q)
                units(NQ - 1, NSLOT, 12, 10 * (NQ - 1))
                sp.wait_ge(np_ready, 2)
                further = sp.value_load(npi[0:1, 1:2], min_val=0, max_val=T // SLOTS - 1)
                with sp.If(further > 0):
                    with sp.Fori(0, further) as k:
                        with sp.Fori(0, NQ) as q:
                            units(q, 0, NSLOT, 10 * (NQ * k + q) + 10 * (NQ - 1))
                            units(q, NSLOT, 12, 10 * (NQ * k + q) + 10 * NQ)
                with sp.If(l < DEPTH - 1):
                    following = nc.s_assert_within(sp.snap(l + 1), 0, DEPTH - 1, skip_runtime_bounds_check_because="the branch is taken before the last layer only")
                    for n in range(NSLOT):
                        sp.wait_ge(units_free, 10 * NQ * further + (10 * (NQ - 1) + RELEASE[12 - NSLOT + n]))
                        sp.sem_inc(pass_seen, 1)
                        sp.dma_start(unit_tile(n), unit_source(following, n)).then_inc(first_in[n], 16)
                sp.wait_ge(layer_done, 4)

                for q in layer_sems:
                    sp.sem_clear(q)
                sp.sem_inc(layer_go, 1)
            sp.dma_start(m1[:, 0:D], a["final_norm_g"].rearrange("(o d) -> o d", o=1).to_broadcast([P, D])).then_inc(final_in, 16)
            sp.wait_ge(last_out, 2)
            sp.dma_start(out.rearrange("b (t p) d -> p (b t) d", p=P), xn[:]).then_inc(stored, 16)
            sp.wait_ge(stored, 16)


N_PARAMS = 16
_INS = ("x", "mem", "mix_norm_g", "w_in", "na_rpb", "ret_norm_g", "pool_w", "pool_scale", "gdn_conv_w", "gdn_a_log", "gdn_dt_bias",
        "gdn_norm_g", "w_out", "mem_q_norm_g", "mem_kv_norm_g", "mem_w_q", "mem_w_k", "mem_w_v", "mem_w_o", "ffn_norm_g", "w_group",
        "b_group", "w_router", "b_router", "w_gate", "w_up", "w_down", "final_norm_g")


def kernel(**inputs):
    import concourse.bacc as _bacc
    from concourse.bass_utils import run_bass_kernel_spmd as _run

    nc = _bacc.Bacc("TRN2", target_bir_lowering=False, num_devices=1)
    small_tables, big_tables = constant_tables()
    arrays = {name: np.ascontiguousarray(inputs[name]) for name in _INS}
    arrays["consts"], arrays["big_consts"] = small_tables, big_tables
    a = {name: nc.dram_tensor(f"in_{name}", v.shape, F32, kind="ExternalInput").ap() for name, v in arrays.items()}
    out = nc.dram_tensor("out_0", (1, T, D), F32, kind="ExternalOutput").ap()
    encoder(nc, a, out, {})
    r = _run(nc, [{f"in_{name}": v for name, v in arrays.items()}], core_ids=[0])
    return r.results[0]["out_0"]
```

```python
from contextlib import ExitStack

import numpy as np
import concourse.bass as bass
from concourse import mybir

F32 = mybir.dt.float32
I32 = mybir.dt.int32
U32 = mybir.dt.uint32
ALU = mybir.AluOpType
ACT = mybir.ActivationFunctionType
AX = mybir.AxisListType.X

P = 128
D = 1024
T = 256
TT = T // P
DC = D // P
DEPTH = 2
GRID_W = 64
ROWS = T // GRID_W
HD = 64
NH = 4
W = NH * HD
RPB_H, RPB_W = 15, 31
NE = 32
EPG = 8
NG = 4
DE = 512
CHUNK = 64
LEVELS = 6
QUAD = 4
SLOTS = 32
NQ = NE // QUAD
NSLOT = 4
ESLOT = 8
AHEAD = 2
EPS = 1e-6
POOL_WINDOWS = (2, 4, 8, 16)
NEG = -1e30

PV_A, PQ_B, PK_B, PV_B, PG_B, PU_C, PG_D, PAB = 0, 256, 512, 768, 1024, 1280, 1536, 1792
PW = PAB + 4 * NH

CONSTS = {}
_at = 0
for _name, _width in (("ident", P), ("anti", P), ("band", T), ("tri", 2 * P), ("level", LEVELS * 2 * P),
                      ("blocks", P), ("ones", P), ("before", P), ("rot_a", TT * HD), ("rot_b", TT * HD),
                      ("slot", SLOTS), ("eight", EPG), ("halves", 2), ("fulls", T // SLOTS - 1)):
    CONSTS[_name] = (_at, _width)
    _at += _width
NCONST = _at


def constant_tables():
    c = np.zeros((P, NCONST), np.float32)

    def put(name, value):
        at, width = CONSTS[name]
        c[:, at:at + width] = np.asarray(value, np.float32).reshape(P, width)

    p = np.arange(P)
    j, i = p[:, None], p[None, :]
    put("ident", j == i)
    put("anti", (j // 64 == i // 64) & (j % 64 == 63 - i % 64))
    qc, kc = (p % GRID_W)[:, None], (np.arange(T) % GRID_W)[None, :]
    lo = np.clip(qc - 8, 0, GRID_W - 16)
    put("band", np.where((kc >= lo) & (kc < lo + 16), 0.0, NEG))
    same = j // CHUNK == i // CHUNK
    put("tri", np.stack([same & (j <= i), same & (j >= i)], 1))
    levels = []
    for n in range(LEVELS):
        b = 1 << n
        pair = j // (2 * b) == i // (2 * b)
        levels += [pair & (j // b % 2 == 0) & (i // b % 2 == 1), pair & (j // b % 2 == 1) & (i // b % 2 == 0)]
    put("level", np.stack(levels, 1))
    put("blocks", same)
    put("ones", np.ones((P, P)))
    put("before", j < i)
    inv = np.float32(10000.0) ** (-np.arange(HD // 2, dtype=np.float32) / np.float32(HD // 2))
    ang = (np.arange(T, dtype=np.float32)[:, None] * inv[None, :]).astype(np.float32)
    cos, sin = np.cos(ang), np.sin(ang)
    tiled = lambda a: a.reshape(TT, P, HD).transpose(1, 0, 2)
    put("rot_a", tiled(np.concatenate([cos, cos], 1)))
    put("rot_b", tiled(np.concatenate([-sin, sin], 1)))
    put("slot", np.broadcast_to(np.arange(SLOTS), (P, SLOTS)))
    put("eight", np.broadcast_to(np.arange(EPG), (P, EPG)))
    put("fulls", np.broadcast_to(SLOTS * np.arange(1, T // SLOTS), (P, T // SLOTS - 1)))
    put("halves", np.stack([p < 64, p >= 64], 1))

    t = np.arange(T)
    diff = (t[None, :] - t[:, None]).astype(np.float64)
    lg = np.log1p(-np.exp2(-5.0 - np.arange(NH)))
    decay = np.stack([np.where(diff >= 0, np.exp(lg[h] * np.maximum(diff, 0)),
                               np.exp(lg[::-1][h] * np.maximum(-diff, 0))) for h in range(NH)]) * HD ** -0.5
    pools = []
    for w in POOL_WINDOWS:
        a, b = np.clip(t - w // 2, 0, T), np.clip(t + w // 2, 0, T)
        inside = (t[:, None] >= a[None, :]) & (t[:, None] < b[None, :])
        pools.append(inside / (b - a)[None, :] - (t[:, None] == t[None, :]))
    fold = lambda m: np.stack(m).reshape(4, TT, P, T).transpose(2, 0, 1, 3).reshape(P, 4 * TT * T)
    big = np.concatenate([fold(decay), fold(pools)], 1).astype(np.float32)
    return c, big


def encoder(nc, a, out):
    ctx = ExitStack()
    with ctx:
        sb = lambda name, shape, dt=F32: ctx.enter_context(nc.sbuf_tensor(name, shape, dt))

        def wide(ap, n):
            return ap.rearrange("p (k o) -> p k o", o=1).to_broadcast([ap.shape[0], ap.shape[1], n])

        def again(ap, n):
            return ap.rearrange("p (o k) -> p o k", o=1).to_broadcast([ap.shape[0], n, ap.shape[1]])

        ring = sb("ring", [P, ESLOT, 4096])
        x = sb("x", [P, TT, D])
        xn = sb("xn", [P, TT, D])
        xnT = sb("xnT", [P, DC, T])
        m1, m2, m3, m4 = (sb(f"m{k}", [P, 2048]) for k in (1, 2, 3, 4))
        conv_in = sb("conv_in", [P, 6, T + 3])
        const = sb("const", [P, NCONST])
        all_gains = sb("all_gains", [P, 5, DEPTH, DC])
        gains = sb("gains", [P, 5, DC])
        cols = sb("cols", [P, 8])
        rows = sb("rows", [P, 16 + 4 + NE])
        router_w = sb("router_w", [P, DC, NG + NE])
        tables = ring[:, NSLOT, :]
        memT, memK = (ring[:, NSLOT + 1, k * 2048:(k + 1) * 2048].rearrange("p (c t) -> p c t", c=DC) for k in range(2))
        PARAMS = TT * PW
        proj = ring[:, NSLOT + 2, 0:PARAMS]
        w_ab = ring[:, NSLOT + 2, PARAMS:PARAMS + 128].rearrange("p (c k) -> p c k", c=DC)
        pool_w = ring[0:HD, NSLOT + 2, PARAMS + 128:PARAMS + 384].rearrange("p (g k) -> p g k", g=4)
        conv_w = ring[:, NSLOT + 2, PARAMS + 384:PARAMS + 408].rearrange("p (k c) -> p k c", k=4)
        rpb = ring[:, NSLOT + 3, 0:2048]
        yT = ring[:, NSLOT + 3, 2048:4096].rearrange("p (c t) -> p c t", c=DC)
        ss = sb("ss", [P, 4, 6])
        rstd = sb("rstd", [P, 4, 2])
        mhalf = sb("mhalf", [P, 16])
        small = sb("small", [P, 512])
        npi = sb("npi", [1, 2], I32)
        idx = sb("idx", [P, 2, TT, 8], U32)
        val = sb("val", [P, 2, TT, 8])
        rank_q = sb("rank_q", [P, TT, QUAD])
        gate_q = sb("gate_q", [P, TT, QUAD])
        ranks = sb("ranks", [P, TT, NE])
        gates = sb("gates", [P, TT, NE])

        def c(name):
            at, width = CONSTS[name]
            return const[:, at:at + width]

        ident, anti, ones, blocks, before = c("ident"), c("anti"), c("ones"), c("blocks"), c("before")
        tri = c("tri").rearrange("p (d k) -> p d k", d=2)
        level = c("level").rearrange("p (n d k) -> p n d k", n=LEVELS, d=2)
        rot_a = c("rot_a").rearrange("p (t k) -> p t k", t=TT)
        rot_b = c("rot_b").rearrange("p (t k) -> p t k", t=TT)
        halves = c("halves")
        projv = proj.rearrange("p (t k) -> p t k", t=TT)

        aqkT = m3[:, 1024:2048].rearrange("p (c t) -> p c t", c=4)
        prob = m1[:, :].rearrange("p (h t k) -> p h t k", h=NH, t=TT)
        probT = m2[:, :].rearrange("p (h c q) -> p h c q", h=NH, c=2)
        bias = rpb.rearrange("p (t h k) -> p t h k", t=TT, h=NH)
        rot1 = m4[:, 0:1024].rearrange("p (t k) -> p t k", t=TT)
        rot2 = m4[:, 1024:2048].rearrange("p (t k) -> p t k", t=TT)
        bqkT = m3[:, 0:1024].rearrange("p (c t) -> p c t", c=4)
        retS = xn[:, :, :].rearrange("p t (u k) -> p (t u) k", k=512)
        ret_o = m4[:, 0:512]
        ret_s = m4[:, 512:1024]
        diffT = m3[0:HD, 1024:2048].rearrange("p (g t) -> p g t", g=4)
        units = lambda m: m.rearrange("p (u k) -> p u k", k=P)
        decay, lT, inv, invT = (units(m[:, :]) for m in (m1, m2, m3, m4))
        low = units(xn[:, :, :].rearrange("p t k -> p (t k)"))
        prod = units(rpb)
        qkv = conv_in[:, :, :].rearrange("p c t -> p (c t)")[:, 0:TT * 768].rearrange("p (t k) -> p t k", t=TT)
        qkT = xnT
        wT = m2[:, 0:1024].rearrange("p (d t f k) -> p d t f k", d=2, t=TT, f=2)
        qdT = m2[:, 1024:2048].rearrange("p (d t f k) -> p d t f k", d=2, t=TT, f=2)
        uval = m3[:, 0:1024].rearrange("p (u k) -> p u k", k=HD)
        decays = tables[:, 0:2048].rearrange("p (h k) -> p h k", h=NH)
        pools = tables[:, 2048:4096].rearrange("p (g s t) -> p g s t", g=4, s=TT)
        vbeta, kdec, kstate, qdec = (tables[:, 1024 * k:1024 * (k + 1)].rearrange("p (u k) -> p u k", k=HD) for k in range(4))
        xnf = xn[:, :, :].rearrange("p t k -> p (t k)")
        gdn_o = xnf[:, 1024:2048]
        state = small[:, 0:256].rearrange("p (d f e) -> p d f e", d=2, f=2)
        vnew = small[:, 256:512].rearrange("p (a f e) -> p a f e", a=2, f=2)
        dsm = sb("dsm", [P, 16 * 16])
        dcol = lambda k, n=16: dsm[:, 16 * k:16 * k + n]
        unit_col = lambda k: dcol(k).rearrange("p (t d h) -> p t d h", t=TT, d=2)
        G, BETA, GC, GL, EGC, ESL, T0, T1, T2, T3 = range(10)
        gmask = dsm[:, 160:192].rearrange("p (v u) -> p v u", v=2)
        egl = dsm[:, 192:208]
        stat = dsm[:, 208:224]
        stat2 = dsm[:, 224:240]
        gdn_q = xnf[:, 0:256].rearrange("p (a f e) -> p a f e", a=2, f=2)
        mem_tok, mem_n = (m[:, :].rearrange("p (t k) -> p t k", t=TT) for m in (m1, m2))
        memV = projv[:, :, 0:D]
        convT = yT
        memQ = yT
        attT = m3[:, :].rearrange("p (c t) -> p c t", c=DC)
        sel = m1[:, 0:256].rearrange("p (t s) -> p t s", t=TT)
        selw = m1[:, 256:512].rearrange("p (t s) -> p t s", t=TT)
        selwT = m1[:, 512:768].rearrange("p (t k) -> p t k", t=TT)
        xg = m2[:, 0:1024].rearrange("p (c s) -> p c s", c=DC)
        xn_by_row = xn[:, :, :].rearrange("p t (k c) -> p t c k", c=DC)
        silu_g, hid = m3[:, 0:512], m3[:, 512:1024]
        hid_by_row = hid.rearrange("p (k c) -> p c k", c=4)
        hidT = m3[:, 1024:1536].rearrange("p (c s) -> p c s", c=4)
        y_e = m4[:, 0:1024]
        logit = small[:, 0:TT * 36].rearrange("p (t k) -> p t k", t=TT)

        bank = [ctx.enter_context(nc.psum_tensor(f"bank{k}", [P, 512], F32)) for k in range(8)]

        sem = lambda name: ctx.enter_context(nc.semaphore(name))
        ident_in, const_in, x_in, preset, layer_go = sem("ident_in"), sem("const_in"), sem("x_in"), sem("preset"), sem("layer_go")
        stored, final_in = sem("stored"), sem("final_in")
        x_squares, last_mean, last_rstd, last_out = sem("x_squares"), sem("last_mean"), sem("last_rstd"), sem("last_out")
        layer_seen, pass_seen = sem("layer_seen"), sem("pass_seen")
        gains_in = sem("gains_in")
        layer_sems = []
        mixer_sems = []

        def lsem(name):
            s = sem(name)
            mixer_sems.append(s)
            return s

        def esem(name):
            s = sem(name)
            layer_sems.append(s)
            return s

        first_in = [sem(f"first_in{k}") for k in range(AHEAD)]
        unit_in = [lsem(f"unit_in{k}") for k in range(NSLOT)]
        expert_in = [esem(f"expert_in{k}") for k in range(ESLOT)]
        params_in, rpb_in, mem_in = lsem("params_in"), lsem("rpb_in"), lsem("mem_in")
        tables_in = lsem("tables_in")
        vec_full, vec_evac, act_full, act_evac = lsem("vec_full"), lsem("vec_evac"), lsem("act_full"), lsem("act_evac")
        vec_step = lsem("vec_step")
        squares, means, rstds, normed = lsem("squares"), lsem("means"), lsem("rstds"), lsem("normed")
        maxed, exped, probs_ready = lsem("maxed"), lsem("exped"), lsem("probs_ready")
        rotated, ret_silu, ret_var, ret_rstd, ret_done = lsem("rotated"), lsem("ret_silu"), lsem("ret_var"), lsem("ret_rstd"), lsem("ret_done")
        conved, conv_silu, qk_sums, qk_rstd, qk_ready = lsem("conved"), lsem("conv_silu"), lsem("qk_sums"), lsem("qk_rstd"), lsem("qk_ready")
        gate_in, gate_exp, gate_ln, g_ready = lsem("gate_in"), lsem("gate_exp"), lsem("gate_ln"), lsem("g_ready")
        gdiff, gexp, dec_exp, dec_masked, low_ready = lsem("gdiff"), lsem("gexp"), lsem("dec_exp"), lsem("dec_masked"), lsem("low_ready")
        inv0_ready, scaled, vnew_ready = lsem("inv0_ready"), lsem("scaled"), lsem("vnew_ready")
        state_ready, gdn_var, gdn_rstd, gdn_silu, gdn_done = lsem("state_ready"), lsem("gdn_var"), lsem("gdn_rstd"), lsem("gdn_silu"), lsem("gdn_done")
        r_max, r_exp, ind_ready, np_ready = lsem("r_max"), lsem("r_exp"), lsem("ind_ready"), lsem("np_ready")
        sel_built, sel_turned, selwT_ready, x_added = esem("sel_built"), esem("sel_turned"), esem("selwT_ready"), esem("x_added")
        gathered, xg_ready = [esem(f"gathered{k}") for k in range(2)], [esem(f"xg_ready{k}") for k in range(2)]
        gate_full, up_full, silu_ready, hid_ready = esem("gate_full"), esem("up_full"), esem("silu_ready"), esem("hid_ready")
        hid_turned, hidT_ready, y_full = esem("hid_turned"), esem("hidT_ready"), [esem(f"y_full{k}") for k in range(2)]
        y_ready, scattered = [esem(f"y_ready{k}") for k in range(2)], [esem(f"scattered{k}") for k in range(4)]
        units_free = esem("units_free")
        layer_done, quad_ready = esem("layer_done"), esem("quad_ready")
        ranks_moved = esem("ranks_moved")

        PRE_UNITS = 16
        slot = lambda n: n % NSLOT
        U_DQK, U_DVG, U_TOK, U_AQK, U_MK, U_MV, U_OUT, U_MQ, U_MO = 0, 1, 2, 5, 6, 8, 10, 12, 14
        last_reader = {}
        done = {}
        filled = {}
        gdn_read = {}

        ring3 = lambda n, k: ring[:, slot(n), 0:DC * k].rearrange("p (c k) -> p c k", k=k)

        block = ctx.enter_context(nc.Block())

        @block.tensor
        def _(pe):
            pe.wait_ge(ident_in, 16)
            pe.wait_ge(preset, 2)
            with pe.Fori(0, DEPTH) as l:
                count = {"v": 0, "a": 0}
                evac = {"v": vec_evac, "a": act_evac}
                full = {"v": vec_full, "a": act_full}

                def fill(r):
                    n = count[r]
                    if n >= 4:
                        pe.wait_ge(evac[r], n - 3)
                    return bank[(0 if r == "v" else 4) + n % 4]

                def end(r, mm, name=None, units=()):
                    mm.then_inc(full[r], 1)
                    count[r] += 1
                    if name:
                        done[name] = (evac[r], count[r])
                        filled[name] = (full[r], count[r])
                    for u in units:
                        last_reader[u] = (full[r], count[r])

                def need(name):
                    pe.wait_ge(*done[name])

                def unit(n):
                    if n < AHEAD:
                        pe.wait_ge(first_in[n], 16 * l + 16)
                    else:
                        pe.wait_ge(unit_in[slot(n)], 16 * (n // NSLOT + (slot(n) >= AHEAD)))

                def turn_x(name, src, k):
                    for t in range(TT):
                        pe.wait_ge(normed, 2 * k + t + 1)
                        for g in range(2):
                            b = fill("v")
                            for q in range(4):
                                mm = pe.transpose(b[:, q * P:(q + 1) * P], src[:, t, (4 * g + q) * P:(4 * g + q + 1) * P], ident)
                            end("v", mm, name)

                def feature_major(n, f, rhsT, r, name):
                    w = ring3(n, 512)
                    b = fill(r)
                    for q in range(2):
                        for ch in range(DC):
                            mm = pe.matmul(b[:, q * T:(q + 1) * T], w[:, ch, (f + q) * P:(f + q + 1) * P], rhsT[:, ch, :],
                                           start=ch == 0, stop=ch == DC - 1)
                    end(r, mm, name, (n,))

                def token_major(n, t, lhsT, r, name):
                    w = ring3(n, 512)
                    b = fill(r)
                    for ch in range(DC):
                        mm = pe.matmul(b[:, :], lhsT[:, ch, t * P:(t + 1) * P], w[:, ch, :], start=ch == 0, stop=ch == DC - 1)
                    end(r, mm, name, (n,))

                def memory_keys(n, f):
                    need("memT")
                    unit(U_MK + n)
                    feature_major(U_MK + n, f, memT, "a", "memK")

                def memory_values(n, t):
                    unit(U_MV + n)
                    token_major(U_MV + n, t, memT, "a", "memV")

                def turn_probs(k):
                    for h in range(NH):
                        pe.wait_ge(probs_ready, NH * k + h + 1)
                        b = fill("a")
                        for kc in range(2):
                            for t in range(TT):
                                mm = pe.transpose(b[:, (2 * kc + t) * P:(2 * kc + t + 1) * P], prob[:, h, t, kc * P:(kc + 1) * P], ident)
                        end("a", mm, f"probT{k}{h}")

                turn_x("xnT", xn, 0)
                need("xnT")
                unit(U_DQK)
                feature_major(U_DQK, 0, xnT, "v", "dqk0")
                feature_major(U_DQK, 2, xnT, "v", "dqk1")
                unit(U_DVG)
                feature_major(U_DVG, 0, xnT, "v", "dv")
                pe.wait_ge(params_in, 16 * N_PARAMS)
                wg = ring3(U_DVG, 512)
                for t in range(TT):
                    b = fill("a")
                    for ch in range(DC):
                        pe.matmul(b[:, 0:W], xnT[:, ch, t * P:(t + 1) * P], wg[:, ch, W:2 * W], start=ch == 0, stop=ch == DC - 1)
                    for ch in range(DC):
                        mm = pe.matmul(b[:, W:W + 16], xnT[:, ch, t * P:(t + 1) * P], w_ab[:, ch, :], start=ch == 0, stop=ch == DC - 1)
                    end("a", mm, f"gate{t}", (U_DVG,))
                pe.wait_ge(const_in, 16)
                turn_x("memT", mem_n, 1)
                for n in range(3):
                    unit(U_TOK + n)
                    for t in range(TT):
                        token_major(U_TOK + n, t, xnT, "av"[t], f"tok{n}{t}")
                unit(U_AQK)
                feature_major(U_AQK, 0, xnT, "a", "aqk0")
                feature_major(U_AQK, 2, xnT, "a", "aqk1")
                filled["projected"] = filled["aqk1"]

                pe.wait_ge(conv_silu, 6)
                for t in range(TT):
                    b = fill("v")
                    for q in range(4):
                        mm = pe.transpose(b[:, q * P:(q + 1) * P], convT[:, q, t * P:(t + 1) * P], ident)
                    end("v", mm)
                    b = fill("v")
                    for q in range(2):
                        mm = pe.transpose(b[:, q * P:(q + 1) * P], convT[:, 4 + q, t * P:(t + 1) * P], ident)
                    end("v", mm)

                need("aqk1")
                pe.wait_ge(rpb_in, 16 * 16)
                for h in range(NH):
                    b = fill("v")
                    r0 = (h % 2) * HD
                    for t in range(TT):
                        o = b[:, t * T:(t + 1) * T]
                        pe.matmul(o, aqkT[r0:r0 + HD, h // 2, t * P:(t + 1) * P], aqkT[r0:r0 + HD, 2 + h // 2, :], start=True, stop=False)
                        mm = pe.matmul(o, anti, bias[:, t, h, :], start=False, stop=True)
                    end("v", mm, f"ascore{h}")
                memory_keys(0, 0)
                pe.wait_ge(g_ready, 1)
                b = fill("v")
                g4 = unit_col(G)
                for d in range(2):
                    for t in range(TT):
                        pe.matmul(b[:, 8 * t + 4 * d:8 * t + 4 * d + 4], tri[:, d, :], g4[:, t, d, :], start=True, stop=True)
                pe.matmul(b[:, 16:32], blocks, dcol(G), start=True, stop=True)
                gm = gmask.rearrange("p v (u h) -> p (v u) h", h=NH)
                for par in range(2):
                    mm = pe.matmul(b[par * HD:(par + 1) * HD, 32:48], ones[:, 0:HD], gm[:, :, par::2], start=True, stop=True)
                end("v", mm, "gc")
                pe.wait_ge(qk_ready, 2)
                for t in range(TT):
                    b = fill("a")
                    for q in range(4):
                        mm = pe.transpose(b[:, q * P:(q + 1) * P], qkv[:, t, q * P:(q + 1) * P], ident)
                    end("a", mm, "qkT")
                turn_probs(0)
                pe.wait_ge(rotated, 2)
                for t in range(TT):
                    b = fill("a")
                    for q in range(4):
                        mm = pe.transpose(b[:, q * P:(q + 1) * P], rot1[:, t, q * P:(q + 1) * P], ident)
                    end("a", mm, "bqkT")
                for d in range(2):
                    for par in range(2):
                        b = fill("v")
                        for t in range(TT):
                            for f in range(2):
                                k = 2 * t + f
                                mm = pe.matmul(b[:, k * P:(k + 1) * P], g4[:, t, d, 2 * f + par:2 * f + par + 1].to_broadcast([P, P]), tri[:, d, :],
                                               start=True, stop=True)
                        end("v", mm)
                need("probT03")
                need("tok01")
                need("tok00")
                b = fill("a")
                for h in range(NH):
                    for kc in range(2):
                        mm = pe.matmul(b[(h % 2) * HD:(h % 2 + 1) * HD, (h // 2) * T:(h // 2 + 1) * T],
                                       projv[:, kc, PV_A + h * HD:PV_A + (h + 1) * HD], probT[:, h, kc, :], start=kc == 0, stop=kc == 1)
                end("a", mm, "yA")

                need("bqkT")
                for h in range(NH):
                    b = fill("v")
                    r0 = (h % 2) * HD
                    for jt in range(TT):
                        mm = pe.matmul(b[:, jt * T:(jt + 1) * T], bqkT[r0:r0 + HD, 2 + h // 2, jt * P:(jt + 1) * P],
                                       bqkT[r0:r0 + HD, h // 2, :], start=True, stop=True)
                    end("v", mm, f"retS{h}")
                memory_keys(0, 2)
                need("retS3")
                for n in range(1, 3):
                    for t in range(TT):
                        need(f"tok{n}{t}")
                b = fill("v")
                for t in range(TT):
                    for h in range(NH):
                        for jt in range(TT):
                            mm = pe.matmul(b[:, t * W + h * HD:t * W + (h + 1) * HD], retS[:, h, jt * T + t * P:jt * T + (t + 1) * P],
                                           projv[:, jt, PV_B + h * HD:PV_B + (h + 1) * HD], start=jt == 0, stop=jt == TT - 1)
                end("v", mm, "ret_o")

                pe.wait_ge(tables_in, 16)
                for f in range(2):
                    b = fill("a")
                    for q in range(2):
                        g = 2 * f + q
                        for st in range(TT):
                            mm = pe.matmul(b[0:HD, q * T:(q + 1) * T], projv[:, st, PU_C + g * HD:PU_C + (g + 1) * HD],
                                           pools[:, g, st, :], start=st == 0, stop=st == TT - 1)
                    end("a", mm, "diffT")
                need("qkT")
                for which in (2, 0):
                    for par in range(2):
                        b = fill("v")
                        r0 = par * HD
                        for t in range(TT):
                            for f in range(2):
                                k = 2 * t + f
                                mm = pe.matmul(b[:, k * P:(k + 1) * P], qkT[r0:r0 + HD, 2 + f, t * P:(t + 1) * P],
                                               qkT[r0:r0 + HD, which + f, t * P:(t + 1) * P], start=True, stop=True)
                        end("v", mm)
                b4 = unit_col(BETA)
                for d in range(2):
                    for par in range(2):
                        b = fill("v")
                        for t in range(TT):
                            for f in range(2):
                                k = 2 * t + f
                                mm = pe.matmul(b[:, k * P:(k + 1) * P], b4[:, t, d, 2 * f + par:2 * f + par + 1].to_broadcast([P, P]), ident,
                                               start=True, stop=True)
                        end("v", mm)
                need("diffT")
                b = fill("v")
                for g in range(4):
                    mm = pe.matmul(b[(g % 2) * HD:(g % 2 + 1) * HD, (g // 2) * T:(g // 2 + 1) * T], pool_w[:, g, :], diffT[:, g, :],
                                   start=True, stop=True)
                end("v", mm, "yC")
                pe.wait_ge(ret_done, 1)
                b = fill("v")
                for f in range(2):
                    for t in range(TT):
                        mm = pe.transpose(b[:, f * T + t * P:f * T + (t + 1) * P], ret_o[:, t * W + f * P:t * W + (f + 1) * P], ident)
                end("v", mm, "yB")
                memory_keys(1, 0)

                for q in range(4):
                    pe.wait_ge(inv0_ready, q + 1)
                    b = fill("a")
                    for k in range(4):
                        mm = pe.transpose(b[:, k * P:(k + 1) * P], invT[:, 4 * q + k, :], ident)
                    end("a", mm, f"inv{q}")
                    done[f"inv0{q}"] = done[f"inv{q}"]
                memory_keys(1, 2)
                for n in range(1, LEVELS):
                    pe.wait_ge(low_ready, 2 * n)
                    for q in range(4):
                        need(f"inv{q}")
                        b = fill("a")
                        for k in range(4):
                            u = 4 * q + k
                            mm = pe.matmul(b[:, k * P:(k + 1) * P], low[:, u, :], inv[:, u, :], start=True, stop=True)
                        end("a", mm, f"prod{q}")
                        if q == 3:
                            filled[f"low_used{n}"] = filled["prod3"]
                    for q in range(4):
                        need(f"prod{q}")
                        if n > 1:
                            need(f"invT{q}")
                        if n < LEVELS - 1:
                            b = fill("v")
                            for k in range(4):
                                u = 4 * q + k
                                mm = pe.matmul(b[:, k * P:(k + 1) * P], invT[:, u, :], prod[:, u, :], start=True, stop=True)
                            end("v", mm, f"inv{q}")
                        b = fill("v")
                        for k in range(4):
                            u = 4 * q + k
                            mm = pe.matmul(b[:, k * P:(k + 1) * P], prod[:, u, :], invT[:, u, :], start=True, stop=True)
                        end("v", mm, f"invT{q}")
                pe.wait_ge(scaled, 4)
                for d in range(2):
                    b = fill("a")
                    for t in range(TT):
                        for f in range(2):
                            u0 = (2 * d + t) * NH + 2 * f
                            mm = pe.transpose(b[:, (2 * t + f) * P:(2 * t + f + 1) * P],
                                              qdec[:, u0:u0 + 2, :].rearrange("p u k -> p (u k)"), ident)
                    end("a", mm, "qdT")
                need("invT3")
                for d in range(2):
                    b = fill("a")
                    for k in range(8):
                        u = 8 * d + k
                        mm = pe.matmul(b[:, k * HD:(k + 1) * HD], invT[:, u, :], vbeta[:, u, :], start=True, stop=True)
                    end("a", mm, "uval")
                for d in range(2):
                    b = fill("a")
                    for par in range(2):
                        for t in range(TT):
                            for f in range(2):
                                u = ((2 * d + par) * TT + t) * 2 + f
                                mm = pe.matmul(b[par * HD:(par + 1) * HD, (2 * t + f) * P:(2 * t + f + 1) * P], kdec[:, u, :], invT[:, u, :],
                                               start=True, stop=True)
                    end("a", mm, "wT")
                need("wT")
                for s in range(4):
                    where = [(d, (s if d == 0 else 3 - s) // 2, (s if d == 0 else 3 - s) % 2) for d in range(2)]
                    if s:
                        pe.wait_ge(state_ready, 4 * s)
                        for par in range(2):
                            b = fill("v")
                            for d, t, hf in where:
                                for f in range(2):
                                    mm = pe.matmul(b[hf * HD:(hf + 1) * HD, f * HD:(f + 1) * HD],
                                                   wT[par * HD:(par + 1) * HD, d, t, f, hf * HD:(hf + 1) * HD],
                                                   state[par * HD:(par + 1) * HD, d, f, :], start=True, stop=True)
                            end("v", mm)
                        for par in range(2):
                            b = fill("a")
                            for d, t, hf in where:
                                for f in range(2):
                                    mm = pe.matmul(b[hf * HD:(hf + 1) * HD, f * HD:(f + 1) * HD],
                                                   qdT[par * HD:(par + 1) * HD, d, t, f, hf * HD:(hf + 1) * HD],
                                                   state[par * HD:(par + 1) * HD, d, f, :], start=True, stop=True)
                            end("a", mm, f"gdn_q{s}")
                    pe.wait_ge(vnew_ready, 4 * (s + 1))
                    if s < 3:
                        for d, t, hf in where:
                            b = fill("v")
                            for par in range(2):
                                for f in range(2):
                                    u = ((2 * d + par) * TT + t) * 2 + f
                                    mm = pe.matmul(b[par * HD:(par + 1) * HD, f * HD:(f + 1) * HD],
                                                   kstate[hf * HD:(hf + 1) * HD, u, :], vnew[hf * HD:(hf + 1) * HD, par, f, :],
                                                   start=True, stop=True)
                            end("v", mm)
                    b = fill("v")
                    for d, t, hf in where:
                        for par in range(2):
                            for f in range(2):
                                u = ((2 * d + par) * TT + t) * 2 + f
                                mm = pe.matmul(b[hf * HD:(hf + 1) * HD, (2 * par + f) * HD:(2 * par + f + 1) * HD],
                                               decay[hf * HD:(hf + 1) * HD, u, hf * HD:(hf + 1) * HD],
                                               vnew[hf * HD:(hf + 1) * HD, par, f, :], start=True, stop=True)
                    end("v", mm)
                    gdn_read[s] = count["v"]
                    if s == 2:
                        memory_values(0, 0)
                memory_values(0, 1)
                memory_values(1, 0)
                pe.wait_ge(gdn_done, 1)
                b = fill("v")
                for f in range(2):
                    for t in range(TT):
                        mm = pe.transpose(b[:, f * T + t * P:f * T + (t + 1) * P], gdn_o[:, t * W + f * P:t * W + (f + 1) * P], ident)
                end("v", mm, "yD")
                memory_values(1, 1)

                for name in ("yA", "yB", "yC", "yD"):
                    need(name)
                for n in range(2):
                    unit(U_OUT + n)
                    for t in range(TT):
                        token_major(U_OUT + n, t, yT, "v", f"x_mix{n}{t}")

                turn_x("xnT", xn, 2)
                need("xnT")
                for n in range(2):
                    unit(U_MQ + n)
                    for f in (0, 2):
                        feature_major(U_MQ + n, f, xnT, "a", "memQ")
                need("memQ")
                for h in range(NH):
                    b = fill("v")
                    for t in range(TT):
                        for ch in range(2):
                            mm = pe.matmul(b[:, t * T:(t + 1) * T], memQ[:, 2 * h + ch, t * P:(t + 1) * P], memK[:, 2 * h + ch, :],
                                           start=ch == 0, stop=ch == 1)
                    end("v", mm, "mem_scores")
                turn_probs(1)
                for h in range(NH):
                    need(f"probT1{h}")
                    b = fill("a")
                    for ch in range(2):
                        for kc in range(2):
                            mm = pe.matmul(b[:, ch * T:(ch + 1) * T], memV[:, kc, h * T + ch * P:h * T + (ch + 1) * P], probT[:, h, kc, :],
                                           start=kc == 0, stop=kc == 1)
                    end("a", mm, "attT")
                need("attT")
                for n in range(2):
                    unit(U_MO + n)
                    for t in range(TT):
                        token_major(U_MO + n, t, attT, "v", f"x_mem{n}{t}")

                turn_x("xnT", xn, 3)
                need("xnT")
                b = fill("v")
                for t in range(TT):
                    for ch in range(DC):
                        mm = pe.matmul(b[:, 36 * t:36 * t + 36], xnT[:, ch, t * P:(t + 1) * P], router_w[:, ch, :], start=ch == 0, stop=ch == DC - 1)
                end("v", mm)
                pe.wait_ge(ind_ready, 1)
                b = fill("v")
                pe.matmul(b[:, 0:NE], before, ranks[:, 0, :], start=True, stop=True)
                pe.matmul(b[:, NE:2 * NE], ones, ranks[:, 0, :], start=True, stop=False)
                pe.matmul(b[:, NE:2 * NE], before, ranks[:, 1, :], start=False, stop=True)
                pe.matmul(b[:, 2 * NE:3 * NE], ones, ranks[:, 0, :], start=True, stop=False)
                mm = pe.matmul(b[:, 2 * NE:3 * NE], ones, ranks[:, 1, :], start=False, stop=True)
                end("v", mm, "ranks")
                pe.wait_ge(np_ready, 2)
                rounds = pe.value_load(npi[0:1, 0:1], min_val=1, max_val=T // SLOTS)

                def expert_pass(it, pairs, odd):
                    def unit(n):
                        at = 12 * odd + n
                        pe.wait_ge(expert_in[at % ESLOT], 16 * (at // ESLOT + 1) + 16 * (24 // ESLOT) * pairs)
                        return ring[:, at % ESLOT, :].rearrange("p (e k) -> p e k", e=QUAD)

                    pe.wait_ge(sel_built, 2 * it)
                    for g in range(2):
                        for q in range(4):
                            for t in range(TT):
                                mm = pe.matmul(bank[g][:, q * P:(q + 1) * P], xn_by_row[:, t, 4 * g + q, :], sel[:, t, :],
                                               start=t == 0, stop=t == TT - 1)
                        mm.then_inc(gathered[g], 1)
                    for t in range(TT):
                        mm = pe.transpose(bank[2][:, t * P:(t + 1) * P], selw[:, t, :], ident)
                    mm.then_inc(sel_turned, 1)
                    for part in range(2):
                        for n in range(4):
                            if part == 0 and n % 2 == 0:
                                pe.wait_ge(xg_ready[n // 2], it)
                            w = unit(4 * part + n)
                            for q in range(2):
                                ch = 2 * n + q
                                for e in range(QUAD):
                                    mm = pe.matmul(bank[3 + part][e * SLOTS:(e + 1) * SLOTS, :], xg[:, ch, e * SLOTS:(e + 1) * SLOTS],
                                                   w[:, e, q * DE:(q + 1) * DE], start=ch == 0, stop=ch == DC - 1)
                            mm.then_inc((gate_full, up_full)[part] if n == 3 else units_free, 1)
                    pe.wait_ge(hid_ready, it)
                    for c4 in range(4):
                        mm = pe.transpose(bank[5][:, c4 * P:(c4 + 1) * P], hid_by_row[:, c4, :], ident)
                    mm.then_inc(hid_turned, 1)
                    pe.wait_ge(hidT_ready, it)
                    for c4 in range(4):
                        w = unit(8 + c4)
                        for n in range(2):
                            for e in range(QUAD):
                                mm = pe.matmul(bank[6 + n][e * SLOTS:(e + 1) * SLOTS, :], hidT[:, c4, e * SLOTS:(e + 1) * SLOTS],
                                               w[:, e, n * 512:(n + 1) * 512], start=c4 == 0, stop=c4 == 3)
                            if c4 == 3:
                                mm.then_inc(y_full[n], 1)
                            elif n == 1:
                                mm.then_inc(units_free, 1)
                    pe.drain().then_inc(units_free, 1)
                    pe.wait_ge(selwT_ready, it)
                    for n in range(2):
                        pe.wait_ge(y_ready[n], it)
                        for t in range(TT):
                            pe.matmul(bank[(0, 1, 2, 5)[2 * n + t]][:, :], selwT[:, t, :], y_e[:, n * 512:(n + 1) * 512],
                                      start=True, stop=True).then_inc(scattered[2 * n + t], 1)

                pe.wait_ge(vec_evac, count["v"])
                pe.wait_ge(act_evac, count["a"])
                with pe.Fori(0, rounds) as k:
                    with pe.Fori(0, NQ // 2) as pair:
                        for odd in range(2):
                            expert_pass(NQ * k + 2 * pair + odd + 1, NQ // 2 * k + pair, odd)
                pe.drain().then_inc(layer_done, 1)
                pe.wait_ge(layer_go, l + 1)
                pe.sem_inc(layer_seen, 1)

        @block.vector
        def _(v):
            v.memset(mhalf[:], -0.5).then_inc(preset, 1)
            v.memset(small[:], 0.0).then_inc(preset, 1)
            v.wait_ge(preset, 2)
            v.wait_ge(x_in, 16)

            with v.Fori(0, DEPTH) as l:
                n_own = [0]
                n_in = [0]

                def own(ins):
                    n_own[0] += 1
                    ins.then_inc(vec_step, 1)
                    v.wait_ge(vec_step, n_own[0])

                def take():
                    v.wait_ge(vec_full, n_in[0] + 1)
                    return bank[n_in[0] % 4]

                def taken(ins):
                    n_in[0] += 1
                    ins.then_inc(vec_evac, 1)
                    v.wait_ge(vec_evac, n_in[0])

                def norm(src, dst, k):
                    if k == 0:
                        v.wait_ge(x_squares, 4 * l + 4)
                    else:
                        v.wait_ge(squares, 4 * k)
                    v.scalar_tensor_tensor(out=ss[:, k, 4:6], in0=ss[:, k, 0:2], scalar=EPS, in1=ss[:, k, 2:4], op0=ALU.add, op1=ALU.add).then_inc(means, 1)
                    v.wait_ge(rstds, k + 1)
                    for t in range(TT):
                        v.tensor_scalar(dst[:, t, :], src[:, t, :], rstd[:, k, t:t + 1], None, ALU.mult).then_inc(normed, 1)

                def take_turned(dstT, k):
                    for t in range(TT):
                        for g in range(2):
                            b = take()
                            taken(v.tensor_tensor(dstT[:, 4 * g:4 * g + 4, t * P:(t + 1) * P], b[:, :].rearrange("p (c k) -> p c k", c=4),
                                                  wide(gains[:, k, 4 * g:4 * g + 4], P), ALU.mult))

                mx = dsm[:, 240:248].rearrange("p (h t) -> p h t", t=TT)

                def scores(mask):
                    for h in range(NH):
                        b = take()
                        bv = b[:, :].rearrange("p (t k) -> p t k", t=TT)
                        if mask:
                            taken(v.tensor_tensor(prob[:, h], bv, again(c("band"), TT), ALU.add))
                        else:
                            taken(v.tensor_copy(prob[:, h], bv))
                        own(v.tensor_reduce(mx[:, h, :], prob[:, h], AX, ALU.max))
                        v.tensor_scalar(mx[:, h, :], mx[:, h, :], -1.0, None, ALU.mult).then_inc(maxed, 1)

                def weights(k):
                    for h in range(NH):
                        v.wait_ge(exped, 2 * (NH * k + h + 1))
                        own(v.reciprocal(stat[:, 2 * h:2 * h + 2], stat2[:, 2 * h:2 * h + 2]))
                        v.tensor_tensor(prob[:, h], prob[:, h], wide(stat[:, 2 * h:2 * h + 2], T), ALU.mult).then_inc(probs_ready, 1)

                norm(x, xn, 0)
                v.wait_ge(gains_in, 16 * 5)
                own(v.tensor_copy(gains[:], all_gains[:, :, bass.ds(l, 1)].rearrange("p k l c -> p k (l c)")))
                take_turned(xnT, 0)
                v.wait_ge(const_in, 16)
                own(v.memset(conv_in[:, :, 0:2], 0.0))
                own(v.memset(conv_in[:, :, T + 2:T + 3], 0.0))
                for f in range(3):
                    b = take()
                    taken(v.tensor_copy(conv_in[:, 2 * f:2 * f + 2, 2:T + 2], b[:, :].rearrange("p (c t) -> p c t", c=2)))
                norm(mem_tok, mem_n, 1)
                take_turned(memT, 2)
                v.wait_ge(params_in, 16 * N_PARAMS)
                for k in range(4):
                    for ch in range(6):
                        o = convT[:, ch, :]
                        if k == 0:
                            ins = v.tensor_scalar(o, conv_in[:, ch, 0:T], conv_w[:, 0, ch:ch + 1], None, ALU.mult)
                        else:
                            ins = v.scalar_tensor_tensor(out=o, in0=conv_in[:, ch, k:k + T], scalar=conv_w[:, k, ch:ch + 1], in1=o, op0=ALU.mult, op1=ALU.add)
                        if k < 3:
                            n_own[0] += 1
                            ins.then_inc(vec_step, 1)
                        else:
                            ins.then_inc(conved, 1)
                        if k < 3 and ch == 5:
                            v.wait_ge(vec_step, n_own[0])
                for t in range(TT):
                    v.wait_ge(*done[f"gate{t}"])
                ab = projv[:, :, PAB:PAB + 16]
                t16 = lambda k: dcol(k).rearrange("p (t u) -> p t u", t=TT)
                own(v.tensor_tensor(t16(T0), ab[:, :, 0:8], again(rows[:, 8:16], TT), ALU.add))
                own(v.tensor_scalar(t16(T1), t16(T0), -1.0, None, ALU.mult))
                own(v.tensor_tensor(t16(T1), t16(T1), t16(T0), ALU.min))
                own(v.tensor_scalar(t16(T0), t16(T0), 0.0, None, ALU.max))
                v.tensor_copy(t16(T2), ab[:, :, 8:16]).then_inc(gate_in, 1)
                for n in range(3):
                    b = take()
                    taken(v.tensor_copy(projv[:, 1, n * 512:(n + 1) * 512], b[:, :]))
                v.wait_ge(gate_exp, 3)
                own(v.tensor_scalar(t16(T2), t16(T2), 1.0, None, ALU.add))
                own(v.reciprocal(dcol(BETA), dcol(T2)))
                v.wait_ge(gate_ln, 1)
                own(v.tensor_tensor(t16(T0), t16(T0), t16(T1), ALU.add))
                own(v.tensor_tensor(t16(T0), t16(T0), again(dcol(T3, 8), TT), ALU.mult))
                own(v.tensor_scalar(dcol(G), dcol(T0), -1.0, None, ALU.mult))
                own(v.tensor_scalar(gmask[:, 0, :], dcol(G), halves[:, 0:1], None, ALU.mult))
                v.tensor_scalar(gmask[:, 1, :], dcol(G), halves[:, 1:2], None, ALU.mult).then_inc(g_ready, 1)
                for n in range(2):
                    v.wait_ge(*done[f"tok{n}0"])
                for t in range(TT):
                    src = projv[:, t, PQ_B:PQ_B + 512].rearrange("p (h k) -> p h k", k=HD)
                    r1 = rot1[:, t, :].rearrange("p (h k) -> p h k", k=HD)
                    r2 = rot2[:, t, :].rearrange("p (h k) -> p h k", k=HD)
                    own(v.tensor_tensor(r1, src, again(rot_a[:, t, :], 8), ALU.mult))
                    own(v.tensor_tensor(r2[:, :, 0:32], src[:, :, 32:64], again(rot_b[:, t, 0:32], 8), ALU.mult))
                    own(v.tensor_tensor(r2[:, :, 32:64], src[:, :, 0:32], again(rot_b[:, t, 32:64], 8), ALU.mult))
                    v.tensor_tensor(r1, r1, r2, ALU.add).then_inc(rotated, 1)
                for t in range(TT):
                    b = take()
                    taken(v.tensor_copy(qkv[:, t, 0:512], b[:, :]))
                    b = take()
                    taken(v.tensor_copy(qkv[:, t, 512:768], b[:, 0:256]))
                for t in range(TT):
                    own(v.tensor_tensor(xnf[:, 512 * t:512 * (t + 1)], qkv[:, t, 0:512], qkv[:, t, 0:512], ALU.mult))
                own(v.tensor_reduce(stat, xnf[:, 0:1024].rearrange("p (u k) -> p u k", k=HD), AX, ALU.add))
                v.tensor_scalar(stat2, stat, EPS, None, ALU.add).then_inc(qk_sums, 1)
                v.wait_ge(qk_rstd, 1)
                stat_t = stat.rearrange("p (t u) -> p t u", t=TT)
                own(v.tensor_scalar(stat_t[:, :, 0:4], stat_t[:, :, 0:4], HD ** -0.5, None, ALU.mult))
                for t in range(TT):
                    q3 = qkv[:, t, 0:512].rearrange("p (u k) -> p u k", k=HD)
                    v.tensor_tensor(q3, q3, wide(stat[:, 8 * t:8 * t + 8], HD), ALU.mult).then_inc(qk_ready, 1)
                v.wait_ge(qk_ready, 2)
                scores(True)
                b = take()
                own(v.tensor_copy(dsm[:, 16 * GC:16 * GC + 32], b[:, 0:32]))
                own(v.tensor_tensor(dcol(T0), dcol(GL), dcol(GC), ALU.subtract))
                taken(v.tensor_copy(egl, b[:, 32:48]))
                v.tensor_copy(dcol(T1), dcol(GC)).then_inc(gdiff, 1)
                weights(0)
                v.wait_ge(*filled["probT03"])
                gc4 = unit_col(GC)
                for d in range(2):
                    for par in range(2):
                        b = take()
                        for k in range(4):
                            t, f = k // 2, k % 2
                            ins = v.tensor_scalar(decay[:, (2 * d + par) * 4 + k, :], b[:, k * P:(k + 1) * P],
                                                  gc4[:, t, d, 2 * f + par:2 * f + par + 1], 0.0, ALU.subtract, ALU.min)
                        taken(ins)
                v.wait_ge(tables_in, 16)
                for h in range(NH):
                    b = take()
                    taken(v.tensor_tensor(retS[:, h, :], b[:, :], decays[:, h, :], ALU.mult))
                b = take()
                taken(v.tensor_copy(ret_o, b[:, :]))
                o3 = ret_o.rearrange("p (u k) -> p u k", k=HD)
                s3 = ret_s.rearrange("p (u k) -> p u k", k=HD)
                own(v.tensor_reduce(stat[:, 0:8], o3, AX, ALU.add))
                own(v.tensor_scalar(stat[:, 0:8], stat[:, 0:8], 1.0 / HD, None, ALU.mult))
                own(v.tensor_tensor(o3, o3, wide(stat[:, 0:8], HD), ALU.subtract))
                own(v.tensor_tensor(s3, o3, o3, ALU.mult))
                own(v.tensor_reduce(stat[:, 0:8], s3, AX, ALU.add))
                v.tensor_scalar(stat[:, 8:16], stat[:, 0:8], 1.0 / HD, EPS, ALU.mult, ALU.add).then_inc(ret_var, 1)
                v.wait_ge(dec_masked, 4)
                v.wait_ge(*filled["probT03"])
                for par in range(2):
                    b = take()
                    for d in range(2):
                        u0 = (2 * d + par) * 4
                        ins = v.tensor_tensor(lT[:, u0:u0 + 4, :], b[:, :].rearrange("p (u k) -> p u k", u=4), decay[:, u0:u0 + 4, :], ALU.mult)
                    taken(ins)
                for par in range(2):
                    b = take()
                    for d in range(2):
                        u0 = (2 * d + par) * 4
                        ins = v.tensor_tensor(decay[:, u0:u0 + 4, :], b[:, :].rearrange("p (u k) -> p u k", u=4), decay[:, u0:u0 + 4, :], ALU.mult)
                    taken(ins)
                v.wait_ge(ret_rstd, 1)
                own(v.tensor_tensor(o3, o3, wide(stat[:, 0:8], HD), ALU.mult))
                v.wait_ge(ret_silu, 1)
                v.tensor_tensor(ret_o.rearrange("p (t k) -> p t k", t=TT), ret_o.rearrange("p (t k) -> p t k", t=TT),
                                projv[:, :, PG_B:PG_B + W], ALU.mult).then_inc(ret_done, 1)
                for q in range(4):
                    b = take()
                    taken(v.tensor_tensor(lT[:, 4 * q:4 * q + 4, :], b[:, :].rearrange("p (u k) -> p u k", u=4), lT[:, 4 * q:4 * q + 4, :], ALU.mult))
                b = take()
                taken(v.tensor_tensor(yT[:, 4:6, :], b[:, :].rearrange("p (c t) -> p c t", c=2), wide(cols[:, 2:4], T), ALU.mult))
                b = take()
                taken(v.tensor_tensor(yT[:, 2:4, :], b[:, :].rearrange("p (c t) -> p c t", c=2), wide(cols[:, 0:2], T), ALU.mult))
                for q in range(4):
                    d = q // 2
                    o = invT[:, 4 * q:4 * q + 4, :]
                    own(v.tensor_tensor(o, lT[:, 4 * q:4 * q + 4, :], again(level[:, 0, d, :], 4), ALU.mult))
                    v.tensor_tensor(o, again(ident, 4), o, ALU.subtract).then_inc(inv0_ready, 1)
                b4, e4, s4 = unit_col(BETA), unit_col(EGC), unit_col(ESL)
                be4 = unit_col(T0)

                def scale_rows(dst, w, col):
                    for d in range(2):
                        for par in range(2):
                            for t in range(TT):
                                u0 = ((2 * d + par) * TT + t) * 2
                                v4 = qkv[:, t, :].rearrange("p (w f a k) -> p w a f k", w=3, f=2, a=2)
                                ins = v.tensor_tensor(dst[:, u0:u0 + 2, :], v4[:, w, par], wide(col[:, t, d, par::2], HD), ALU.mult)
                    ins.then_inc(scaled, 1)

                for n in range(1, LEVELS):
                    for q in range(4):
                        for m in ((inv, invT) if n < LEVELS - 1 else (invT,)):
                            if n == 1 and m is inv:
                                v.wait_ge(*done[f"inv0{q}"])
                            b = take()
                            o = m[:, 4 * q:4 * q + 4, :]
                            taken(v.tensor_tensor(o, o, b[:, :].rearrange("p (u k) -> p u k", u=4), ALU.subtract))
                    if n == 1:
                        v.wait_ge(gexp, 3)
                        v.wait_ge(*filled["diffT"])
                        own(v.tensor_tensor(dcol(T0), dcol(BETA), dcol(EGC), ALU.mult))
                        scale_rows(vbeta, 2, b4)
                    if n == 2:
                        scale_rows(kdec, 1, be4)
                    if n == 3:
                        scale_rows(kstate, 1, s4)
                        for d in range(2):
                            for t in range(TT):
                                ins = v.tensor_tensor(qdec[:, (2 * d + t) * NH:(2 * d + t + 1) * NH, :], qkv[:, t, 0:W].rearrange("p (h k) -> p h k", h=NH),
                                                      wide(e4[:, t, d, :], HD), ALU.mult)
                        ins.then_inc(scaled, 1)
                v.wait_ge(*done["uval"])
                ov = gdn_o.rearrange("p (d t f a e) -> p d t a f e", d=2, t=TT, f=2, a=2)
                u6 = uval.rearrange("p (d a t f) e -> p d a t f e", d=2, a=2, t=TT)
                for s in range(4):
                    where = [(d, (s if d == 0 else 3 - s) // 2, (s if d == 0 else 3 - s) % 2) for d in range(2)]
                    for par in range(2):
                        if s:
                            b = take()
                        for d, t, hf in where:
                            r = slice(hf * HD, (hf + 1) * HD)
                            if s:
                                v.tensor_tensor(vnew[r, par], u6[r, d, par, t], b[r, 0:P].rearrange("p (f e) -> p f e", f=2), ALU.subtract).then_inc(vnew_ready, 1)
                            else:
                                v.tensor_copy(vnew[r, par], u6[r, d, par, t]).then_inc(vnew_ready, 1)
                        if s:
                            taken(v.tensor_copy(stat2[:, 0:1], b[:, 0:1]))
                    if s < 3:
                        for d, t, hf in where:
                            b = take()
                            for f in range(2):
                                k = ((hf * TT + t) * 2 + d) * 2 + f
                                if s:
                                    v.scalar_tensor_tensor(out=state[:, d, f, :], in0=state[:, d, f, :], scalar=egl[:, k:k + 1],
                                                           in1=b[:, f * HD:(f + 1) * HD], op0=ALU.mult, op1=ALU.add).then_inc(state_ready, 1)
                                else:
                                    v.tensor_copy(state[:, d, f, :], b[:, f * HD:(f + 1) * HD]).then_inc(state_ready, 1)
                            taken(v.tensor_copy(stat2[:, 0:1], b[:, 0:1]))
                        v.wait_ge(state_ready, 4 * (s + 1))
                    if s:
                        v.wait_ge(*done[f"gdn_q{s}"])
                    b = take()
                    for d, t, hf in where:
                        r = slice(hf * HD, (hf + 1) * HD)
                        bv = b[r, 0:256].rearrange("p (a f e) -> p a f e", a=2, f=2)
                        for par in range(2):
                            if s:
                                ins = v.tensor_tensor(ov[r, d, t, par], gdn_q[r, par], bv[:, par], ALU.add)
                            else:
                                ins = v.tensor_copy(ov[r, d, t, par], bv[:, par])
                    taken(ins)
                g3 = gdn_o[:, 0:512].rearrange("p (u k) -> p u k", k=HD)
                own(v.tensor_tensor(gdn_o[:, 0:512], gdn_o[:, 0:512], gdn_o[:, 512:1024], ALU.add))
                own(v.tensor_tensor(gdn_o[:, 512:1024], gdn_o[:, 0:512], gdn_o[:, 0:512], ALU.mult))
                own(v.tensor_reduce(stat[:, 0:8], gdn_o[:, 512:1024].rearrange("p (u k) -> p u k", k=HD), AX, ALU.add))
                v.tensor_scalar(stat[:, 8:16], stat[:, 0:8], 1.0 / HD, EPS, ALU.mult, ALU.add).then_inc(gdn_var, 1)
                v.wait_ge(gdn_rstd, 1)
                own(v.tensor_tensor(g3, g3, wide(stat[:, 0:8], HD), ALU.mult))
                v.wait_ge(gdn_silu, 1)
                v.tensor_tensor(gdn_o[:, 0:512].rearrange("p (t k) -> p t k", t=TT), gdn_o[:, 0:512].rearrange("p (t k) -> p t k", t=TT),
                                projv[:, :, PG_D:PG_D + W], ALU.mult).then_inc(gdn_done, 1)
                b = take()
                taken(v.tensor_scalar(yT[:, 6:8, :], b[:, :].rearrange("p (c t) -> p c t", c=2), cols[:, 4:5], None, ALU.mult))

                def add_to_x():
                    for n in range(2):
                        for t in range(TT):
                            b = take()
                            o = x[:, t, n * 512:(n + 1) * 512]
                            taken(v.tensor_tensor(o, o, b[:, :], ALU.add))

                add_to_x()
                norm(x, xn, 2)
                take_turned(xnT, 1)
                scores(False)
                weights(1)
                add_to_x()
                norm(x, xn, 3)
                take_turned(xnT, 3)

                b = take()
                taken(v.tensor_tensor(logit, b[:, 0:72].rearrange("p (t k) -> p t k", t=TT), again(rows[:, 16:52], TT), ALU.add))
                rt = lambda k: small[:, 80 + 16 * k:96 + 16 * k].rearrange("p (t k) -> p t k", t=TT)
                GP, EL, E1, OH1, OH2, GOH, DF, W1, W2 = (rt(k) for k in range(9))
                own(v.tensor_scalar(GP, logit[:, :, 0:8], 0.0, NEG, ALU.mult, ALU.add))
                own(v.tensor_copy(GP[:, :, 0:4], logit[:, :, 0:4]))
                for t in range(TT):
                    own(v.max(val[:, 0, t, :], GP[:, t, :]))
                    own(v.max_index(idx[:, 0, t, :], val[:, 0, t, :], GP[:, t, :]))
                g1 = DF[:, :, 0:1]
                own(v.tensor_copy(g1, idx[:, 0, :, 0:1]))
                per = lambda ap, n: ap.to_broadcast([P, TT, n])
                by_group = lambda ap: ap[:, :, 0:NG].rearrange("p t (g o) -> p t g o", o=1).to_broadcast([P, TT, NG, EPG])
                by_expert = lambda ap: ap.rearrange("p t (o e) -> p t o e", o=1).to_broadcast([P, TT, NG, EPG])
                grouped = lambda ap: ap.rearrange("p t (g e) -> p t g e", g=NG)
                own(v.tensor_tensor(GOH, again(c("eight"), TT), per(g1, EPG), ALU.is_equal))
                own(v.tensor_tensor(W1[:, :, 0:4], GP[:, :, 0:4], per(val[:, 0, :, 0:1], 4), ALU.subtract))
                masked = small[:, 320:384].rearrange("p (t g e) -> p t g e", t=TT, g=NG)
                own(v.tensor_tensor(masked, grouped(logit[:, :, 4:36]), by_group(GOH), ALU.mult))
                own(v.tensor_reduce(EL, masked.rearrange("p t g e -> p t e g"), AX, ALU.add))
                for t in range(TT):
                    own(v.max(val[:, 1, t, :], EL[:, t, :]))
                    own(v.max_index(idx[:, 1, t, :], val[:, 1, t, :], EL[:, t, :]))
                v.tensor_tensor(W1[:, :, 4:5], val[:, 1, :, 1:2], val[:, 1, :, 0:1], ALU.subtract).then_inc(r_max, 1)
                own(v.tensor_copy(DF[:, :, 0:2], idx[:, 1, :, 0:2]))
                own(v.tensor_tensor(OH1, again(c("eight"), TT), per(DF[:, :, 0:1], EPG), ALU.is_equal))
                own(v.tensor_tensor(OH2, again(c("eight"), TT), per(DF[:, :, 1:2], EPG), ALU.is_equal))
                own(v.tensor_tensor(E1, OH1, OH2, ALU.add))
                v.wait_ge(r_exp, 1)
                v.tensor_tensor(grouped(ranks[:, :, :]), by_expert(E1), by_group(GOH), ALU.mult).then_inc(ind_ready, 1)
                v.wait_ge(ind_ready, 1)
                own(v.tensor_reduce(DF[:, :, 2], W2[:, :, 0:4], AX, ALU.add))
                own(v.tensor_scalar(DF[:, :, 3:4], W2[:, :, 4:5], 1.0, None, ALU.add))
                own(v.tensor_tensor(DF[:, :, 4:5], DF[:, :, 2:3], DF[:, :, 3:4], ALU.mult))
                own(v.reciprocal(DF[:, :, 5:6], DF[:, :, 4:5]))
                own(v.tensor_tensor(DF[:, :, 6:7], DF[:, :, 5:6], W2[:, :, 4:5], ALU.mult))
                own(v.tensor_tensor(OH1, OH1, per(DF[:, :, 5:6], EPG), ALU.mult))
                own(v.tensor_tensor(OH2, OH2, per(DF[:, :, 6:7], EPG), ALU.mult))
                own(v.tensor_tensor(W1, OH1, OH2, ALU.add))
                own(v.tensor_tensor(grouped(gates[:, :, :]), by_expert(W1), by_group(GOH), ALU.mult))
                b = take()
                ind = small[:, 256:320].rearrange("p (t e) -> p t e", t=TT)
                own(v.tensor_copy(ind, ranks[:, :, :]))
                own(v.scalar_tensor_tensor(out=ranks[:, :, :], in0=b[:, 0:2 * NE].rearrange("p (t e) -> p t e", t=TT), scalar=1.0, in1=ind,
                                           op0=ALU.add, op1=ALU.mult))
                own(v.tensor_scalar(ranks[:, :, :], ranks[:, :, :], -1.0, None, ALU.add))
                taken(v.tensor_reduce(stat[:, 0:1], b[:, 2 * NE:3 * NE], AX, ALU.max))
                over = small[:, 384:384 + T // SLOTS - 1]
                own(v.tensor_tensor(over, c("fulls"), stat[:, 0:1].to_broadcast([P, T // SLOTS - 1]), ALU.is_lt))
                own(v.tensor_reduce(stat[:, 1:2], over, AX, ALU.add))
                v.tensor_scalar(npi[0:1, 0:1], stat[0:1, 1:2], 1.0, None, ALU.add).then_inc(np_ready, 1)
                v.tensor_copy(npi[0:1, 1:2], stat[0:1, 1:2]).then_inc(np_ready, 1)
                v.wait_ge(np_ready, 2)
                rounds = v.value_load(npi[0:1, 0:1], min_val=1, max_val=T // SLOTS)

                def expert_pass(it, before_it, q):
                    v.tensor_copy(rank_q[:], ranks[:, :, bass.ds(QUAD * q, QUAD)]).then_inc(quad_ready, 1)
                    v.tensor_copy(gate_q[:], gates[:, :, bass.ds(QUAD * q, QUAD)]).then_inc(quad_ready, 1)
                    v.wait_ge(quad_ready, 2 * it)
                    s3 = sel.rearrange("p t (e s) -> p (t e) s", e=QUAD)
                    w3 = selw.rearrange("p t (e s) -> p (t e) s", e=QUAD)
                    slots8 = again(c("slot"), TT * QUAD)
                    v.tensor_tensor(s3, slots8, wide(rank_q[:].rearrange("p t e -> p (t e)"), SLOTS), ALU.is_equal).then_inc(sel_built, 1)
                    v.wait_ge(sel_built, 2 * before_it + 1)
                    v.tensor_tensor(w3, s3, wide(gate_q[:].rearrange("p t e -> p (t e)"), SLOTS), ALU.mult).then_inc(sel_built, 1)
                    for g in range(2):
                        v.wait_ge(gathered[g], it)
                        v.tensor_tensor(xg[:, 4 * g:4 * g + 4, :], bank[g][:, :].rearrange("p (c s) -> p c s", c=4),
                                        wide(gains[:, 4, 4 * g:4 * g + 4], P), ALU.mult).then_inc(xg_ready[g], 1)
                    v.wait_ge(silu_ready, it)
                    v.wait_ge(up_full, it)
                    v.tensor_tensor(hid, silu_g, bank[4][:, :], ALU.mult).then_inc(hid_ready, 1)
                    for n in range(2):
                        for t in range(TT):
                            v.wait_ge(scattered[2 * n + t], it)
                            o = x[:, t, n * 512:(n + 1) * 512]
                            v.tensor_tensor(o, o, bank[(0, 1, 2, 5)[2 * n + t]][:, :], ALU.add).then_inc(x_added, 1)
                    v.wait_ge(x_added, 4 * it)
                    v.sem_inc(pass_seen, 1)

                with v.Fori(0, rounds) as k:
                    with v.Fori(0, NQ) as q:
                        expert_pass(NQ * k + q + 1, NQ * k + q, q)
                    v.tensor_scalar(ranks[:, :, :], ranks[:, :, :], -float(SLOTS), None, ALU.add).then_inc(ranks_moved, 1)
                    v.wait_ge(ranks_moved, k + 1)
                    v.sem_inc(pass_seen, 1)
                v.drain().then_inc(layer_done, 1)
                v.wait_ge(layer_go, l + 1)
                v.sem_inc(layer_seen, 1)

            v.wait_ge(x_squares, 4 * DEPTH + 4)
            v.scalar_tensor_tensor(out=ss[:, 0, 4:6], in0=ss[:, 0, 0:2], scalar=EPS, in1=ss[:, 0, 2:4], op0=ALU.add, op1=ALU.add).then_inc(last_mean, 1)
            v.wait_ge(last_rstd, 1)
            v.wait_ge(final_in, 16)
            for t in range(TT):
                v.scalar_tensor_tensor(out=xn[:, t, :], in0=x[:, t, :], scalar=rstd[:, 0, t:t + 1], in1=m1[:, 0:D], op0=ALU.mult, op1=ALU.mult).then_inc(last_out, 1)

        @block.scalar
        def _(s):
            s.wait_ge(x_in, 16)

            def x_square(i):
                quarter = slice(i // 2 * 512, i // 2 * 512 + 512)
                s.activation(xn[:, i % 2, quarter], x[:, i % 2, quarter], ACT.Square, scale=D ** -0.5,
                             accum_out=ss[:, 0, i:i + 1]).then_inc(x_squares, 1)

            for i in range(4):
                x_square(i)
            with s.Fori(0, DEPTH) as l:
                n_in = [0]

                def take():
                    s.wait_ge(act_full, n_in[0] + 1)
                    return bank[4 + n_in[0] % 4]

                def taken(ins):
                    n_in[0] += 1
                    ins.then_inc(act_evac, 1)

                def squares_of(src, junk, k, part=None):
                    for n in range(2):
                        for t in range(TT):
                            if part:
                                s.wait_ge(*done[f"{part}{n}{t}"])
                            quarter = slice(n * 512, (n + 1) * 512)
                            s.activation(junk[:, t, quarter], src[:, t, quarter], ACT.Square, scale=D ** -0.5,
                                         accum_out=ss[:, k, 2 * n + t:2 * n + t + 1]).then_inc(squares, 1)

                def exps(k):
                    for h in range(NH):
                        s.wait_ge(maxed, NH * k + h + 1)
                        for t in range(TT):
                            s.activation(prob[:, h, t, :], prob[:, h, t, :], ACT.Exp, bias=dsm[:, 240 + 2 * h + t:241 + 2 * h + t],
                                         accum_out=stat2[:, 2 * h + t:2 * h + t + 1]).then_inc(exped, 1)

                def memory_keys(n, f):
                    b = take()
                    taken(s.copy(memK[:, 4 * n + f:4 * n + f + 2, :], b[:, :].rearrange("p (c t) -> p c t", c=2)))

                def memory_values(n, t):
                    b = take()
                    taken(s.copy(memV[:, t, n * 512:(n + 1) * 512], b[:, :]))

                s.wait_ge(mem_in, 16)
                squares_of(mem_tok, mem_n, 1)
                for t in range(TT):
                    b = take()
                    taken(s.copy(projv[:, t, PG_D:PW], b[:, 0:PW - PG_D]))
                b = take()
                taken(s.copy(projv[:, 0, 0:512], b[:, :]))
                for ch in range(6):
                    s.wait_ge(conved, ch + 1)
                    s.activation(convT[:, ch, :], convT[:, ch, :], ACT.Silu).then_inc(conv_silu, 1)
                s.wait_ge(*done["gate1"])
                s.activation(projv[:, :, PG_D:PG_D + W], projv[:, :, PG_D:PG_D + W], ACT.Silu).then_inc(gdn_silu, 1)
                s.wait_ge(gate_in, 1)
                s.wait_ge(params_in, 16 * N_PARAMS)
                s.activation(dcol(T1), dcol(T1), ACT.Exp).then_inc(gate_exp, 1)
                s.activation(dcol(T2), dcol(T2), ACT.Exp, scale=-1.0).then_inc(gate_exp, 1)
                s.activation(dcol(T3, 8), rows[:, 0:8], ACT.Exp).then_inc(gate_exp, 1)
                s.wait_ge(gate_exp, 3)
                s.activation(dcol(T1), dcol(T1), ACT.Ln, bias=1.0).then_inc(gate_ln, 1)
                for n in range(1, 3):
                    b = take()
                    taken(s.copy(projv[:, 0, n * 512:(n + 1) * 512], b[:, :]))
                s.wait_ge(*done["tok21"])
                s.wait_ge(*done["tok20"])
                s.activation(projv[:, :, PG_B:PG_B + W], projv[:, :, PG_B:PG_B + W], ACT.Silu).then_inc(ret_silu, 1)
                b = take()
                taken(s.mul(aqkT[:, 0:2, :], b[:, :].rearrange("p (c t) -> p c t", c=2), HD ** -0.5))
                b = take()
                taken(s.copy(aqkT[:, 2:4, :], b[:, :].rearrange("p (c t) -> p c t", c=2)))
                exps(0)
                memory_keys(0, 0)
                for t in range(TT):
                    b = take()
                    taken(s.copy(qkT[:, 0:4, t * P:(t + 1) * P], b[:, :].rearrange("p (c k) -> p c k", c=4)))
                s.wait_ge(gdiff, 1)
                s.activation(dcol(EGC), dcol(T1), ACT.Exp).then_inc(gexp, 1)
                s.activation(dcol(ESL), dcol(T0), ACT.Exp).then_inc(gexp, 1)
                s.wait_ge(*done["gc"])
                s.activation(egl, egl, ACT.Exp).then_inc(gexp, 1)
                for h in range(NH):
                    b = take()
                    taken(s.copy(probT[:, h].rearrange("p c q -> p (c q)"), b[:, :]))
                for t in range(TT):
                    b = take()
                    taken(s.copy(bqkT[:, :, t * P:(t + 1) * P], b[:, :].rearrange("p (c k) -> p c k", c=4)))
                b = take()
                taken(s.copy(yT[:, 0:2, :], b[:, :].rearrange("p (c t) -> p c t", c=2)))
                for q in range(4):
                    s.wait_ge(vec_evac, done["gc"][1] + q + 1)
                    o = decay[:, 4 * q:4 * q + 4, :]
                    s.activation(o, o, ACT.Exp).then_inc(dec_exp, 1)
                memory_keys(0, 2)
                for f in range(2):
                    b = take()
                    taken(s.copy(diffT[:, 2 * f:2 * f + 2, :], b[0:HD, :].rearrange("p (c t) -> p c t", c=2)))
                memory_keys(1, 0)
                for q in range(4):
                    b = take()
                    taken(s.copy(inv[:, 4 * q:4 * q + 4, :], b[:, :].rearrange("p (u k) -> p u k", u=4)))
                memory_keys(1, 2)
                for n in range(1, LEVELS):
                    for q in range(4):
                        b = take()
                        taken(s.copy(prod[:, 4 * q:4 * q + 4, :], b[:, :].rearrange("p (u k) -> p u k", u=4)))
                for d in range(2):
                    b = take()
                    taken(s.copy(qdT[:, d].rearrange("p t f k -> p (t f) k"), b[:, :].rearrange("p (u k) -> p u k", u=4)))
                for d in range(2):
                    b = take()
                    taken(s.copy(uval[:, 8 * d:8 * d + 8, :], b[:, :].rearrange("p (u k) -> p u k", u=8)))
                for d in range(2):
                    b = take()
                    taken(s.copy(wT[:, d].rearrange("p t f k -> p (t f) k"), b[:, :].rearrange("p (u k) -> p u k", u=4)))
                for step in range(1, 4):
                    for par in range(2):
                        b = take()
                        if step > 1:
                            s.wait_ge(vec_evac, gdn_read[step - 1])
                        taken(s.copy(gdn_q[:, par], b[:, 0:P].rearrange("p (f e) -> p f e", f=2)))
                    if step == 2:
                        memory_values(0, 0)
                memory_values(0, 1)
                memory_values(1, 0)
                memory_values(1, 1)
                squares_of(x, xn, 2, "x_mix")
                for n in range(2):
                    for f in range(2):
                        b = take()
                        taken(s.mul(memQ[:, 4 * n + 2 * f:4 * n + 2 * f + 2, :], b[:, :].rearrange("p (c t) -> p c t", c=2), 256 ** -0.5))
                exps(1)
                for h in range(NH):
                    b = take()
                    taken(s.copy(probT[:, h].rearrange("p c q -> p (c q)"), b[:, :]))
                for h in range(NH):
                    b = take()
                    taken(s.copy(attT[:, 2 * h:2 * h + 2, :], b[:, :].rearrange("p (c t) -> p c t", c=2)))
                squares_of(x, xn, 3, "x_mem")
                s.wait_ge(r_max, 1)
                rw = small[:, 80 + 16 * 7:80 + 16 * 9].rearrange("p (w t k) -> p w t k", w=2, t=TT)
                s.activation(rw[:, 1, :, 0:5], rw[:, 0, :, 0:5], ACT.Exp).then_inc(r_exp, 1)
                s.wait_ge(np_ready, 2)
                rounds = s.value_load(npi[0:1, 0:1], min_val=1, max_val=T // SLOTS)
                further = s.value_load(npi[0:1, 1:2], min_val=0, max_val=T // SLOTS - 1)

                def expert_pass(it):
                    s.wait_ge(sel_turned, it)
                    s.copy(selwT, bank[2][:, 0:T].rearrange("p (t k) -> p t k", t=TT)).then_inc(selwT_ready, 1)
                    s.wait_ge(gate_full, it)
                    s.activation(silu_g, bank[3][:, :], ACT.Silu).then_inc(silu_ready, 1)
                    s.wait_ge(hid_turned, it)
                    s.copy(hidT, bank[5][:, :].rearrange("p (c s) -> p c s", c=4)).then_inc(hidT_ready, 1)
                    for n in range(2):
                        s.wait_ge(y_full[n], it)
                        s.copy(y_e[:, n * 512:(n + 1) * 512], bank[6 + n][:, :]).then_inc(y_ready[n], 1)

                with s.Fori(0, rounds) as k:
                    with s.Fori(0, NQ) as q:
                        expert_pass(NQ * k + q + 1)
                for i in range(4):
                    s.wait_ge(x_added, 4 * NQ * further + (4 * NQ - 3 + i))
                    x_square(i)
                s.drain().then_inc(layer_done, 1)
                s.wait_ge(layer_go, l + 1)
                s.sem_inc(layer_seen, 1)

        @block.gpsimd
        def _(g):
            g.wait_ge(preset, 2)
            with g.Fori(0, DEPTH) as l:
                def root(k):
                    g.wait_ge(means, k + 1)
                    g.tensor_tensor(rstd[:, k, :], ss[:, k, 4:6], mhalf[:, 0:2], ALU.pow).then_inc(rstds, 1)

                root(0)
                root(1)
                g.wait_ge(const_in, 16)
                g.wait_ge(qk_sums, 1)
                g.tensor_tensor(stat, stat2, mhalf[:], ALU.pow).then_inc(qk_rstd, 1)
                for q in range(4):
                    g.wait_ge(dec_exp, q + 1)
                    o = decay[:, 4 * q:4 * q + 4, :]
                    g.tensor_tensor(o, o, again(tri[:, q // 2, :], 4), ALU.mult).then_inc(dec_masked, 1)
                g.wait_ge(ret_var, 1)
                g.tensor_tensor(stat[:, 0:8], stat[:, 8:16], mhalf[:, 0:8], ALU.pow).then_inc(ret_rstd, 1)
                g.wait_ge(inv0_ready, 4)
                for n in range(1, LEVELS):
                    if n > 1:
                        g.wait_ge(*filled[f"low_used{n - 1}"])
                    for d in range(2):
                        g.tensor_tensor(low[:, 8 * d:8 * d + 8, :], lT[:, 8 * d:8 * d + 8, :], again(level[:, n, d, :], 8), ALU.mult).then_inc(low_ready, 1)
                g.wait_ge(gdn_var, 1)
                g.tensor_tensor(stat[:, 0:8], stat[:, 8:16], mhalf[:, 0:8], ALU.pow).then_inc(gdn_rstd, 1)
                root(2)
                root(3)
                g.drain().then_inc(layer_done, 1)
                g.wait_ge(layer_go, l + 1)
                g.sem_inc(layer_seen, 1)
            g.wait_ge(last_mean, 1)
            g.tensor_tensor(rstd[:, 0, :], ss[:, 0, 4:6], mhalf[:, 0:2], ALU.pow).then_inc(last_rstd, 1)

        @block.sync
        def _(sp):
            def unit_source(layer, n):
                names = {U_DQK: ("w_in", 2048), U_DVG: ("w_in", 2560), U_TOK: ("w_in", 512), U_TOK + 1: ("w_in", 1024),
                         U_TOK + 2: ("w_in", 1536), U_AQK: ("w_in", 0)}
                for u, name in ((U_MK, "mem_w_k"), (U_MV, "mem_w_v"), (U_OUT, "w_out"), (U_MQ, "mem_w_q"), (U_MO, "mem_w_o")):
                    names[u], names[u + 1] = (name, 0), (name, 512)
                name, lo = names[n]
                w = a[name][layer:layer + 1] if isinstance(layer, int) else a[name][bass.ds(layer, 1)]
                return w[:, :, lo:lo + 512].rearrange("l (c p) n -> p (l c) n", p=P)

            def unit_tile(n):
                return ring[:, slot(n), :].rearrange("p (c k) -> p c k", c=DC)

            sp.dma_start(x[:], a["x"].rearrange("b (t p) d -> p (b t) d", p=P)).then_inc(x_in, 16)
            for k, name in enumerate(("mix_norm_g", "mem_q_norm_g", "mem_kv_norm_g", "ffn_norm_g", "ffn_norm_g")):
                order = "l (c p) -> p l c" if k < 4 else "l (p c) -> p l c"
                sp.dma_start(all_gains[:, k, :, :], a[name].rearrange(order, p=P), allow_slow_non_contiguous=True).then_inc(gains_in, 16)
            sp.dma_start(const[:, 0:P], a["consts"][:, 0:P]).then_inc(ident_in, 16)
            for n in range(AHEAD):
                sp.dma_start(unit_tile(n), unit_source(0, n)).then_inc(first_in[n], 16)
                if n == 0:
                    sp.dma_start(const[:, P:], a["consts"][:, P:]).then_inc(const_in, 16)
            with sp.Fori(0, DEPTH) as l:
                lay = lambda name: a[name][bass.ds(l, 1)]
                n_par = [0]

                def param(dst, src):
                    sp.dma_start(dst, src, allow_slow_non_contiguous=True).then_inc(params_in, 16)
                    n_par[0] += 1

                sp.dma_start(mem_tok, a["mem"].rearrange("b (t p) d -> p (b t) d", p=P)).then_inc(mem_in, 16)
                param(w_ab, lay("w_in")[:, :, 3072:3088].rearrange("l (c p) n -> p (l c) n", p=P))
                for k in range(4):
                    param(conv_w[:, k, :], lay("gdn_conv_w")[:, k, :].rearrange("l (c p) -> p (l c)", p=P))
                param(rows[:, 0:8], lay("gdn_a_log").rearrange("l d h -> l (d h)").to_broadcast([P, 8]))
                param(rows[:, 8:16], lay("gdn_dt_bias").rearrange("l d h -> l (d h)").to_broadcast([P, 8]))
                param(rows[:, 16:20], lay("b_group").to_broadcast([P, 4]))
                param(rows[:, 20:52], lay("b_router").to_broadcast([P, NE]))
                param(cols[:, 0:2], lay("ret_norm_g").rearrange("l (c p) -> p (l c)", p=P))
                param(cols[:, 2:4], lay("pool_scale").rearrange("l (c p) -> p (l c)", p=P))
                for k in range(2):
                    param(cols[k * HD:(k + 1) * HD, 4:5], lay("gdn_norm_g").rearrange("l p -> p l"))
                param(pool_w, lay("pool_w").rearrange("l g c e -> c (l g) e"))
                param(router_w[:, :, 0:NG], lay("w_group").rearrange("l (c p) n -> p (l c) n", p=P))
                param(router_w[:, :, NG:NG + NE], lay("w_router").rearrange("l (c p) n -> p (l c) n", p=P))
                assert n_par[0] == N_PARAMS, n_par
                for n in range(AHEAD, NSLOT):
                    sp.dma_start(unit_tile(n), unit_source(l, n)).then_inc(unit_in[slot(n)], 16)
                for t in range(TT):
                    for r in range(2):
                        for h in range(NH):
                            row = 2 * t + r
                            src = bass.AP(a["na_rpb"].tensor, l * (NH * RPB_H * RPB_W) + ((7 - row) * RPB_W + 15 - 63 + RPB_H * RPB_W * h),
                                          [[1, GRID_W], [RPB_W, ROWS], [1, GRID_W]])
                            sp.dma_start(bias[GRID_W * r:GRID_W * (r + 1), t, h, :].rearrange("p (r k) -> p r k", r=ROWS), src).then_inc(rpb_in, 16)
                sp.dma_start(tables, a["big_consts"]).then_inc(tables_in, 16)

                def expert_unit(at, first):
                    n = at % 12
                    name, k = (("w_gate", n), ("w_up", n - 4), ("w_down", n - 8))[n // 4]
                    rows_of = a[name].rearrange("l e (p c) f -> (l e) p (c f)", p=P)[bass.ds(first, QUAD)]
                    sp.dma_start(ring[:, at % ESLOT, :].rearrange("p (e k) -> p e k", e=QUAD),
                                 rows_of[:, :, 1024 * k:1024 * (k + 1)].rearrange("e p k -> p e k")).then_inc(expert_in[at % ESLOT], 16)

                RELEASE = tuple(10 * odd + n for odd in range(2) for n in (1, 2, 3, 4, 4, 5, 6, 7, 7, 8, 9, 10))

                def units(pair, lo, hi, released):
                    for n in range(lo, hi):
                        if n == lo or n == 12:
                            first = sp.snap(l * NE + 2 * QUAD * pair + QUAD * (n // 12))
                        sp.wait_ge(units_free, released + RELEASE[(n + 24 - ESLOT) % 24])
                        if n == lo or n % 4 == 0:
                            sp.sem_inc(pass_seen, 1)
                        expert_unit(n, first)

                for n in range(NSLOT, PRE_UNITS):
                    if n == U_MO:
                        sp.wait_ge(*filled["yD"])
                        expert_unit(4, l * NE)
                    sp.wait_ge(*last_reader[n - NSLOT])
                    sp.dma_start(unit_tile(n), unit_source(l, n)).then_inc(unit_in[slot(n)], 16)
                for n in (0, 1, 5, 7, 6, 2, 3):
                    if n == 5:
                        sp.wait_ge(*filled["mem_scores"])
                    elif n == 6:
                        sp.wait_ge(*filled["attT"])
                    elif n != 7:
                        sp.wait_ge(*last_reader[PRE_UNITS - NSLOT + n])
                    expert_unit(n, l * NE)
                PAIRS = NQ // 2
                with sp.Fori(0, PAIRS - 1) as pair:
                    units(pair, ESLOT, 24, 20 * pair)
                    units(pair + 1, 0, ESLOT, 20 * pair)
                units(PAIRS - 1, ESLOT, 24, 20 * (PAIRS - 1))
                sp.wait_ge(np_ready, 2)
                further = sp.value_load(npi[0:1, 1:2], min_val=0, max_val=T // SLOTS - 1)
                for q in mixer_sems:
                    sp.sem_clear(q)
                with sp.If(further > 0):
                    with sp.Fori(0, further) as k:
                        with sp.Fori(0, PAIRS) as pair:
                            units(pair, 0, ESLOT, 20 * (PAIRS * k + pair) + 20 * (PAIRS - 1))
                            units(pair, ESLOT, 24, 20 * (PAIRS * k + pair) + 20 * PAIRS)
                with sp.If(l < DEPTH - 1):
                    following = nc.s_assert_within(sp.snap(l + 1), 0, DEPTH - 1, skip_runtime_bounds_check_because="the branch is taken before the last layer only")
                    for n in range(AHEAD):
                        sp.wait_ge(units_free, 10 * NQ * further + (20 * (PAIRS - 1) + RELEASE[24 - ESLOT + n]))
                        sp.sem_inc(pass_seen, 1)
                        sp.dma_start(unit_tile(n), unit_source(following, n)).then_inc(first_in[n], 16)
                sp.wait_ge(layer_done, 4)
                for q in layer_sems:
                    sp.sem_clear(q)
                sp.sem_inc(layer_go, 1)
            sp.dma_start(m1[:, 0:D], a["final_norm_g"].rearrange("(o d) -> o d", o=1).to_broadcast([P, D])).then_inc(final_in, 16)
            for t in range(TT):
                sp.wait_ge(last_out, t + 1)
                sp.dma_start(out[0, t * P:(t + 1) * P, :], xn[:, t, :]).then_inc(stored, 16)
            sp.wait_ge(stored, 16 * TT)


N_PARAMS = 16
_INS = ("x", "mem", "mix_norm_g", "w_in", "na_rpb", "ret_norm_g", "pool_w", "pool_scale", "gdn_conv_w", "gdn_a_log", "gdn_dt_bias",
        "gdn_norm_g", "w_out", "mem_q_norm_g", "mem_kv_norm_g", "mem_w_q", "mem_w_k", "mem_w_v", "mem_w_o", "ffn_norm_g", "w_group",
        "b_group", "w_router", "b_router", "w_gate", "w_up", "w_down", "final_norm_g")


def kernel(**inputs):
    import concourse.bacc as _bacc
    from concourse.bass_utils import run_bass_kernel_spmd as _run

    nc = _bacc.Bacc("TRN2", target_bir_lowering=False, num_devices=1)
    small_tables, big_tables = constant_tables()
    arrays = {name: np.ascontiguousarray(inputs[name]) for name in _INS}
    arrays["consts"], arrays["big_consts"] = small_tables, big_tables
    a = {name: nc.dram_tensor(f"in_{name}", v.shape, F32, kind="ExternalInput").ap() for name, v in arrays.items()}
    out = nc.dram_tensor("out_0", (1, T, D), F32, kind="ExternalOutput").ap()
    encoder(nc, a, out)
    r = _run(nc, [{f"in_{name}": v for name, v in arrays.items()}], core_ids=[0])
    return r.results[0]["out_0"]
```
